# Optimizing a Trainium2 kernel written in Bass

```python
import math
import jax
import jax.numpy as jnp
from jax import lax
import numpy as np

D_MODEL = 1024
BATCH = 1
SEQ = 512
DEPTH = 2

GRID_W = 64
CTX_LEN = 256
GROUP_W = D_MODEL // 4
D_MIX = 4 * GROUP_W
NA_HEADS = 4
NA_HD = GROUP_W // NA_HEADS
NA_KH = 8
NA_KW = 16
MLA_HEADS = 4
MLA_NOPE = 64
MLA_ROPE = 32
MLA_V = GROUP_W // MLA_HEADS
MLA_Q_RANK = 256
MLA_KV_RANK = 128
DIFF_HEADS = 4
DIFF_V = GROUP_W // DIFF_HEADS
DIFF_QK = DIFF_V // 2
SSD_D_INNER = GROUP_W
SSD_HD = 64
SSD_HEADS = SSD_D_INNER // SSD_HD
SSD_GROUPS = 2
SSD_STATE = 128
SSD_CONV = 5
SSD_CHUNK = 64
SSD_XBC = SSD_D_INNER + 2 * SSD_GROUPS * SSD_STATE
NA_IN = 3 * NA_HEADS * NA_HD
MLA_IN = MLA_Q_RANK + MLA_KV_RANK + MLA_ROPE
DIFF_IN = 2 * DIFF_HEADS * 2 * DIFF_QK + DIFF_HEADS * DIFF_V
SSD_IN = SSD_D_INNER + SSD_XBC + 2 * SSD_HEADS
N_IN = NA_IN + MLA_IN + DIFF_IN + SSD_IN
SPLIT_AT = [NA_IN, NA_IN + MLA_IN, NA_IN + MLA_IN + DIFF_IN]
ROPE_DIM = 32
ROPE_BASE = 10000.0
Q_BLOCK = 128
MOE_GROUPS = 4
MOE_EPG = 4
MOE_EXPERTS = MOE_GROUPS * MOE_EPG
MOE_TOP_K = 2
MOE_FF = 512
MOE_BLOCK = 128
NORM_EPS = 1e-6

kernel_name = 'hybrid_grid_flow_block'

def _rmsnorm(x, g):
    xf = x.astype(jnp.float32)
    y = xf * lax.rsqrt(jnp.mean(xf * xf, axis=-1, keepdims=True) + NORM_EPS)
    return (y * g.astype(jnp.float32)).astype(x.dtype)

def _axial_rope(n_tok, dtype):
    n_freq = ROPE_DIM // 4
    inv = jnp.power(ROPE_BASE, -jnp.arange(n_freq, dtype=jnp.float32) / n_freq)
    t = jnp.arange(n_tok, dtype=jnp.int32)
    row = (t // GRID_W).astype(jnp.float32)
    col = (t % GRID_W).astype(jnp.float32)
    ang = jnp.concatenate([row[:, None] * inv, col[:, None] * inv], axis=-1)
    return jnp.cos(ang).astype(dtype), jnp.sin(ang).astype(dtype)

def _apply_rope(x, cos, sin):
    half = x.shape[-1] // 2
    x1, x2 = x[..., :half], x[..., half:]
    return jnp.concatenate([x1 * cos - x2 * sin, x1 * sin + x2 * cos], axis=-1)

def _softmax_attend(q, k, v, scale):
    s = jnp.einsum('bqhd,bkhd->bhqk', q, k, preferred_element_type=jnp.float32) * scale
    p = jax.nn.softmax(s, axis=-1).astype(v.dtype)
    return jnp.einsum('bhqk,bkhd->bqhd', p, v)

def _diff_attend(q1, q2, k1, k2, v, lam, scale):
    s1 = jnp.einsum('bqhd,bkhd->bhqk', q1, k1, preferred_element_type=jnp.float32) * scale
    s2 = jnp.einsum('bqhd,bkhd->bhqk', q2, k2, preferred_element_type=jnp.float32) * scale
    p = (jax.nn.softmax(s1, axis=-1) - lam * jax.nn.softmax(s2, axis=-1)).astype(v.dtype)
    return jnp.einsum('bhqk,bkhd->bqhd', p, v)

def _over_query_blocks(fn, *qs):
    b, s = qs[0].shape[:2]
    nb = s // Q_BLOCK
    blocks = tuple(q.reshape((b, nb, Q_BLOCK) + q.shape[2:]).swapaxes(0, 1) for q in qs)
    out = lax.map(lambda qb: fn(*qb), blocks)
    return out.swapaxes(0, 1).reshape((b, s) + out.shape[3:])

def _na_mixer(p_ctx, p_lat, g_q, g_k, rel_bias, with_ctx_out):
    def heads(p):
        b, n = p.shape[:2]
        q, k, v = (t.reshape(b, n, NA_HEADS, NA_HD) for t in jnp.split(p, 3, axis=-1))
        return _rmsnorm(q, g_q), _rmsnorm(k, g_k), v
    qc, kc, vc = heads(p_ctx)
    ql, kl, vl = heads(p_lat)
    b, n = p_lat.shape[:2]
    n_ctx = kc.shape[1]
    rows = n // GRID_W
    kh = min(NA_KH, rows)
    scale = NA_HD ** -0.5
    r = np.arange(rows)
    row_idx = np.clip(r - kh // 2, 0, rows - kh)[:, None] + np.arange(kh)[None, :]
    cq = np.arange(GRID_W)
    col_lo = np.clip(cq - NA_KW // 2, 0, GRID_W - NA_KW)
    col_mask = (cq[None, :] >= col_lo[:, None]) & (cq[None, :] < col_lo[:, None] + NA_KW)
    row_off = row_idx - r[:, None] + (NA_KH - 1)
    col_off = np.clip(cq[None, :] - cq[:, None], 1 - NA_KW, NA_KW - 1) + (NA_KW - 1)
    bias = rel_bias[:, row_off[:, None, :, None], col_off[None, :, None, :]]
    bias = jnp.where(col_mask[None, None, :, None, :], bias, -jnp.inf)
    qg = ql.reshape(b, rows, GRID_W, NA_HEADS, NA_HD)
    kg = kl.reshape(b, rows, GRID_W, NA_HEADS, NA_HD)[:, row_idx]
    vg = vl.reshape(b, rows, GRID_W, NA_HEADS, NA_HD)[:, row_idx]
    s_nb = jnp.einsum('brqhd,brkwhd->bhrqkw', qg, kg, preferred_element_type=jnp.float32) * scale + bias[None]
    s_nb = s_nb.reshape(b, NA_HEADS, rows, GRID_W, kh * GRID_W)
    s_cx = jnp.einsum('brqhd,bchd->bhrqc', qg, kc, preferred_element_type=jnp.float32) * scale
    p = jax.nn.softmax(jnp.concatenate([s_cx, s_nb], axis=-1), axis=-1).astype(vl.dtype)
    p_nb = p[..., n_ctx:].reshape(b, NA_HEADS, rows, GRID_W, kh, GRID_W)
    o = (jnp.einsum('bhrqc,bchd->brqhd', p[..., :n_ctx], vc)
         + jnp.einsum('bhrqkw,brkwhd->brqhd', p_nb, vg))
    o_lat = o.reshape(b, n, NA_HEADS * NA_HD)
    o_ctx = _softmax_attend(qc, kc, vc, scale).reshape(b, n_ctx, -1) if with_ctx_out else None
    return o_ctx, o_lat

def _mla_project(p, g_qa, w_qb, g_kva, w_kvb, g_q, g_k, cos, sin):
    b, n = p.shape[:2]
    cq, ckv, kr = jnp.split(p, [MLA_Q_RANK, MLA_Q_RANK + MLA_KV_RANK], axis=-1)
    q = (_rmsnorm(cq, g_qa) @ w_qb).reshape(b, n, MLA_HEADS, MLA_NOPE + MLA_ROPE)
    kv = (_rmsnorm(ckv, g_kva) @ w_kvb).reshape(b, n, MLA_HEADS, MLA_NOPE + MLA_V)
    k_nope, v = jnp.split(kv, [MLA_NOPE], axis=-1)
    k = jnp.concatenate([k_nope, jnp.broadcast_to(kr[:, :, None, :], (b, n, MLA_HEADS, MLA_ROPE))], axis=-1)
    q = _rmsnorm(q, g_q)
    k = _rmsnorm(k, g_k)
    if cos is not None:
        q = jnp.concatenate([q[..., :MLA_NOPE], _apply_rope(q[..., MLA_NOPE:], cos[:, None], sin[:, None])], axis=-1)
        k = jnp.concatenate([k[..., :MLA_NOPE], _apply_rope(k[..., MLA_NOPE:], cos[:, None], sin[:, None])], axis=-1)
    return q, k, v

def _mla_mixer(p_ctx, p_lat, cos, sin, g_qa, w_qb, g_kva, w_kvb, g_q, g_k, with_ctx_out):
    qc, kc, vc = _mla_project(p_ctx, g_qa, w_qb, g_kva, w_kvb, g_q, g_k, None, None)
    ql, kl, vl = _mla_project(p_lat, g_qa, w_qb, g_kva, w_kvb, g_q, g_k, cos, sin)
    scale = (MLA_NOPE + MLA_ROPE) ** -0.5
    k_all = jnp.concatenate([kc, kl], axis=1)
    v_all = jnp.concatenate([vc, vl], axis=1)
    o_lat = _over_query_blocks(lambda qb: _softmax_attend(qb, k_all, v_all, scale), ql)
    b, n = p_lat.shape[:2]
    o_ctx = _softmax_attend(qc, kc, vc, scale).reshape(b, kc.shape[1], -1) if with_ctx_out else None
    return o_ctx, o_lat.reshape(b, n, -1)

def _diff_mixer(p_ctx, p_lat, cos, sin, g_q, g_k, lam_vecs, g_sub, lam_init, with_ctx_out):
    def heads(p, cos_t, sin_t):
        b, n = p.shape[:2]
        nq = DIFF_HEADS * 2 * DIFF_QK
        q, k, v = jnp.split(p, [nq, 2 * nq], axis=-1)
        q = _rmsnorm(q.reshape(b, n, DIFF_HEADS, 2, DIFF_QK), g_q)
        k = _rmsnorm(k.reshape(b, n, DIFF_HEADS, 2, DIFF_QK), g_k)
        if cos_t is not None:
            q = _apply_rope(q, cos_t[:, None, None], sin_t[:, None, None])
            k = _apply_rope(k, cos_t[:, None, None], sin_t[:, None, None])
        return q[..., 0, :], q[..., 1, :], k[..., 0, :], k[..., 1, :], v.reshape(b, n, DIFF_HEADS, DIFF_V)
    lv = lam_vecs.astype(jnp.float32)
    lam = jnp.exp(jnp.sum(lv[0] * lv[1])) - jnp.exp(jnp.sum(lv[2] * lv[3])) + lam_init
    scale = DIFF_QK ** -0.5
    q1c, q2c, k1c, k2c, vc = heads(p_ctx, None, None)
    q1l, q2l, k1l, k2l, vl = heads(p_lat, cos, sin)
    k1 = jnp.concatenate([k1c, k1l], axis=1)
    k2 = jnp.concatenate([k2c, k2l], axis=1)
    v_all = jnp.concatenate([vc, vl], axis=1)
    o_lat = _over_query_blocks(lambda q1b, q2b: _diff_attend(q1b, q2b, k1, k2, v_all, lam, scale), q1l, q2l)

    def finish(o):
        return (_rmsnorm(o, g_sub) * (1.0 - lam_init)).reshape(o.shape[0], o.shape[1], -1)
    o_ctx = finish(_diff_attend(q1c, q2c, k1c, k2c, vc, lam, scale)) if with_ctx_out else None
    return o_ctx, finish(o_lat)

def _dwconv_centred(u, w, bias):
    k = w.shape[0]
    out = lax.conv_general_dilated(u, w[:, None, :], window_strides=(1,), padding=[(k // 2, k // 2)],
                                   dimension_numbers=('NWC', 'WIO', 'NWC'), feature_group_count=u.shape[-1])
    return out + bias

def _ssd_chunked(x, dt, a, b_in, c_in, h0):
    bsz, seqlen, nh, hp = x.shape
    ng, ns = b_in.shape[2], b_in.shape[3]
    nc = seqlen // SSD_CHUNK
    rep = nh // ng
    xdt = (x * dt[..., None]).reshape(bsz, nc, SSD_CHUNK, nh, hp)
    bh = jnp.repeat(b_in, rep, axis=2).reshape(bsz, nc, SSD_CHUNK, nh, ns)
    ch = jnp.repeat(c_in, rep, axis=2).reshape(bsz, nc, SSD_CHUNK, nh, ns)
    la = (dt.astype(jnp.float32) * a).reshape(bsz, nc, SSD_CHUNK, nh).transpose(0, 1, 3, 2)
    la_cum = jnp.cumsum(la, axis=-1)
    tril = np.tril(np.ones((SSD_CHUNK, SSD_CHUNK), dtype=bool))
    seg = la_cum[..., :, None] - la_cum[..., None, :]
    decay = jnp.where(tril, jnp.exp(jnp.where(tril, seg, 0.0)), 0.0).astype(x.dtype)
    scores = jnp.einsum('bclhn,bcshn->bchls', ch, bh) * decay
    y_diag = jnp.einsum('bchls,bcshp->bclhp', scores, xdt)
    to_end = jnp.exp(la_cum[..., -1:] - la_cum).astype(x.dtype)
    chunk_states = jnp.einsum('bclhn,bchl,bclhp->bchpn', bh, to_end, xdt)
    chunk_decay = jnp.exp(la_cum[..., -1]).astype(x.dtype)

    def step(h, inp):
        st, dec = inp
        return h * dec[..., None, None] + st, h
    h_final, h_enter = lax.scan(step, h0, (jnp.moveaxis(chunk_states, 1, 0), jnp.moveaxis(chunk_decay, 1, 0)))
    h_enter = jnp.moveaxis(h_enter, 0, 1)
    y_off = jnp.einsum('bclhn,bchpn,bchl->bclhp', ch, h_enter, jnp.exp(la_cum).astype(x.dtype))
    return (y_diag + y_off).reshape(bsz, seqlen, nh, hp), h_final

def _ssd_mixer(p_ctx, p_lat, conv_w, conv_b, dt_bias, a_log, d_skip, g_norm, with_ctx_out):
    def prep(p):
        b, n = p.shape[:2]
        z, xbc, dt_raw = jnp.split(p, [SSD_D_INNER, SSD_D_INNER + SSD_XBC], axis=-1)
        xbc = jax.nn.silu(_dwconv_centred(xbc, conv_w, conv_b))
        xs, bs, cs = jnp.split(xbc, [SSD_D_INNER, SSD_D_INNER + SSD_GROUPS * SSD_STATE], axis=-1)
        return (z, xs.reshape(b, n, SSD_HEADS, SSD_HD), bs.reshape(b, n, SSD_GROUPS, SSD_STATE),
                cs.reshape(b, n, SSD_GROUPS, SSD_STATE), dt_raw.reshape(b, n, 2, SSD_HEADS))
    zc, xc, bc, cc, dtc = prep(p_ctx)
    zl, xl, bl, cl, dtl = prep(p_lat)
    bsz = xl.shape[0]
    ys_c, ys_l = [], []
    for d in range(2):
        flip = (lambda u: jnp.flip(u, axis=1)) if d == 1 else (lambda u: u)
        a = -jnp.exp(a_log[d].astype(jnp.float32))
        dt_c = jax.nn.softplus(dtc[:, :, d] + dt_bias[d])
        dt_l = jax.nn.softplus(dtl[:, :, d] + dt_bias[d])
        h0 = jnp.zeros((bsz, SSD_HEADS, SSD_HD, SSD_STATE), xl.dtype)
        yc, h_ctx = _ssd_chunked(flip(xc), flip(dt_c), a, flip(bc), flip(cc), h0)
        yl, _ = _ssd_chunked(flip(xl), flip(dt_l), a, flip(bl), flip(cl), h_ctx)
        ys_c.append(flip(yc) + d_skip[d][:, None] * xc)
        ys_l.append(flip(yl) + d_skip[d][:, None] * xl)

    def finish(y, z):
        b, n = z.shape[:2]
        return _rmsnorm(y.reshape(b, n, SSD_D_INNER) * jax.nn.silu(z), g_norm)
    o_ctx = finish(ys_c[0] + ys_c[1], zc) if with_ctx_out else None
    return o_ctx, finish(ys_l[0] + ys_l[1], zl)

def _moe_dispatch(h, expert_idx, expert_w, w_gate, w_up, w_down):
    n_tok, d = h.shape
    k = expert_idx.shape[1]
    n_asg = n_tok * k
    n_exp = w_gate.shape[0]
    flat_e = expert_idx.reshape(-1)
    order = jnp.argsort(flat_e)
    sorted_e = flat_e[order]
    counts = jnp.bincount(flat_e, length=n_exp)
    padded = (counts + MOE_BLOCK - 1) // MOE_BLOCK * MOE_BLOCK
    pad_end = jnp.cumsum(padded)
    pad_start = pad_end - padded
    seg_start = jnp.cumsum(counts) - counts
    dest = pad_start[sorted_e] + jnp.arange(n_asg, dtype=jnp.int32) - seg_start[sorted_e]
    n_blocks = -(-n_asg // MOE_BLOCK) + n_exp
    cap = n_blocks * MOE_BLOCK
    slot_tok = jnp.full((cap,), n_tok, jnp.int32).at[dest].set((order // k).astype(jnp.int32))
    slot_w = jnp.zeros((cap,), h.dtype).at[dest].set(expert_w.reshape(-1)[order])
    block_e = jnp.minimum(jnp.searchsorted(pad_end, jnp.arange(n_blocks) * MOE_BLOCK, side='right'), n_exp - 1)
    h_pad = jnp.concatenate([h, jnp.zeros((1, d), h.dtype)], axis=0)

    def run_block(args):
        tok, e = args
        xb = h_pad[tok]
        return (jax.nn.silu(xb @ w_gate[e]) * (xb @ w_up[e])) @ w_down[e]
    y = lax.map(run_block, (slot_tok.reshape(n_blocks, MOE_BLOCK), block_e)).reshape(cap, d)
    out = jnp.zeros((n_tok + 1, d), h.dtype).at[slot_tok].add(y * slot_w[:, None])
    return out[:n_tok]

def _hier_moe(h, w_group, b_group, w_expert, b_expert, w_gate, w_up, w_down):
    n_tok = h.shape[0]
    g_prob = jax.nn.softmax((h @ w_group + b_group).astype(jnp.float32), axis=-1)
    g_top_p, g_top = lax.top_k(g_prob, 1)
    e_logits = (h @ w_expert + b_expert).astype(jnp.float32).reshape(n_tok, MOE_GROUPS, MOE_EPG)
    e_in = jnp.take_along_axis(e_logits, g_top[:, :, None], axis=1)[:, 0]
    e_top_l, e_top = lax.top_k(e_in, MOE_TOP_K)
    e_w = jax.nn.softmax(e_top_l, axis=-1) * g_top_p
    expert_idx = g_top * MOE_EPG + e_top
    return _moe_dispatch(h, expert_idx, e_w.astype(h.dtype), w_gate, w_up, w_down)

def setup_inputs(seed: int = 0) -> dict:
    key = jax.random.key(seed)
    keys = iter(jax.random.split(key, 40))
    f32 = jnp.float32
    L, D = DEPTH, D_MODEL

    def nrm(shape, std):
        return jax.random.normal(next(keys), shape, f32) * std

    def gain(shape):
        return 1.0 + nrm(shape, 0.02)
    x = nrm((BATCH, SEQ, D), 1.0)
    c = nrm((BATCH, D), 1.0)
    ctx = nrm((BATCH, CTX_LEN, D), 1.0)
    c_ctx = nrm((D,), 1.0)
    w_mod = nrm((L, D, 6 * D), 0.5 * D ** -0.5)
    b_mod = nrm((L, 6 * D), 0.02)
    g_mix = gain((L, D))
    w_in = nrm((L, D, N_IN), D ** -0.5)
    w_out = nrm((L, D_MIX, D), D_MIX ** -0.5)
    na_g_q = gain((L, NA_HD))
    na_g_k = gain((L, NA_HD))
    na_rel_bias = nrm((L, NA_HEADS, 2 * NA_KH - 1, 2 * NA_KW - 1), 0.1)
    mla_g_qa = gain((L, MLA_Q_RANK))
    mla_w_qb = nrm((L, MLA_Q_RANK, MLA_HEADS * (MLA_NOPE + MLA_ROPE)), MLA_Q_RANK ** -0.5)
    mla_g_kva = gain((L, MLA_KV_RANK))
    mla_w_kvb = nrm((L, MLA_KV_RANK, MLA_HEADS * (MLA_NOPE + MLA_V)), MLA_KV_RANK ** -0.5)
    mla_g_q = gain((L, MLA_NOPE + MLA_ROPE))
    mla_g_k = gain((L, MLA_NOPE + MLA_ROPE))
    diff_g_q = gain((L, DIFF_QK))
    diff_g_k = gain((L, DIFF_QK))
    diff_lambda = nrm((L, 4, DIFF_QK), 0.1)
    diff_g_sub = gain((L, DIFF_V))
    ssd_conv_w = nrm((L, SSD_CONV, SSD_XBC), SSD_CONV ** -0.5)
    ssd_conv_b = nrm((L, SSD_XBC), 0.02)
    dt0 = jnp.exp(jax.random.uniform(next(keys), (L, 2, SSD_HEADS), f32, math.log(1e-3), math.log(1e-1)))
    ssd_dt_bias = dt0 + jnp.log(-jnp.expm1(-dt0))
    ssd_a_log = jnp.log(jax.random.uniform(next(keys), (L, 2, SSD_HEADS), f32, 1.0, 16.0))
    ssd_d = 1.0 + nrm((L, 2, SSD_HEADS), 0.1)
    ssd_g_norm = gain((L, SSD_D_INNER))
    g_ffn = gain((L, D))
    moe_w_group = nrm((L, D, MOE_GROUPS), D ** -0.5)
    moe_b_group = nrm((L, MOE_GROUPS), 0.01)
    moe_w_expert = nrm((L, D, MOE_EXPERTS), D ** -0.5)
    moe_b_expert = nrm((L, MOE_EXPERTS), 0.01)
    moe_w_gate = nrm((L, MOE_EXPERTS, D, MOE_FF), D ** -0.5)
    moe_w_up = nrm((L, MOE_EXPERTS, D, MOE_FF), D ** -0.5)
    moe_w_down = nrm((L, MOE_EXPERTS, MOE_FF, D), MOE_FF ** -0.5)
    return {'x': x, 'c': c, 'ctx': ctx, 'c_ctx': c_ctx, 'w_mod': w_mod, 'b_mod': b_mod,
            'g_mix': g_mix, 'w_in': w_in, 'w_out': w_out,
            'na_g_q': na_g_q, 'na_g_k': na_g_k, 'na_rel_bias': na_rel_bias,
            'mla_g_qa': mla_g_qa, 'mla_w_qb': mla_w_qb, 'mla_g_kva': mla_g_kva, 'mla_w_kvb': mla_w_kvb,
            'mla_g_q': mla_g_q, 'mla_g_k': mla_g_k,
            'diff_g_q': diff_g_q, 'diff_g_k': diff_g_k, 'diff_lambda': diff_lambda, 'diff_g_sub': diff_g_sub,
            'ssd_conv_w': ssd_conv_w, 'ssd_conv_b': ssd_conv_b, 'ssd_dt_bias': ssd_dt_bias,
            'ssd_a_log': ssd_a_log, 'ssd_d': ssd_d, 'ssd_g_norm': ssd_g_norm,
            'g_ffn': g_ffn, 'moe_w_group': moe_w_group, 'moe_b_group': moe_b_group,
            'moe_w_expert': moe_w_expert, 'moe_b_expert': moe_b_expert,
            'moe_w_gate': moe_w_gate, 'moe_w_up': moe_w_up, 'moe_w_down': moe_w_down}

def reference(x, c, ctx, c_ctx, w_mod, b_mod, g_mix, w_in, w_out, na_g_q, na_g_k, na_rel_bias,
              mla_g_qa, mla_w_qb, mla_g_kva, mla_w_kvb, mla_g_q, mla_g_k,
              diff_g_q, diff_g_k, diff_lambda, diff_g_sub,
              ssd_conv_w, ssd_conv_b, ssd_dt_bias, ssd_a_log, ssd_d, ssd_g_norm,
              g_ffn, moe_w_group, moe_b_group, moe_w_expert, moe_b_expert, moe_w_gate, moe_w_up, moe_w_down):
    bsz, n_lat, d_model = x.shape
    n_ctx = ctx.shape[1]
    cos, sin = _axial_rope(n_lat, x.dtype)
    silu_c = jax.nn.silu(c)
    silu_cc = jax.nn.silu(c_ctx)
    h_lat, h_ctx = x, ctx
    for layer in range(DEPTH):
        ctx_out = layer < DEPTH - 1
        mod_l = jnp.split((silu_c @ w_mod[layer] + b_mod[layer])[:, None, :], 6, axis=-1)
        mod_c = jnp.split(silu_cc @ w_mod[layer] + b_mod[layer], 6, axis=-1)
        a_lat = _rmsnorm(h_lat, g_mix[layer]) * (1 + mod_l[1]) + mod_l[0]
        a_ctx = _rmsnorm(h_ctx, g_mix[layer]) * (1 + mod_c[1]) + mod_c[0]
        p_lat = jnp.split(a_lat @ w_in[layer], SPLIT_AT, axis=-1)
        p_ctx = jnp.split(a_ctx @ w_in[layer], SPLIT_AT, axis=-1)
        lam_init = 0.8 - 0.6 * math.exp(-0.3 * layer)
        outs = [
            _na_mixer(p_ctx[0], p_lat[0], na_g_q[layer], na_g_k[layer], na_rel_bias[layer], ctx_out),
            _mla_mixer(p_ctx[1], p_lat[1], cos, sin, mla_g_qa[layer], mla_w_qb[layer], mla_g_kva[layer],
                       mla_w_kvb[layer], mla_g_q[layer], mla_g_k[layer], ctx_out),
            _diff_mixer(p_ctx[2], p_lat[2], cos, sin, diff_g_q[layer], diff_g_k[layer], diff_lambda[layer],
                        diff_g_sub[layer], lam_init, ctx_out),
            _ssd_mixer(p_ctx[3], p_lat[3], ssd_conv_w[layer], ssd_conv_b[layer], ssd_dt_bias[layer],
                       ssd_a_log[layer], ssd_d[layer], ssd_g_norm[layer], ctx_out),
        ]
        h_lat = h_lat + mod_l[2] * (jnp.concatenate([o[1] for o in outs], axis=-1) @ w_out[layer])
        if ctx_out:
            h_ctx = h_ctx + mod_c[2] * (jnp.concatenate([o[0] for o in outs], axis=-1) @ w_out[layer])
        moe_p = (moe_w_group[layer], moe_b_group[layer], moe_w_expert[layer], moe_b_expert[layer],
                 moe_w_gate[layer], moe_w_up[layer], moe_w_down[layer])
        f_lat = (_rmsnorm(h_lat, g_ffn[layer]) * (1 + mod_l[4]) + mod_l[3]).reshape(-1, d_model)
        if ctx_out:
            f_ctx = (_rmsnorm(h_ctx, g_ffn[layer]) * (1 + mod_c[4]) + mod_c[3]).reshape(-1, d_model)
            y = _hier_moe(jnp.concatenate([f_ctx, f_lat], axis=0), *moe_p)
            n_ctx_tok = f_ctx.shape[0]
            h_ctx = h_ctx + mod_c[5] * y[:n_ctx_tok].reshape(bsz, n_ctx, d_model)
            y_lat = y[n_ctx_tok:]
        else:
            y_lat = _hier_moe(f_lat, *moe_p)
        h_lat = h_lat + mod_l[5] * y_lat.reshape(bsz, n_lat, d_model)
    return h_lat


_drawn_inputs = setup_inputs


def setup_inputs(seed=0):
    import zlib

    import numpy as np

    out = dict(_drawn_inputs(seed))
    spreads = {}
    factors = {'g_mix': 5.407,
     'na_g_q': 8.0,
     'na_g_k': 8.0,
     'na_rel_bias': 8.0,
     'mla_g_qa': 8.0,
     'mla_g_kva': 8.0,
     'mla_g_q': 8.0,
     'mla_g_k': 8.0,
     'diff_g_q': 8.0,
     'diff_g_k': 8.0,
     'diff_lambda': 4.279,
     'diff_g_sub': 8.0,
     'ssd_conv_b': 6.153,
     'ssd_d': 102.442,
     'ssd_g_norm': 7.896,
     'g_ffn': 3.72,
     'moe_b_group': 7.813,
     'moe_b_expert': 8.0}
    for name, (base, spread) in spreads.items():
        noise = np.random.default_rng([zlib.crc32(name.encode()), seed]).standard_normal(out[name].shape)
        drawn = base * np.exp(spread * noise) if base else spread * noise
        out[name] = jnp.asarray(drawn.astype(out[name].dtype))
    for name, factor in factors.items():
        out[name] = (out[name] * factor).astype(out[name].dtype)
    return out
```

```python
from contextlib import ExitStack
import math

import numpy as np
import concourse.bass as bass
from concourse import mybir

ALU = mybir.AluOpType
ACT = mybir.ActivationFunctionType
AX = mybir.AxisListType
F32 = mybir.dt.float32
I32 = mybir.dt.int32

P = 128
D = 1024
DC = D // P
LAYERS = 2
CTX = 256
SEQ = 512
N = CTX + SEQ
NT = N // P
CT = CTX // P
GRID = 64
NA_KH, NA_KW = 8, 16
ROFF = 2 * NA_KH - 1
COFF = 2 * NA_KW - 1
HEADS = 4
HD = 64
MLA_D = 96
DQK = 32
GW = 256
STATE = 128
CONV = 5
EPS = 1e-6
BIG = 1e30

NA0, MLA0, DIF0, Z0 = 0, 768, 1184, 1952
XBC0, DT0, N_IN = 2208, 2976, 2984
PW = XBC0 + 8
PDT = XBC0
XBC = DT0 - XBC0
XM = XBC // P

REL_PAD = GRID
REL_W = HEADS * ROFF * COFF + 2 * REL_PAD

EXP, EPG, GROUPS, FF = 16, 4, 4, 512
FC = FF // P
TOPK = 2

C_ID, C_U, C_L, C_SU, C_ONE = 0, 128, 256, 384, 512
C_MASK = 640
C_COS = C_MASK + GRID
C_SIN = C_COS + 4 * 16
C_THR = C_SIN + 4 * 16
C_TRI = C_THR + NT
C_BLK = C_TRI + EXP * EXP
NBMAX = N * TOPK // P + EXP
C_DEC = C_BLK + NBMAX
C_TOK = C_DEC + EXP
C_W = C_TOK + NT

ROWS = [("na_g_q", 64), ("na_g_k", 64), ("mla_g_qa", 256), ("mla_g_kva", 128), ("mla_g_q", 96),
        ("mla_g_k", 96), ("diff_g_q", 32), ("diff_g_k", 32), ("diff_g_sub", 64), ("ssd_g_norm", 256),
        ("ssd_dt_bias", 8), ("ssd_a_log", 8), ("ssd_d", 8), ("diff_lambda", 128),
        ("moe_b_group", 4), ("moe_b_expert", 16)]
ROW_AT = {}
_at = 0
for _name, _w in ROWS:
    ROW_AT[_name] = (_at, _w)
    _at += _w
ROWS_W = _at

A_B = 0
A_C = A_B + DC * N
A_D = A_C + NT * PW
XW = N + 4
A_RAW = A_D + XM * XW
RAWW = XW + 4
A_E = A_RAW + 2 * RAWW
E_W = 8192
A_F = A_E + E_W
F_KM, F_KN, F_XB = 0, 3072, 6144
ARENA = A_F + 9216
M_W = A_B + DC * N
M_WSET = 2 * DC * FF + FC * D
M_X = 0
M_Y = M_W + 2 * M_WSET


LAM_INIT = [0.8 - 0.6 * math.exp(-0.3 * layer) for layer in range(LAYERS)]


def constants():
    c = np.zeros((P, C_W), np.float32)
    i = np.arange(P)
    c[:, C_ID:C_ID + P] = np.eye(P)
    c[:, C_U:C_U + P] = i[:, None] <= i[None, :]
    c[:, C_L:C_L + P] = i[:, None] >= i[None, :]
    c[:, C_SU:C_SU + P] = i[:, None] < i[None, :]
    c[:, C_ONE:C_ONE + P] = 1.0
    q, k = np.arange(GRID)[:, None], np.arange(GRID)[None, :]
    lo = np.clip(q - NA_KW // 2, 0, GRID - NA_KW)
    m = np.where((k >= lo) & (k < lo + NA_KW), 0.0, -BIG)
    c[:, C_MASK:C_MASK + GRID] = np.concatenate([m, m])
    inv = np.power(np.float32(10000.0), -np.arange(8, dtype=np.float32) / np.float32(8)).astype(np.float32)
    t = np.arange(SEQ)
    ang = np.concatenate([(t // GRID).astype(np.float32)[:, None] * inv,
                          (t % GRID).astype(np.float32)[:, None] * inv], axis=-1)
    c[:, C_COS:C_COS + 64] = np.cos(ang).astype(np.float32).reshape(4, P, 16).transpose(1, 0, 2).reshape(P, 64)
    c[:, C_SIN:C_SIN + 64] = np.sin(ang).astype(np.float32).reshape(4, P, 16).transpose(1, 0, 2).reshape(P, 64)
    c[:, C_THR:C_THR + NT] = P * np.arange(NT)
    e = np.arange(EXP)
    c[:, C_TRI:C_TRI + EXP * EXP] = (e[None, :] < e[:, None]).astype(np.float32).reshape(-1)
    c[:, C_BLK:C_BLK + NBMAX] = np.arange(NBMAX)
    c[:, C_DEC:C_DEC + EXP] = EXP - e
    c[:, C_TOK:C_TOK + NT] = i[:, None] + P * np.arange(NT)[None, :]
    return c


def bc(ap, *free):
    return bass.AP(ap.tensor, ap.offset, [list(ap.ap[0])] + [list(x) for x in free])


class Chain:

    def __init__(self, eng, sem):
        self.eng, self.sem, self.n = eng, sem, 0

    def __call__(self, ins):
        self.n += 1
        ins.then_inc(self.sem, 1)
        self.eng.wait_ge(self.sem, self.n)


def build(nc, io, out):
    st = ExitStack()
    with st:
        sems = {}

        def S(name):
            if name not in sems:
                sems[name] = st.enter_context(nc.semaphore(name))
            return sems[name]

        def sb(name, w, dt=F32):
            return st.enter_context(nc.sbuf_tensor(name, [P, w], dt))

        hT_ = sb("hT", DC * N)
        X = sb("arena", ARENA)
        K = sb("consts", C_W)
        rows = sb("rows", ROWS_W)
        modcol = sb("modcol", LAYERS * 48 * 2)
        acol = sb("acol", LAYERS * 2 * DC * 2)
        gcol = sb("gcol", LAYERS * 2 * DC)
        convw = sb("convw", LAYERS * XM * 6)
        ss = sb("ss", NT * 26)
        ss2 = sb("ss2", NT * 8)
        sc = sb("sc", 32)
        cc = sb("cc", 16)
        ssd = sb("ssd", 10 * 48)
        att = sb("att_small", 16)
        wtok = sb("wtok", NT * TOPK)
        dest = sb("dest", NT * TOPK, I32)
        tokid = sb("tokid", NT, I32)
        blk_e = sb("blk_e", NBMAX, I32)
        slots = sb("slots", NBMAX, I32)
        slot1 = sb("slot1", 2, I32)

        PS = st.enter_context(nc.psum_tensor("ps", [P, 8, 512], F32))

        dram = {}
        for nm, shape, dt in (("slot_tok", (NBMAX * P, 1), I32), ("f_rows", (N + 1, D), F32),
                              ("y_rows", (NBMAX * P, D), F32), ("rel_rows", (LAYERS * GRID, REL_W), F32)):
            dram[nm] = nc.dram_tensor(nm, shape, dt).ap()

        hT = hT_[:, :].rearrange("p (c n) -> p c n", c=DC)

        def ar(off, n):
            return X[:, off:off + n]

        aT = ar(A_B, DC * N).rearrange("p (c n) -> p c n", c=DC)
        ot = ar(A_B, NT * D).rearrange("p (t d) -> p t d", t=NT)
        p = ar(A_C, NT * PW).rearrange("p (t d) -> p t d", t=NT)
        oT = ar(A_C, DC * N).rearrange("p (c n) -> p c n", c=DC)
        xbcT = ar(A_D, XM * XW).rearrange("p (m n) -> p m n", m=XM)
        raw = ar(A_RAW, 2 * RAWW).rearrange("p (b n) -> p b n", b=2)
        sq2 = ar(A_RAW, 2 * N).rearrange("p (b n) -> p b n", b=2)
        wbuf = ar(A_E, E_W).rearrange("p (b k n) -> p b k n", b=2, k=DC)
        kTm = ar(A_F + F_KM, 4 * N).rearrange("p (h n) -> p h n", h=4)
        kTn = ar(A_F + F_KN, 4 * N).rearrange("p (h n) -> p h n", h=4)
        xB = ar(A_F + F_XB, NT * 512).rearrange("p (t d) -> p t d", t=NT)
        ident = K[:, C_ID:C_ID + P]
        triU = K[:, C_U:C_U + P]
        triL = K[:, C_L:C_L + P]
        strictU = K[:, C_SU:C_SU + P]
        ones = K[:, C_ONE:C_ONE + P]
        mod4 = modcol[:, :].rearrange("p (l j s) -> p l j s", l=LAYERS, s=2)
        acol4 = acol[:, :].rearrange("p (l w c s) -> p l w c s", l=LAYERS, w=2, s=2)
        gcol3 = gcol[:, :].rearrange("p (l w c) -> p l w c", l=LAYERS, w=2)
        cw = convw[:, :].rearrange("p (l m j) -> p l m j", l=LAYERS, j=6)

        def row(name, off=0, n=None):
            a, w = ROW_AT[name]
            return rows[:, a + off:a + off + (n or w)]

        def xcol(t):
            return t * P if t < CT else t * P + 4

        def out_tiles(L):
            return list(range(NT)) if L < LAYERS - 1 else list(range(CT, NT))

        def streams(lo, hi):
            r = []
            if lo < CTX:
                r.append((1, lo, CTX))
            r.append((0, max(lo, CTX), hi))
            return r

        def tok_lo(L):
            return 0 if L < LAYERS - 1 else CTX

        def segs(lo):
            return [(0, 512), (512, N)] if lo == 0 else [(CTX, N)]

        MODN = 6 * D // 512
        mod_jobs = [(L, n) for L in range(LAYERS) for n in range(MODN)]
        CH = [("x", 0, 4), ("x", 4, 2), ("t", 0, 512), ("t", 512, 512), ("t", 1024, 512), ("t", 1536, 512),
              ("t", 2048, 168)]
        NCH = len(CH)
        NTOKCH = sum(1 for c in CH if c[0] == "t")

        def units(L):
            r = []
            for g, nh in (("mla", 4), ("na", 4), ("dif", 8)):
                for t in out_tiles(L):
                    r += [(g, h, t) for h in range(nh)]
            return r

        UN = [units(L) for L in range(LAYERS)]
        U0 = [0, len(UN[0])]
        ALLU = UN[0] + UN[1]
        FULLS = [0]
        for _g, _h, _t in ALLU:
            FULLS.append(FULLS[-1] + (1 if _t >= CT else 0))
        PERJOB = {"mla": 1, "na": 2, "dif": 4}
        JOB = []
        jobs = []
        for _u, (_g, _h, _t) in enumerate(ALLU):
            if _h % PERJOB[_g] == 0:
                jobs.append((_u, _g, _h, _t))
            JOB.append(len(jobs) - 1)
        SU = []
        for L in range(LAYERS):
            o0, o1 = [0, 1, 2, 3, 4, 5], [1, 0, 5, 4, 3, 2]
            SU += [(L, dd, o[i]) for i in range(NT) for dd, o in ((0, o0), (1, o1))]
        YU = [0]
        for L, dd, t in SU:
            YU.append(YU[-1] + (1 if t in out_tiles(L) else 0))
        NB = [len(out_tiles(L)) * P * TOPK // P + EXP for L in range(LAYERS)]
        NB0 = [0, NB[0]]
        OT0 = [0, NT]
        OTN = [NT, NT - CT]

        modrow = ar(A_C, LAYERS * 6 * D)

        def mod_w(i):
            return ar(A_E + (i % 3) * 4096, 4096)

        rs = ar(A_F + 3264, N)
        cT = ar(A_E, 3 * N).rearrange("p (c n) -> p c n", c=3)
        wqb = ar(A_E + 2304, 768)
        wkvb = ar(A_E + 3072, 512)
        scr = A_E + 3584
        Pb = ar(A_E, 2 * N).rearrange("p (b n) -> p b n", b=2)
        PTb = ar(A_E + 2 * N, 2 * N).rearrange("p (b n) -> p b n", b=2)
        qT = ar(A_E + 4 * N, 2 * P).rearrange("p (b n) -> p b n", b=2)
        bias4 = ar(A_E + 4352, HEADS * ROFF * GRID).rearrange("p (h r c) -> p h r c", h=HEADS, r=ROFF)
        wo = ar(A_E, E_W)

        def sv(k):
            return ssd[:, k * 48:(k + 1) * 48].rearrange("p (t h) -> p t h", t=NT)

        def GMb(w):
            return ar(A_E + 256 * (YU[w] % 2), 256)

        def Mall(w):
            return ar(A_E + 512 + 512 * (YU[w] % 2), 512)

        def Mb(w, h):
            return Mall(w)[:, h * P:(h + 1) * P]

        def xdt(w):
            return ar(A_E + 1536 + 256 * (w % 2), 256)

        def xdte(w):
            return ar(A_E + 2048 + 256 * (w % 2), 256)

        def state(dd):
            return ar(A_E + 2560 + 256 * dd, 256)

        ytmp = ar(A_E + 3072, 256)
        ftok = ar(A_F, 2 * D).rearrange("p (b n) -> p b n", b=2)
        zrow = ar(A_F + 2 * D, D)[0:1, :]
        wr = ar(A_F + 3 * D, DC * 20).rearrange("p (k n) -> p k n", k=DC)
        RT = A_F + 4 * D

        def r_(off, n):
            return ar(RT + off, n)

        r_lg = r_(0, 120).rearrange("p (t n) -> p t n", t=NT)
        r_oh = [r_(420, 96).rearrange("p (t e) -> p t e", t=NT), r_(516, 96).rearrange("p (t e) -> p t e", t=NT)]
        r_sel = r_(612, 96).rearrange("p (t e) -> p t e", t=NT)

        def r6(k):
            return r_(168 + 6 * k, 6)

        def xg(par):
            return ar(M_X + par * D, D)

        def xT(par):
            return ar(M_X + 2 * D + par * D, D)

        def hid(par):
            return ar(M_X + 4 * D + par * FF, FF)

        def hidT(par):
            return ar(M_X + 4 * D + 2 * FF + par * FF, FF)

        def ysb(par):
            return ar(M_Y + par * D, D)

        def moe_w(par):
            o = M_W + par * M_WSET
            return (ar(o, DC * FF).rearrange("p (k n) -> p k n", k=DC),
                    ar(o + DC * FF, DC * FF).rearrange("p (k n) -> p k n", k=DC),
                    ar(o + 2 * DC * FF, FC * D).rearrange("p (k n) -> p k n", k=FC))

        def r12(i, k):
            return ar(A_F + 4 * D + (2 * (i % 2) + k) * D, D)

        restok = ftok

        def win_loads(L, j):
            n = [sum(2 if q == NCH - 1 else 1 for q in range(top) if q % 2 == j % 2) for top in (NCH, j + 1)]
            return 16 * (n[0] * L + n[1])

        def win_done(L, j):
            if CH[j][0] == "x":
                return S("xp_ps"), XM * L + CH[j][1] + CH[j][2]
            return S("pj_ps"), NTOKCH * NT * L + NT * (j - (NCH - NTOKCH) + 1)

        def cnt2(L, i):
            return NT // 2 * L + i // 2

        block = st.enter_context(nc.Block())

        @block.sync
        def _(sp):
            sp.dma_start(K[:, :], io["consts"]).then_inc(S("consts_in"), 16)
            with nc.allow_non_contiguous_dma(reason="small columns"):
                sp.dma_start(cc[:, 0:8], io["c"][0].rearrange("(k p) -> p k", p=P)).then_inc(S("cc_in"), 16)
                sp.dma_start(cc[:, 8:16], io["c_ctx"].rearrange("(k p) -> p k", p=P)).then_inc(S("cc_in"), 16)
            for t in range(NT):
                src = io["ctx"][0, t * P:(t + 1) * P, :] if t < CT else io["x"][0, (t - CT) * P:(t - CT + 1) * P, :]
                sp.dma_start(ar(A_B + t * D, D), src).then_inc(S("x_in"), 16)
            sp.dma_start(modrow[0:2, :],
                         io["b_mod"].rearrange("l n -> (l n)").partition_broadcast(2)).then_inc(S("bmod_in"), 16)
            for i, (L, n) in enumerate(mod_jobs):
                if i >= 3:
                    sp.wait_ge(S("wmod_used"), i - 2)
                sp.dma_start(mod_w(i).rearrange("p (k n) -> p k n", k=DC),
                             io["w_mod"][L].rearrange("(k p) n -> p k n", p=P)[:, :, n * 512:(n + 1) * 512]
                             ).then_inc(S(f"wmod_in{i % 3}"), 16)
                if i == 2:
                    with nc.allow_non_contiguous_dma(reason="small columns"):
                        for l2 in range(LAYERS):
                            for w, nm in ((0, "g_mix"), (1, "g_ffn")):
                                sp.dma_start(gcol3[:, l2, w, :], io[nm][l2].rearrange("(k p) -> p k", p=P)
                                             ).then_inc(S("cols_in"), 16)
                            for m in range(XM):
                                sp.dma_start(cw[:, l2, m, 0:CONV],
                                             io["ssd_conv_w"][l2, :, m * P:(m + 1) * P].rearrange("j p -> p j")
                                             ).then_inc(S("cols_in"), 16)
                            sp.dma_start(cw[:, l2, :, CONV], io["ssd_conv_b"][l2].rearrange("(m p) -> p m", p=P)
                                         ).then_inc(S("cols_in"), 16)
            for l2 in range(LAYERS):
                sp.dma_start(dram["rel_rows"][l2 * GRID:(l2 + 1) * GRID, :], io["rel_pad"][l2].partition_broadcast(GRID)
                             ).then_inc(S("rel_copied"), 16)
            for L in range(LAYERS):
                if L:
                    sp.wait_ge(S("h_final"), 1)
                for nm, w in ROWS:
                    src = io[nm][L]
                    if len(src.shape) == 2:
                        src = src.rearrange("a b -> (a b)")
                    sp.dma_start(row(nm), src.partition_broadcast(P)).then_inc(S("rows_in"), 16)
                if L == 0:
                    sp.wait_ge(S("wmod_used"), len(mod_jobs))
                for j, ch in enumerate(CH):
                    if j >= 2:
                        sp.wait_ge(*win_done(L, j - 2))
                    src = io["w_in"][L].rearrange("(k p) n -> p k n", p=P)
                    b = wbuf[:, j % 2]
                    if ch[0] == "x":
                        a, w = XBC0 + ch[1] * P, ch[2] * P
                        sp.dma_start(b[:, :, 0:w], src[:, :, a:a + w]).then_inc(S(f"win_in{j % 2}"), 16)
                    elif ch[2] == 512:
                        sp.dma_start(b, src[:, :, ch[1]:ch[1] + 512]).then_inc(S(f"win_in{j % 2}"), 16)
                    else:
                        sp.dma_start(b[:, :, 0:160], src[:, :, ch[1]:XBC0]).then_inc(S(f"win_in{j % 2}"), 16)
                        with nc.allow_non_contiguous_dma(reason="dt columns"):
                            sp.dma_start(b[:, :, 160:168], src[:, :, DT0:N_IN]).then_inc(S(f"win_in{j % 2}"), 16)
                sp.wait_ge(*win_done(L, NCH - 1))
                sp.dma_start(wqb.rearrange("p (k n) -> p k n", k=2),
                             io["mla_w_qb"][L].rearrange("(k p) n -> p k n", p=P)).then_inc(S("wmla_in"), 16)
                sp.dma_start(wkvb, io["mla_w_kvb"][L]).then_inc(S("wmla_in"), 16)
                sp.wait_ge(S("m_norm"), L + 1)
                sp.wait_ge(S("rel_copied"), 16 * LAYERS)
                rb = dram["rel_rows"]
                for half in range(2):
                    base = rb.offset + L * GRID * REL_W + REL_PAD + (NA_KW - 1)
                    n_ro = ROFF - half
                    for h in range(HEADS):
                        dst = bias4[64 * half:64 * half + 64, h, half:ROFF, :]
                        src = bass.AP(rb.tensor, base + h * ROFF * COFF, [[REL_W - 1, GRID], [COFF, n_ro], [1, GRID]])
                        sp.dma_start(dst, src).then_inc(S("bias_in"), 16)
                sp.wait_ge(S("mix_done"), L + 1)
                sp.dma_start(wo.rearrange("p (k n) -> p k n", k=DC),
                             io["w_out"][L].rearrange("(k p) n -> p k n", p=P)).then_inc(S("wo_in"), 16)
                sp.wait_ge(S("h_mid"), L + 1)
                with nc.allow_non_contiguous_dma(reason="router columns"):
                    sp.dma_start(wr[:, :, 0:GROUPS], io["moe_w_group"][L].rearrange("(k p) n -> p k n", p=P)
                                 ).then_inc(S("wr_in"), 16)
                    sp.dma_start(wr[:, :, GROUPS:], io["moe_w_expert"][L].rearrange("(k p) n -> p k n", p=P)
                                 ).then_inc(S("wr_in"), 16)
                for i, t in enumerate(out_tiles(L)):
                    sp.wait_ge(S("ftok_a"), OT0[L] + i + 1)
                    sp.wait_ge(S("ftok_d"), OT0[L] + i + 1)
                    sp.dma_start(dram["f_rows"][t * P:(t + 1) * P, :], ftok[:, i % 2, :]).then_inc(S(f"f_out{i % 2}"), 16)
                if L == 0:
                    sp.wait_ge(S("zero_row"), 1)
                    sp.dma_start(dram["f_rows"][N:N + 1, :], zrow).then_inc(S("zrow_out"), 16)
                sp.wait_ge(S("slots_fill"), L + 1)
                sp.dma_start(dram["slot_tok"].rearrange("(p b) o -> p (b o)", p=P), slots[:, :]).then_inc(S("slots_init"), 16)
                sp.wait_ge(S("slot_scat"), 16 * TOPK * (OT0[L] + OTN[L]))
                with nc.allow_non_contiguous_dma(reason="slot columns"):
                    sp.dma_start(slots[:, :], dram["slot_tok"].rearrange("(b p) o -> p (b o)", p=P)).then_inc(S("slots_in"), 16)
                wgv = io["moe_w_gate"][L].rearrange("e (k p) n -> e p k n", p=P)
                wuv = io["moe_w_up"][L].rearrange("e (k p) n -> e p k n", p=P)
                wdv = io["moe_w_down"][L].rearrange("e (k p) n -> e p k n", p=P)
                sp.wait_ge(S("blk_ready"), L + 1)

                def load_block(i, par, first):
                    b = 2 * i + par
                    e = sp.value_load(blk_e[0:1, bass.ds(b, 1)], min_val=0, max_val=EXP - 1)
                    if not first:
                        sp.wait_ge(S("dn_ps"), NB0[L] + b - 1)
                    wg, wu, wd = moe_w(par)
                    for dst, v in ((wg, wgv), (wu, wuv)):
                        sp.dma_start(dst, v[bass.ds(e, 1)].rearrange("e p k n -> p (e k) n")).then_inc(S(f"gu_in{par}"), 16)
                    sp.dma_start(wd, wdv[bass.ds(e, 1)].rearrange("e p k n -> p (e k) n")).then_inc(S(f"wd_in{par}"), 16)

                for par in range(2):
                    load_block(0, par, True)
                with sp.Fori(1, NB[L] // 2) as i:
                    for par in range(2):
                        load_block(i, par, False)
            for i in range(NT - CT):
                sp.wait_ge(S("res_a"), i + 1)
                sp.wait_ge(S("res_d"), i + 1)
                sp.dma_start(out[0, i * P:(i + 1) * P, :], restok[:, i % 2, :]).then_inc(S(f"res_out{i % 2}"), 16)
            for q in range(2):
                sp.wait_ge(S(f"res_out{q}"), 16 * ((NT - CT) // 2))

        @block.tensor
        def _(pe):
            pe.wait_ge(S("consts_in"), 16)
            pe.wait_ge(S("x_in"), 16 * NT)
            for t in range(NT):
                if t >= 2:
                    pe.wait_ge(S("x_ev_a"), t - 1)
                    pe.wait_ge(S("x_ev_d"), t - 1)
                for c in range(DC):
                    last = pe.transpose(PS[:, 2 * (t % 2) + c // 4, (c % 4) * P:(c % 4 + 1) * P],
                                        ar(A_B + t * D + c * P, P), ident)
                last.then_inc(S("x_ps"), 1)
            pe.wait_ge(S("cc_silu"), 1)
            for i in range(len(mod_jobs)):
                pe.wait_ge(S(f"wmod_in{i % 3}"), 16 * (i // 3 + 1))
                if i >= 2:
                    pe.wait_ge(S("mod_ev"), i - 1)
                for k in range(DC):
                    last = pe.matmul(PS[0:2, 4 + i % 2, :], bc(cc[:, k:k + 1], (8, 2)),
                                     mod_w(i)[:, k * 512:(k + 1) * 512], start=(k == 0), stop=(k == DC - 1))
                last.then_inc(S("wmod_used"), 1)
            pe.wait_ge(S("mod_ev"), len(mod_jobs))
            for j in range(LAYERS * 48):
                last = pe.transpose(PS[:, 6, 2 * j:2 * j + 2], modrow[0:2, j * P:(j + 1) * P], ident[0:2, 0:2])
            last.then_inc(S("modT_ps"), 1)

            def norm_sums(L, w):
                lo = 0 if w == 0 else tok_lo(L)
                base = (2 * L + w) * DC
                for c in range(DC):
                    pe.wait_ge(S("sq_done"), base + c + 1)
                    for bk, (a, b) in enumerate(segs(lo)):
                        last = pe.matmul(PS[:, bk, 0:b - a], ones, sq2[:, c % 2, a:b], start=(c == 0), stop=(c == DC - 1))
                    last.then_inc(S("sq_used"), 1)

            def in_proj(L):
                pe.wait_ge(S("aT_ready"), L + 1)
                k = 0
                for j, ch in enumerate(CH):
                    pe.wait_ge(S(f"win_in{j % 2}"), win_loads(L, j))
                    if ch[0] == "x":
                        for m in range(ch[1], ch[1] + ch[2]):
                            if m >= 2:
                                pe.wait_ge(S("raw_ready"), XM * L + m - 1)
                            mm = m - ch[1]
                            for bk, (a, b) in enumerate(segs(0)):
                                for c in range(DC):
                                    last = pe.matmul(PS[:, 2 * (m % 2) + bk, 0:b - a],
                                                     wbuf[:, j % 2, c, mm * P:(mm + 1) * P], aT[:, c, a:b],
                                                     start=(c == 0), stop=(c == DC - 1))
                            last.then_inc(S("xp_ps"), 1)
                    else:
                        for t in range(NT):
                            if k >= 4:
                                pe.wait_ge(S("pj_ev"), NTOKCH * NT * L + k - 3)
                            for c in range(DC):
                                last = pe.matmul(PS[:, 4 + k % 4, 0:ch[2]], aT[:, c, t * P:(t + 1) * P],
                                                 wbuf[:, j % 2, c, 0:ch[2]], start=(c == 0), stop=(c == DC - 1))
                            last.then_inc(S("pj_ps"), 1)
                            k += 1

            def mla_prep(L):
                pe.wait_ge(S("stats_done"), L + 1)
                for t in range(NT):
                    if t >= 2:
                        pe.wait_ge(S("cT_ev"), NT * L + t - 1)
                    for c in range(3):
                        last = pe.transpose(PS[:, t % 2, c * P:(c + 1) * P], p[:, t, MLA0 + c * P:MLA0 + (c + 1) * P], ident)
                    last.then_inc(S("cT_ps"), 1)
                pe.wait_ge(S("wmla_in"), 32 * (L + 1))
                for t in range(NT):
                    pe.wait_ge(S("cT_ev"), NT * L + t + 1)
                    if t >= 2:
                        pe.wait_ge(S("mq_ev"), NT * L + t - 1)
                        pe.wait_ge(S("mkv_ev"), NT * L + t - 1)
                    for c in range(2):
                        pe.matmul(PS[:, 2 + t % 2, 0:384], cT[:, c, t * P:(t + 1) * P], wqb[:, c * 384:(c + 1) * 384],
                                  start=(c == 0), stop=(c == 1))
                    last = pe.matmul(PS[:, 4 + t % 2, :], cT[:, 2, t * P:(t + 1) * P], wkvb, start=True, stop=True)
                    last.then_inc(S("mla_ps"), 1)

            def key_transposes(L):
                pe.wait_ge(S("xbc_ready"), XM * (L + 1))
                for n in range(3 * NT):
                    kind, t = n // NT, n % NT
                    if n >= 2:
                        pe.wait_ge(S("kt_ev"), 3 * NT * L + n - 1)
                    if n == 0:
                        pe.wait_ge(S("na_norm"), L + 1)
                        pe.wait_ge(S("dif_norm"), L + 1)
                    if kind == 2 and t == 0:
                        pe.wait_ge(S("m_norm"), L + 1)
                    for q in range(4):
                        if kind == 0:
                            a = NA0 + 256 + q * P if q < 2 else DIF0 + 256 + (q - 2) * P
                            src, rows_ = p[:, t, a:a + P], P
                        elif kind == 1:
                            src, rows_ = xbcT[:, q, xcol(t):xcol(t) + P], P
                        else:
                            a = 640 + MLA_D * q
                            src, rows_ = ot[:, t, a:a + MLA_D], MLA_D
                        last = pe.transpose(PS[0:rows_, 6 + n % 2, q * P:(q + 1) * P], src, ident)
                    last.then_inc(S("kt_ps"), 1)

            def attention(L):
                n, u0 = len(UN[L]), U0[L]
                pe.wait_ge(S("kt_ev"), 3 * NT * (L + 1))

                def q_transpose(j):
                    _, g, h, t = jobs[j]
                    if j:
                        pe.wait_ge(S("qT_ev"), j)
                    if g == "mla":
                        src, r = ot[:, t, 256 + MLA_D * h:256 + MLA_D * (h + 1)], MLA_D
                    elif g == "na":
                        src, r = p[:, t, NA0 + HD * h:NA0 + HD * h + P], P
                    else:
                        src, r = p[:, t, DIF0 + DQK * h:DIF0 + DQK * h + P], P
                    pe.transpose(PS[0:r, 7, 0:P], src, ident).then_inc(S("qT_ps"), 1)

                for i in range(n + 2):
                    if i < n:
                        u = u0 + i
                        g, h, t = ALLU[u]
                        if i == 0:
                            q_transpose(JOB[u])
                        if i + 1 < n and JOB[u + 1] != JOB[u]:
                            q_transpose(JOB[u + 1])
                        pe.wait_ge(S("qT_ev"), JOB[u] + 1)
                        if u >= 2:
                            pe.wait_ge(S("exp_done"), u - 1)
                        qb = qT[:, JOB[u] % 2]
                        if g == "mla":
                            lo, hi, kt = 0, MLA_D, kTm[:, h]
                        elif g == "na":
                            lo, hi, kt = HD * (h % 2), HD * (h % 2) + HD, kTn[:, h // 2]
                        else:
                            lo, hi, kt = DQK * (h % 4), DQK * (h % 4) + DQK, kTn[:, 2 + h // 4]
                        if g == "na" and t == CT:
                            pe.wait_ge(S("bias_ready"), L + 1)
                        b0 = 2 * (u % 2)
                        full = t >= CT
                        bias = g == "na" and full
                        last = pe.matmul(PS[:, b0, 0:(512 if full else CTX)], qb[lo:hi], kt[lo:hi, 0:(512 if full else CTX)],
                                         start=True, stop=not bias, skip_group_check=True)
                        if full:
                            last = pe.matmul(PS[:, b0 + 1, 0:256], qb[lo:hi], kt[lo:hi, 512:N], start=True,
                                             stop=not bias, skip_group_check=True)
                        if bias:
                            s0 = NA_KH - 1 - 2 * (t - CT)
                            pe.matmul(PS[:, b0, 256:512], ident, bias4[:, h, s0:s0 + 4, :], start=False, stop=True,
                                      skip_group_check=True)
                            last = pe.matmul(PS[:, b0 + 1, 0:256], ident, bias4[:, h, s0 + 4:s0 + 8, :], start=False,
                                             stop=True, skip_group_check=True)
                        last.then_inc(S("s_ps"), 1)
                    if 1 <= i <= n:
                        u = u0 + i - 1
                        t = ALLU[u][2]
                        pe.wait_ge(S("exp_done"), u + 1)
                        if u >= 1:
                            pe.wait_ge(S("pt_ev_a"), u)
                            if FULLS[u]:
                                pe.wait_ge(S("pt_ev_d"), FULLS[u])
                        for c in range(NT if t >= CT else CT):
                            last = pe.transpose(PS[:, 4 + c // 4, (c % 4) * P:(c % 4 + 1) * P],
                                                Pb[:, u % 2, c * P:(c + 1) * P], ident)
                        last.then_inc(S("t_ps"), 1)
                    if i >= 2:
                        u = u0 + i - 2
                        g, h, t = ALLU[u]
                        pe.wait_ge(S("pt_ev_a"), u + 1)
                        if FULLS[u + 1]:
                            pe.wait_ge(S("pt_ev_d"), FULLS[u + 1])
                        if u >= 1:
                            pe.wait_ge(S("o_ev"), u)
                        v0 = {"mla": MLA0 + HD * h, "na": NA0 + 512 + HD * h, "dif": DIF0 + 512 + HD * (h // 2)}[g]
                        nk = NT if t >= CT else CT
                        for c in range(nk):
                            last = pe.matmul(PS[:, 6, 0:HD], PTb[:, u % 2, c * P:(c + 1) * P], p[:, c, v0:v0 + HD],
                                             start=(c == 0), stop=(c == nk - 1))
                        last.then_inc(S("o_ps"), 1)

            def scan(L):
                pe.wait_ge(S("la_done"), L + 1)
                la = sv(0)
                pe.matmul(PS[:, 0, 0:24], triU, la[:, :, 0:4], start=True, stop=True)
                pe.matmul(PS[:, 0, 24:48], triL, la[:, :, 4:8], start=True, stop=True)
                pe.matmul(PS[:, 0, 48:96], ones, la, start=True, stop=True).then_inc(S("cum_ps"), 1)
                pe.wait_ge(S("cum_done"), L + 1)
                n = 2 * NT
                for i in range(n + 1):
                    if i < n:
                        w = n * L + i
                        _, dd, t = SU[w]
                        if t in out_tiles(L):
                            if YU[w] >= 2:
                                pe.wait_ge(S("front_done"), YU[w] - 1)
                            yp = YU[w] % 2
                            tri = triU if dd == 0 else triL
                            for h in range(HEADS):
                                pe.matmul(PS[:, yp, h * P:(h + 1) * P], bc(la[:, t, dd * 4 + h:dd * 4 + h + 1], (0, P)), tri,
                                          start=True, stop=True)
                            x0 = xcol(t)
                            for g in range(2):
                                last = pe.matmul(PS[:, 2 + yp, g * P:(g + 1) * P], xbcT[:, 2 + g, x0:x0 + P],
                                                 xbcT[:, 4 + g, x0:x0 + P], start=True, stop=True)
                            last.then_inc(S("rg_ps"), 1)
                    if i >= 1:
                        w = n * L + i - 1
                        _, dd, t = SU[w]
                        pe.wait_ge(S("xdt_done"), w + 1)
                        if w >= 2:
                            pe.wait_ge(S("state_done"), w - 1)
                        if t in out_tiles(L):
                            pe.wait_ge(S("m_done"), YU[w] + 1)
                            if YU[w] >= 2:
                                pe.wait_ge(S("y_done"), YU[w] - 1)
                            yp = YU[w] % 2
                            x0 = xcol(t)
                            for h in range(HEADS):
                                pe.matmul(PS[:, 4 + yp, h * HD:(h + 1) * HD], Mb(w, h), xdt(w)[:, h * HD:(h + 1) * HD],
                                          start=True, stop=True)
                            for g in range(2):
                                last = pe.matmul(PS[:, 4 + yp, 256 + g * P:256 + (g + 1) * P], xbcT[:, 4 + g, x0:x0 + P],
                                                 state(dd)[:, g * P:(g + 1) * P], start=True, stop=True)
                            last.then_inc(S("y_ps"), 1)
                        for g in range(2):
                            last = pe.matmul(PS[:, 6 + w % 2, g * P:(g + 1) * P], xB[:, t, 256 + g * P:256 + (g + 1) * P],
                                             xdte(w)[:, g * P:(g + 1) * P], start=True, stop=True)
                        last.then_inc(S("st_ps"), 1)

            def out_proj(L):
                pe.wait_ge(S("mix_done"), L + 1)
                for i, t in enumerate(out_tiles(L)):
                    if i >= 2:
                        pe.wait_ge(S("oT_a"), OT0[L] + i - 1)
                        pe.wait_ge(S("oT_d"), OT0[L] + i - 1)
                    for c in range(DC):
                        f = {0: 2, 1: 3, 2: 0, 3: 1}.get(c, c)
                        last = pe.transpose(PS[:, 2 * (i % 2) + c // 4, (c % 4) * P:(c % 4 + 1) * P],
                                            ot[:, t, f * P:(f + 1) * P], ident)
                    last.then_inc(S("oT_ps"), 1)
                pe.wait_ge(S("oT_a"), OT0[L] + OTN[L])
                pe.wait_ge(S("oT_d"), OT0[L] + OTN[L])
                pe.wait_ge(S("wo_in"), 16 * (L + 1))
                for m in range(DC):
                    if m >= 2:
                        pe.wait_ge(S("op_ev"), DC * L + m - 1)
                    for bk, (a, b) in enumerate(segs(tok_lo(L))):
                        for c in range(DC):
                            last = pe.matmul(PS[:, 4 + 2 * (m % 2) + bk, 0:b - a], wo[:, c * D + m * P:c * D + (m + 1) * P],
                                             oT[:, c, a:b], start=(c == 0), stop=(c == DC - 1))
                    last.then_inc(S("op_ps"), 1)

            def route_and_rows(L):
                pe.wait_ge(S("fT_ready"), L + 1)
                pe.wait_ge(S("wr_in"), 32 * (L + 1))
                for t in out_tiles(L):
                    for c in range(DC):
                        last = pe.matmul(PS[:, 4, t * 20:(t + 1) * 20], aT[:, c, t * P:(t + 1) * P], wr[:, c, :],
                                         start=(c == 0), stop=(c == DC - 1))
                last.then_inc(S("lg_ps"), 1)
                for i, t in enumerate(out_tiles(L)):
                    if i >= 2:
                        pe.wait_ge(S("ftok_a"), OT0[L] + i - 1)
                        pe.wait_ge(S("ftok_d"), OT0[L] + i - 1)
                    for c in range(DC):
                        last = pe.transpose(PS[:, 2 * (i % 2) + c // 4, (c % 4) * P:(c % 4 + 1) * P],
                                            aT[:, c, t * P:(t + 1) * P], ident)
                    last.then_inc(S("ftok_ps"), 1)
                pe.wait_ge(S("sel_done"), L + 1)
                tl = out_tiles(L)
                for n_, t in enumerate(tl):
                    for j, t2 in enumerate(tl[:n_ + 1]):
                        pe.matmul(PS[:, 5, t * EXP:(t + 1) * EXP], strictU if t2 == t else ones, r_sel[:, t2, :],
                                  start=(j == 0), stop=(t2 == t))
                for j, t in enumerate(tl):
                    last = pe.matmul(PS[:, 5, NT * EXP:(NT + 1) * EXP], ones, r_sel[:, t, :], start=(j == 0),
                                     stop=(j == len(tl) - 1))
                last.then_inc(S("rank_ps"), 1)

            def experts(L):
                n0 = NB0[L]

                def x_transposes(i, par, first=False):
                    b = 2 * i + par
                    pe.wait_ge(S(f"xg_in{par}"), 16 * (i + 1) + 16 * (n0 // 2))
                    if not first:
                        pe.wait_ge(S("xT_a"), n0 + b)
                        pe.wait_ge(S("xT_d"), n0 + b)
                    for c in range(DC):
                        last = pe.transpose(PS[:, c // 4, (c % 4) * P:(c % 4 + 1) * P], xg(par)[:, c * P:(c + 1) * P], ident)
                    last.then_inc(S("xt_ps"), 1)

                def gate_up(i, par, first=False):
                    b = 2 * i + par
                    wg, wu, _ = moe_w(par)
                    pe.wait_ge(S(f"gu_in{par}"), 32 * (i + 1) + 32 * (n0 // 2))
                    pe.wait_ge(S("xT_a"), n0 + b + 1)
                    pe.wait_ge(S("xT_d"), n0 + b + 1)
                    if not first:
                        pe.wait_ge(S("h_done"), n0 + b)
                    for bk, w in ((2, wg), (3, wu)):
                        for c in range(DC):
                            last = pe.matmul(PS[:, bk, :], xT(par)[:, c * P:(c + 1) * P], w[:, c, :], start=(c == 0),
                                             stop=(c == DC - 1))
                    last.then_inc(S("gu_ps"), 1)

                def down(i, par, first=False):
                    b = 2 * i + par
                    pe.wait_ge(S("h_done"), n0 + b + 1)
                    if not first:
                        pe.wait_ge(S("hT_ev"), n0 + b)
                    for c in range(FC):
                        last = pe.transpose(PS[:, 4, c * P:(c + 1) * P], hid(par)[:, c * P:(c + 1) * P], ident)
                    last.then_inc(S("ht_ps"), 1)
                    _, _, wd = moe_w(par)
                    pe.wait_ge(S("hT_ev"), n0 + b + 1)
                    pe.wait_ge(S(f"wd_in{par}"), 16 * (i + 1) + 16 * (n0 // 2))
                    if not first:
                        pe.wait_ge(S("y_a"), n0 + b)
                        pe.wait_ge(S("y_d"), n0 + b)
                    for half in range(2):
                        for c in range(FC):
                            last = pe.matmul(PS[:, 5 + half, :], hidT(par)[:, c * P:(c + 1) * P],
                                             wd[:, c, half * 512:(half + 1) * 512], start=(c == 0), stop=(c == FC - 1))
                    last.then_inc(S("dn_ps"), 1)

                half_n = NB[L] // 2
                fl = L == 0
                x_transposes(0, 0, fl)
                gate_up(0, 0, fl)
                x_transposes(0, 1)
                down(0, 0, fl)
                gate_up(0, 1)
                x_transposes(1, 0)
                down(0, 1)
                with pe.Fori(1, half_n - 1) as i:
                    gate_up(i, 0)
                    x_transposes(i, 1)
                    down(i, 0)
                    gate_up(i, 1)
                    x_transposes(i + 1, 0)
                    down(i, 1)
                gate_up(half_n - 1, 0)
                x_transposes(half_n - 1, 1)
                down(half_n - 1, 0)
                gate_up(half_n - 1, 1)
                down(half_n - 1, 1)

            def combine(L):
                for i, t in enumerate(out_tiles(L)):
                    pe.wait_ge(S("comb"), OT0[L] + i + 1)
                    if i >= 2:
                        pe.wait_ge(S("hup"), OT0[L] + i - 1)
                    for c in range(DC):
                        last = pe.transpose(PS[:, 2 * (i % 2) + c // 4, (c % 4) * P:(c % 4 + 1) * P],
                                            r12(i, 0)[:, c * P:(c + 1) * P], ident)
                    last.then_inc(S("comb_ps"), 1)

            for L in range(LAYERS):
                norm_sums(L, 0)
                in_proj(L)
                mla_prep(L)
                key_transposes(L)
                attention(L)
                scan(L)
                out_proj(L)
                norm_sums(L, 1)
                route_and_rows(L)
                experts(L)
                combine(L)
            pe.wait_ge(S("h_final"), LAYERS)
            for i, t in enumerate(out_tiles(1)):
                if i >= 2:
                    pe.wait_ge(S("res_a"), i - 1)
                    pe.wait_ge(S("res_d"), i - 1)
                for c in range(DC):
                    last = pe.transpose(PS[:, 2 * (i % 2) + c // 4, (c % 4) * P:(c % 4 + 1) * P],
                                        hT[:, c, t * P:(t + 1) * P], ident)
                last.then_inc(S("res_ps"), 1)

        @block.scalar
        def _(act):
            for t in range(NT):
                act.wait_ge(S("x_ps"), t + 1)
                act.activation(hT[:, 0:4, t * P:(t + 1) * P], PS[:, 2 * (t % 2), :].rearrange("p (c n) -> p c n", c=4),
                               ACT.Copy).then_inc(S("x_ev_a"), 1)
            act.wait_ge(S("cc_in"), 32)
            act.activation(cc[:, :], cc[:, :], ACT.Silu).then_inc(S("cc_silu"), 1)

            def norm(L, w):
                lo = 0 if w == 0 else tok_lo(L)
                base = (2 * L + w) * DC
                if w == 1:
                    act.wait_ge(S("h_mid"), L + 1)
                elif L:
                    act.wait_ge(S("h_final"), L)
                else:
                    act.wait_ge(S("x_ev_d"), NT)
                    act.wait_ge(S("x_ev_a"), NT)
                for c in range(DC):
                    if base + c >= 2:
                        act.wait_ge(S("sq_used"), base + c - 1)
                    act.activation(sq2[:, c % 2, lo:N], hT[:, c, lo:N], ACT.Square).then_inc(S("sq_done"), 1)
                act.wait_ge(S("var_done"), 2 * L + w + 1)
                act.activation(rs[:, lo:N], rs[:, lo:N], ACT.Sqrt).then_inc(S("sqrt_done"), 1)
                act.wait_ge(S("acol_ready"), 1)
                for c in range(DC):
                    act.wait_ge(S("nrm_x"), base + c + 1)
                    for s, a, b in streams(lo, N):
                        last = act.activation(aT[:, c, a:b], aT[:, c, a:b], ACT.Identity,
                                              scale=acol4[:, L, w, c, s:s + 1], bias=mod4[:, L, 24 * w + c, s:s + 1])
                last.then_inc(S("fT_ready" if w else "aT_ready"), 1)

            def in_proj(L):
                act.wait_ge(S("pads_ready"), L + 1)
                for m in range(XM + 1):
                    if m < XM:
                        act.wait_ge(S("xp_ps"), XM * L + m + 1)
                        if m >= 2:
                            act.wait_ge(S("conv_done"), XM * L + m - 1)
                        b0 = 2 * (m % 2)
                        act.activation(raw[:, m % 2, 2:2 + CTX], PS[:, b0, 0:CTX], ACT.Copy)
                        act.activation(raw[:, m % 2, 6 + CTX:6 + 512], PS[:, b0, CTX:512], ACT.Copy)
                        act.activation(raw[:, m % 2, 6 + 512:6 + N], PS[:, b0 + 1, 0:N - 512], ACT.Copy
                                       ).then_inc(S("raw_ready"), 1)
                    if m:
                        act.wait_ge(S("conv_done"), XM * L + m)
                        act.activation(xbcT[:, m - 1, :], xbcT[:, m - 1, :], ACT.Silu).then_inc(S("xbc_ready"), 1)
                k = 0
                for ch in CH:
                    if ch[0] == "t":
                        for t in range(NT):
                            act.wait_ge(S("pj_ps"), NTOKCH * NT * L + k + 1)
                            act.activation(p[:, t, ch[1]:ch[1] + ch[2]], PS[:, 4 + k % 4, 0:ch[2]], ACT.Copy
                                           ).then_inc(S("pj_ev"), 1)
                            k += 1

            def stats(L):
                act.wait_ge(S("pj_ev"), NTOKCH * NT * (L + 1))
                act.activation(ar(scr, NT * 384).rearrange("p (t d) -> p t d", t=NT), p[:, :, MLA0:MLA0 + 384], ACT.Square
                               ).then_inc(S("sq_stats"), 1)
                act.activation(ar(A_B, NT * 512).rearrange("p (t d) -> p t d", t=NT), p[:, :, NA0:NA0 + 512], ACT.Square
                               ).then_inc(S("sq_stats"), 1)
                act.activation(ar(A_B + NT * 512, NT * 512).rearrange("p (t d) -> p t d", t=NT),
                               p[:, :, DIF0:DIF0 + 512], ACT.Square).then_inc(S("sq_stats"), 1)
                act.wait_ge(S("var_s"), L + 1)
                act.activation(ss[:, :], ss[:, :], ACT.Sqrt).then_inc(S("sqrt_s"), 1)

            def mla_prep(L):
                for t in range(NT):
                    act.wait_ge(S("cT_ps"), NT * L + t + 1)
                    act.activation(cT[:, :, t * P:(t + 1) * P], PS[:, t % 2, 0:384].rearrange("p (c n) -> p c n", c=3),
                                   ACT.Copy).then_inc(S("cT_ev"), 1)
                for t in range(NT):
                    act.wait_ge(S("mla_ps"), NT * L + t + 1)
                    act.activation(ot[:, t, 256:640], PS[:, 2 + t % 2, 0:384], ACT.Copy).then_inc(S("mq_ev"), 1)
                act.wait_ge(S("mq_ev"), NT * (L + 1))
                act.wait_ge(S("mkv_ev"), NT * (L + 1))
                act.activation(ar(scr, NT * 768).rearrange("p (t d) -> p t d", t=NT), ot[:, :, 256:1024], ACT.Square
                               ).then_inc(S("sq_m"), 1)
                act.wait_ge(S("var_m"), L + 1)
                act.activation(ss2[:, :], ss2[:, :], ACT.Sqrt).then_inc(S("sqrt_m"), 1)
                for n in range(3 * NT):
                    kind, t = n // NT, n % NT
                    act.wait_ge(S("kt_ps"), 3 * NT * L + n + 1)
                    src = PS[:, 6 + n % 2, :].rearrange("p (q n) -> p q n", q=4)
                    if kind == 0:
                        act.activation(kTn[:, :, t * P:(t + 1) * P], src, ACT.Copy).then_inc(S("kt_ev"), 1)
                    elif kind == 1:
                        act.activation(xB[:, t, :], PS[:, 6 + n % 2, :], ACT.Copy).then_inc(S("kt_ev"), 1)
                    else:
                        act.activation(kTm[0:MLA_D, :, t * P:(t + 1) * P], src[0:MLA_D], ACT.Copy).then_inc(S("kt_ev"), 1)

            def attention(L):
                n, u0 = len(UN[L]), U0[L]
                act.wait_ge(S("lam_in"), L + 1)
                act.activation(sc[:, 0:2], sc[:, 0:2], ACT.Exp).then_inc(S("lam_exp"), 1)

                def q_evac(j):
                    act.wait_ge(S("qT_ps"), j + 1)
                    r = MLA_D if jobs[j][1] == "mla" else P
                    act.activation(qT[0:r, j % 2], PS[0:r, 7, 0:P], ACT.Copy).then_inc(S("qT_ev"), 1)

                for i in range(n + 1):
                    if i < n:
                        u = u0 + i
                        t = ALLU[u][2]
                        if i == 0:
                            q_evac(JOB[u])
                        if i + 1 < n and JOB[u + 1] != JOB[u]:
                            q_evac(JOB[u + 1])
                        act.wait_ge(S("nm_done"), u + 1)
                        if u >= 2:
                            act.wait_ge(S("t_ps"), u - 1)
                            if u >= 4:
                                act.wait_ge(S("o_ev"), u - 3)
                        w = N if t >= CT else CTX
                        act.activation(Pb[:, u % 2, 0:w], PS[:, 2 * (u % 2):2 * (u % 2) + 2, :].rearrange("p b n -> p (b n)")[:, 0:w],
                                       ACT.Exp, bias=att[:, 4 + u % 4:5 + u % 4],
                                       accum_out=att[:, 8 + u % 4:9 + u % 4]).then_inc(S("exp_done"), 1)
                    if i >= 1:
                        u = u0 + i - 1
                        t = ALLU[u][2]
                        act.wait_ge(S("t_ps"), u + 1)
                        if u >= 2:
                            act.wait_ge(S("o_ps"), u - 1)
                        w = 512 if t >= CT else CTX
                        act.activation(PTb[:, u % 2, 0:w], PS[:, 4, 0:w], ACT.Copy).then_inc(S("pt_ev_a"), 1)

            def scan(L):
                act.wait_ge(S("sp_in"), L + 1)
                act.activation(ssd[:, 8 * 48:9 * 48], ssd[:, 8 * 48:9 * 48], ACT.Exp).then_inc(S("sp_u"), 1)
                act.wait_ge(S("sp_w"), L + 1)
                act.activation(ssd[:, 48:96], ssd[:, 9 * 48:10 * 48], ACT.Ln)
                act.activation(sc[:, 8:16], row("ssd_a_log"), ACT.Exp).then_inc(S("sp_ln"), 1)
                act.wait_ge(S("cum_in"), L + 1)
                act.activation(ssd[:, 5 * 48:6 * 48], ssd[:, 2 * 48:3 * 48], ACT.Exp)
                act.activation(ssd[:, 4 * 48:5 * 48], ssd[:, 4 * 48:5 * 48], ACT.Exp)
                act.activation(ssd[:, 6 * 48:7 * 48], ssd[:, 3 * 48:4 * 48], ACT.Exp).then_inc(S("cum_exp"), 1)
                for w in range(2 * NT * L, 2 * NT * (L + 1)):
                    if SU[w][2] in out_tiles(L):
                        act.wait_ge(S("front_done"), YU[w] + 1)
                        act.activation(Mall(w), Mall(w), ACT.Exp).then_inc(S("seg_exp"), 1)
                act.activation(p[:, :, Z0:Z0 + GW], p[:, :, Z0:Z0 + GW], ACT.Silu).then_inc(S("z_silu"), 1)
                act.wait_ge(S("fin_in"), L + 1)
                act.activation(ar(scr, 2 * NT * GW).rearrange("p (t d) -> p t d", t=NT), ot[:, :, 512:1024], ACT.Square
                               ).then_inc(S("fin_sq"), 1)
                act.wait_ge(S("var_f"), L + 1)
                act.activation(ss[:, 0:30], ss[:, 0:30], ACT.Sqrt).then_inc(S("sqrt_f"), 1)

            def out_proj(L):
                for i, t in enumerate(out_tiles(L)):
                    act.wait_ge(S("oT_ps"), OT0[L] + i + 1)
                    act.activation(oT[:, 0:4, t * P:(t + 1) * P], PS[:, 2 * (i % 2), :].rearrange("p (c n) -> p c n", c=4),
                                   ACT.Copy).then_inc(S("oT_a"), 1)

            def rows_and_route(L):
                def f_evac():
                    for i, t in enumerate(out_tiles(L)):
                        act.wait_ge(S("ftok_ps"), OT0[L] + i + 1)
                        if cnt2(L, i):
                            act.wait_ge(S(f"f_out{i % 2}"), 16 * cnt2(L, i))
                        act.activation(ftok[:, i % 2, 0:512], PS[:, 2 * (i % 2), :], ACT.Copy).then_inc(S("ftok_a"), 1)
                f_evac()
                act.wait_ge(S("rt_g"), L + 1)
                act.activation(r_(120, 24), r_(120, 24), ACT.Exp).then_inc(S("rt_ge"), 1)
                act.wait_ge(S("rt_m"), L + 1)
                act.activation(r6(4), r6(4), ACT.Exp).then_inc(S("rt_me"), 1)

            def experts(L):
                n0 = NB0[L]
                fl = L == 0

                def x_evac(i, par):
                    b = 2 * i + par
                    act.wait_ge(S("xt_ps"), n0 + b + 1)
                    act.activation(xT(par)[:, 0:512], PS[:, 0, :], ACT.Copy).then_inc(S("xT_a"), 1)

                def gate(i, par):
                    b = 2 * i + par
                    act.wait_ge(S("gu_ps"), n0 + b + 1)
                    act.activation(hid(par), PS[:, 2, :], ACT.Silu).then_inc(S("silu_done"), 1)

                def y_store(i, par, first=False):
                    b = 2 * i + par
                    act.wait_ge(S("dn_ps"), n0 + b + 1)
                    if not first:
                        act.wait_ge(S(f"y_out{par}"), 16 * (n0 // 2) + 16 * i)
                    act.activation(ysb(par)[:, 0:512], PS[:, 5, :], ACT.Copy).then_inc(S("y_a"), 1)
                    act.wait_ge(S("y_a"), n0 + b + 1)
                    act.wait_ge(S("y_d"), n0 + b + 1)
                    act.dma_start(dram["y_rows"].rearrange("(b p) n -> b p n", p=P)[bass.ds(b, 1)].rearrange("b p n -> p (b n)"),
                                  ysb(par)).then_inc(S(f"y_out{par}"), 16)

                half_n = NB[L] // 2
                x_evac(0, 0)
                gate(0, 0)
                x_evac(0, 1)
                y_store(0, 0, fl)
                gate(0, 1)
                x_evac(1, 0)
                y_store(0, 1, fl)
                with act.Fori(1, half_n - 1) as i:
                    gate(i, 0)
                    x_evac(i, 1)
                    y_store(i, 0)
                    gate(i, 1)
                    x_evac(i + 1, 0)
                    y_store(i, 1)
                gate(half_n - 1, 0)
                x_evac(half_n - 1, 1)
                y_store(half_n - 1, 0)
                gate(half_n - 1, 1)
                y_store(half_n - 1, 1)

            for L in range(LAYERS):
                norm(L, 0)
                in_proj(L)
                stats(L)
                mla_prep(L)
                attention(L)
                scan(L)
                out_proj(L)
                norm(L, 1)
                rows_and_route(L)
                experts(L)
            for i, t in enumerate(out_tiles(1)):
                act.wait_ge(S("res_ps"), i + 1)
                if i >= 2:
                    act.wait_ge(S(f"res_out{i % 2}"), 16 * (i // 2))
                act.activation(restok[:, i % 2, 0:512], PS[:, 2 * (i % 2), :], ACT.Copy).then_inc(S("res_a"), 1)

        @block.vector
        def _(dve):
            link = Chain(dve, S("dve_chain"))
            dve.wait_ge(S("consts_in"), 16)
            link(dve.tensor_copy(tokid[:, :], K[:, C_TOK:C_TOK + NT]))
            mul = ALU.mult
            for t in range(NT):
                dve.wait_ge(S("x_ps"), t + 1)
                dve.tensor_copy(hT[:, 4:8, t * P:(t + 1) * P],
                                PS[:, 2 * (t % 2) + 1, :].rearrange("p (c n) -> p c n", c=4)).then_inc(S("x_ev_d"), 1)
            dve.wait_ge(S("bmod_in"), 16)
            for i in range(len(mod_jobs)):
                dve.wait_ge(S("wmod_used"), i + 1)
                mr = modrow[0:2, i * 512:(i + 1) * 512]
                dve.tensor_tensor(mr, PS[0:2, 4 + i % 2, :], mr, ALU.add).then_inc(S("mod_ev"), 1)
            dve.wait_ge(S("modT_ps"), 1)
            link(dve.tensor_copy(modcol[:, :], PS[:, 6, 0:LAYERS * 96]))
            dve.wait_ge(S("cols_in"), 16 * LAYERS * (3 + XM))
            for l2 in range(LAYERS):
                for w in range(2):
                    g = gcol3[:, l2, w, :]
                    last = dve.scalar_tensor_tensor(out=acol4[:, l2, w], in0=mod4[:, l2, 24 * w + 8:24 * w + 16, :], scalar=1.0,
                                                    in1=bc(g, (1, DC), (0, 2)), op0=ALU.add, op1=mul)
            last.then_inc(S("acol_ready"), 1)

            def norm(L, w):
                lo = 0 if w == 0 else tok_lo(L)
                base = (2 * L + w) * DC
                dve.wait_ge(S("sq_used"), base + DC)
                for bk, (a, b) in enumerate(segs(lo)):
                    last = dve.tensor_scalar(rs[:, a:b], PS[:, bk, 0:b - a], 1.0 / D, EPS, mul, ALU.add)
                last.then_inc(S("var_done"), 1)
                if w == 0:
                    dve.memset(raw[:, :, 0:2], 0.0)
                    dve.memset(raw[:, :, 2 + CTX:6 + CTX], 0.0)
                    dve.memset(raw[:, :, RAWW - 2:RAWW], 0.0).then_inc(S("pads_ready"), 1)
                dve.wait_ge(S("sqrt_done"), 2 * L + w + 1)
                link(dve.reciprocal(rs[:, lo:N], rs[:, lo:N]))
                for c in range(DC):
                    dve.tensor_tensor(aT[:, c, lo:N], hT[:, c, lo:N], rs[:, lo:N], mul).then_inc(S("nrm_x"), 1)

            def conv(L):
                for m in range(XM):
                    dve.wait_ge(S("raw_ready"), XM * L + m + 1)
                    o = xbcT[:, m, :]
                    link(dve.tensor_scalar(o, raw[:, m % 2, 0:XW], cw[:, L, m, 0:1], cw[:, L, m, 5:6], mul, ALU.add))
                    for j in range(1, CONV):
                        ins = dve.scalar_tensor_tensor(out=o, in0=raw[:, m % 2, j:j + XW], scalar=cw[:, L, m, j:j + 1],
                                                       in1=o, op0=mul, op1=ALU.add)
                        if j < CONV - 1:
                            link(ins)
                    ins.then_inc(S("conv_done"), 1)

            ss3 = ss[:, :].rearrange("p (t h) -> p t h", t=NT)
            ss23 = ss2[:, :].rearrange("p (t h) -> p t h", t=NT)

            def heads(v, h):
                return v.rearrange("p t (h d) -> p t h d", h=h)

            def over(a3, d):
                return bc(a3, list(a3.ap[1]), list(a3.ap[2]), (0, d))

            def gain(name, t, h):
                g = row(name)
                return bc(g, (0, t), (0, h), (1, ROW_AT[name][1]))

            def rotate(v, tmp, nh):
                x1, x2 = v[:, :, :, 0:16], v[:, :, :, 16:32]
                cosb = bc(K[:, C_COS:C_COS + 1], (16, 4), (0, nh), (1, 16))
                sinb = bc(K[:, C_SIN:C_SIN + 1], (16, 4), (0, nh), (1, 16))
                n = 4 * nh * 16
                tm = [ar(tmp + q * n, n).rearrange("p (t h d) -> p t h d", t=4, h=nh) for q in range(4)]
                dve.tensor_tensor(tm[0], x1, cosb, mul)
                dve.tensor_tensor(tm[1], x2, sinb, mul)
                dve.tensor_tensor(tm[2], x1, sinb, mul)
                link(dve.tensor_tensor(tm[3], x2, cosb, mul))
                dve.tensor_tensor(x1, tm[0], tm[1], ALU.subtract)
                return dve.tensor_tensor(x2, tm[2], tm[3], ALU.add)

            def stats(L):
                dve.wait_ge(S("sq_stats"), 3 * L + 1)
                m2 = ar(scr, NT * 384).rearrange("p (t d) -> p t d", t=NT)
                dve.tensor_reduce(ss3[:, :, 24], m2[:, :, 0:256], AX.X, ALU.add)
                dve.tensor_reduce(ss3[:, :, 25], m2[:, :, 256:384], AX.X, ALU.add)
                dve.wait_ge(S("sq_stats"), 3 * L + 2)
                dve.tensor_reduce(ss3[:, :, 0:8], ar(A_B, NT * 512).rearrange("p (t h d) -> p t h d", t=NT, h=8), AX.X, ALU.add)
                dve.wait_ge(S("sq_stats"), 3 * L + 3)
                link(dve.tensor_reduce(ss3[:, :, 8:24], ar(A_B + NT * 512, NT * 512).rearrange("p (t h d) -> p t h d", t=NT, h=16),
                                       AX.X, ALU.add))
                for a, b, d in ((0, 8, HD), (8, 24, DQK), (24, 25, 256), (25, 26, 128)):
                    last = dve.tensor_scalar(ss3[:, :, a:b], ss3[:, :, a:b], 1.0 / d, EPS, mul, ALU.add)
                last.then_inc(S("var_s"), 1)
                dve.wait_ge(S("sqrt_s"), L + 1)
                link(dve.reciprocal(ss[:, :], ss[:, :]))
                dve.tensor_scalar(ss3[:, :, 0:4], ss3[:, :, 0:4], HD ** -0.5, None, mul)
                dve.tensor_scalar(ss3[:, :, 8:16], ss3[:, :, 8:16], DQK ** -0.5, None, mul).then_inc(S("rstd_done"), 1)
                cq, ckv = p[:, :, MLA0:MLA0 + 256], p[:, :, MLA0 + 256:MLA0 + 384]
                dve.wait_ge(S("rows_in"), 16 * len(ROWS) * (L + 1))
                dve.tensor_tensor(cq, cq, bc(ss3[:, :, 24], (26, NT), (0, 256)), mul)
                link(dve.tensor_tensor(ckv, ckv, bc(ss3[:, :, 25], (26, NT), (0, 128)), mul))
                dve.tensor_tensor(cq, cq, bc(row("mla_g_qa"), (0, NT), (1, 256)), mul)
                dve.tensor_tensor(ckv, ckv, bc(row("mla_g_kva"), (0, NT), (1, 128)), mul).then_inc(S("stats_done"), 1)
                dve.wait_ge(S("rstd_done"), L + 1)
                v = heads(p[:, :, DIF0:DIF0 + 512], 16)
                link(dve.tensor_tensor(v, v, over(ss3[:, :, 8:24], DQK), mul))
                dve.tensor_tensor(v[:, :, 0:8], v[:, :, 0:8], gain("diff_g_q", NT, 8), mul)
                link(dve.tensor_tensor(v[:, :, 8:16], v[:, :, 8:16], gain("diff_g_k", NT, 8), mul))
                rotate(v[:, CT:], scr, 16).then_inc(S("dif_norm"), 1)

            def mla_prep(L):
                for t in range(NT):
                    dve.wait_ge(S("mla_ps"), NT * L + t + 1)
                    kv = PS[:, 4 + t % 2, :].rearrange("p (h d) -> p h d", h=HEADS)
                    mk = ot[:, t, 640:1024].rearrange("p (h d) -> p h d", h=HEADS)
                    dve.tensor_copy(mk[:, :, 0:HD], kv[:, :, 0:HD])
                    dve.tensor_copy(p[:, t, MLA0:MLA0 + 256].rearrange("p (h d) -> p h d", h=HEADS), kv[:, :, HD:2 * HD])
                    dve.tensor_copy(mk[:, :, HD:MLA_D], bc(p[:, t, MLA0 + 384:MLA0 + 385], (0, HEADS), (1, 32))
                                    ).then_inc(S("mkv_ev"), 1)
                dve.wait_ge(S("sq_m"), L + 1)
                link(dve.tensor_reduce(ss23, ar(scr, NT * 768).rearrange("p (t h d) -> p t h d", t=NT, h=8), AX.X, ALU.add))
                dve.tensor_scalar(ss2[:, :], ss2[:, :], 1.0 / MLA_D, EPS, mul, ALU.add).then_inc(S("var_m"), 1)
                dve.wait_ge(S("sqrt_m"), L + 1)
                link(dve.reciprocal(ss2[:, :], ss2[:, :]))
                link(dve.tensor_scalar(ss23[:, :, 0:4], ss23[:, :, 0:4], MLA_D ** -0.5, None, mul))
                v = heads(ot[:, :, 256:1024], 8)
                link(dve.tensor_tensor(v, v, over(ss23, MLA_D), mul))
                dve.tensor_tensor(v[:, :, 0:4], v[:, :, 0:4], gain("mla_g_q", NT, 4), mul)
                link(dve.tensor_tensor(v[:, :, 4:8], v[:, :, 4:8], gain("mla_g_k", NT, 4), mul))
                rotate(v[:, CT:, :, HD:MLA_D], scr, 8).then_inc(S("m_norm"), 1)

            def attention(L):
                n, u0 = len(UN[L]), U0[L]
                lv = row("diff_lambda")
                lt = ssd[:, 0:64].rearrange("p (a d) -> p a d", a=2)
                link(dve.tensor_tensor(lt, bc(lv, (64, 2), (1, 32)), bc(row("diff_lambda", 32, 96), (64, 2), (1, 32)), mul))
                dve.tensor_reduce(sc[:, 0:2], lt, AX.X, ALU.add).then_inc(S("lam_in"), 1)
                dve.wait_ge(S("lam_exp"), L + 1)
                link(dve.tensor_tensor(sc[:, 2:3], sc[:, 1:2], sc[:, 0:1], ALU.subtract))
                link(dve.tensor_scalar(sc[:, 3:4], sc[:, 2:3], -LAM_INIT[L], None, ALU.add))

                for i in range(n + 2):
                    if i < n:
                        u = u0 + i
                        w = N if ALLU[u][2] >= CT else CTX
                        dve.wait_ge(S("s_ps"), u + 1)
                        link(dve.tensor_reduce(att[:, u % 4:u % 4 + 1],
                                               PS[:, 2 * (u % 2):2 * (u % 2) + 2, :].rearrange("p b n -> p (b n)")[:, 0:w],
                                               AX.X, ALU.max))
                        dve.tensor_scalar(att[:, 4 + u % 4:5 + u % 4], att[:, u % 4:u % 4 + 1], -1.0, None, mul
                                          ).then_inc(S("nm_done"), 1)
                    if 1 <= i <= n:
                        u = u0 + i - 1
                        if ALLU[u][2] >= CT:
                            dve.wait_ge(S("t_ps"), u + 1)
                            if u >= 2:
                                dve.wait_ge(S("o_ps"), u - 1)
                            dve.tensor_copy(PTb[:, u % 2, 512:N], PS[:, 5, 0:N - 512]).then_inc(S("pt_ev_d"), 1)
                    if i >= 2:
                        u = u0 + i - 2
                        g, h, t = ALLU[u]
                        dve.wait_ge(S("o_ps"), u + 1)
                        link(dve.reciprocal(att[:, 12:13], att[:, 8 + u % 4:9 + u % 4]))
                        o = PS[:, 6, 0:HD]
                        c0 = {"mla": HD * h, "na": 256 + HD * h, "dif": 512 + HD * (h // 2)}[g]
                        dst = ot[:, t, c0:c0 + HD]
                        if g == "dif" and h % 2:
                            link(dve.tensor_tensor(att[:, 13:14], att[:, 12:13], sc[:, 3:4], mul))
                            dve.scalar_tensor_tensor(out=dst, in0=o, scalar=att[:, 13:14], in1=dst, op0=mul, op1=ALU.add
                                                     ).then_inc(S("o_ev"), 1)
                        else:
                            dve.tensor_scalar(dst, o, att[:, 12:13], None, mul).then_inc(S("o_ev"), 1)
                        dve.wait_ge(S("o_ev"), u + 1)

            def scan(L):
                la, dt, cum, tot, toend, ecum, etot, x_, u_, w_ = [ssd[:, k * 48:(k + 1) * 48] for k in range(10)]
                la3, dt3, cum3, tot3, toend3, ecum3, etot3 = [sv(k) for k in range(7)]
                ul = out_tiles(L)
                link(dve.tensor_tensor(sv(7), p[:, :, PDT:PDT + 8], bc(row("ssd_dt_bias"), (0, NT), (1, 8)), ALU.add))
                link(dve.tensor_scalar(u_, x_, -1.0, None, mul))
                dve.tensor_tensor(u_, u_, x_, ALU.min).then_inc(S("sp_in"), 1)
                dve.wait_ge(S("sp_u"), L + 1)
                dve.tensor_scalar(w_, u_, 1.0, None, ALU.add).then_inc(S("sp_w"), 1)
                dve.wait_ge(S("sp_ln"), L + 1)
                link(dve.tensor_scalar(cum, w_, -1.0, 1e-7, ALU.add, ALU.max))
                link(dve.reciprocal(cum, cum))
                link(dve.tensor_tensor(cum, cum, u_, mul))
                link(dve.tensor_tensor(dt, dt, cum, mul))
                link(dve.tensor_scalar(w_, w_, 1.0, None, ALU.is_equal))
                link(dve.tensor_tensor(w_, w_, u_, mul))
                link(dve.tensor_tensor(dt, dt, w_, ALU.max))
                link(dve.tensor_scalar(x_, x_, 0.0, None, ALU.max))
                link(dve.tensor_tensor(dt, dt, x_, ALU.add))
                link(dve.tensor_tensor(la3, dt3, bc(sc[:, 8:16], (0, NT), (1, 8)), mul))
                dve.tensor_scalar(la, la, -1.0, None, mul).then_inc(S("la_done"), 1)
                for dd in range(2):
                    last = dve.memset(state(dd), 0.0)
                link(last)
                dve.wait_ge(S("cum_ps"), L + 1)
                pc = PS[:, 0, 0:96]
                for dd in range(2):
                    dve.tensor_copy(cum3[:, :, 4 * dd:4 * dd + 4], pc[:, 24 * dd:24 * dd + 24].rearrange("p (t h) -> p t h", t=NT))
                link(dve.tensor_copy(tot, pc[:, 48:96]))
                dve.tensor_tensor(toend, tot, cum, ALU.subtract).then_inc(S("cum_in"), 1)
                dve.wait_ge(S("cum_exp"), L + 1)
                dve.tensor_copy(w_, cum).then_inc(S("cum_done"), 1)
                dve.wait_ge(S("cum_done"), L + 1)

                def hp(v2):
                    return v2.rearrange("p (h d) -> p h d", h=HEADS)

                def front(w):
                    _, dd, t = SU[w]
                    if t in ul:
                        dve.wait_ge(S("rg_ps"), YU[w] + 1)
                        yp = YU[w] % 2
                        tri = triU if dd == 0 else triL
                        if YU[w] >= 2:
                            dve.wait_ge(S("y_ps"), YU[w] - 1)
                        dve.tensor_tensor(GMb(w).rearrange("p (g n) -> p g n", g=2), PS[:, 2 + yp, 0:256].rearrange("p (g n) -> p g n", g=2),
                                          bc(tri, (0, 2), (1, P)), mul)
                        for h in range(HEADS):
                            last = dve.tensor_scalar(Mb(w, h), PS[:, yp, h * P:(h + 1) * P],
                                                     cum3[:, t, 4 * dd + h:4 * dd + h + 1], 0.0, ALU.subtract, ALU.min)
                        last.then_inc(S("front_done"), 1)
                    if w >= 2:
                        dve.wait_ge(S("st_ps"), w - 1)
                    link(dve.tensor_tensor(hp(xdt(w)), hp(xB[:, t, 0:256]), bc(dt3[:, t, 4 * dd:4 * dd + 4], (1, 4), (0, HD)), mul))
                    dve.tensor_tensor(hp(xdte(w)), hp(xdt(w)), bc(toend3[:, t, 4 * dd:4 * dd + 4], (1, 4), (0, HD)), mul
                                      ).then_inc(S("xdt_done"), 1)
                    if t in ul:
                        dve.wait_ge(S("seg_exp"), YU[w] + 1)
                        dve.wait_ge(S("xdt_done"), w + 1)
                        m4 = Mall(w).rearrange("p (g h n) -> p g h n", g=2, h=2)
                        dve.tensor_tensor(m4, m4, bc(GMb(w), (P, 2), (0, 2), (1, P)), mul).then_inc(S("m_done"), 1)

                def back(w):
                    _, dd, t = SU[w]
                    if t in ul:
                        dve.wait_ge(S("y_ps"), YU[w] + 1)
                        yp = YU[w] % 2
                        link(dve.tensor_tensor(hp(ytmp), hp(PS[:, 4 + yp, 256:512]), bc(ecum3[:, t, 4 * dd:4 * dd + 4], (1, 4), (0, HD)), mul))
                        acc = ot[:, t, 768:1024]
                        if (L, 1 - dd, t) in SU[2 * NT * L:w]:
                            link(dve.tensor_tensor(acc, acc, ytmp, ALU.add))
                            dve.tensor_tensor(acc, PS[:, 4 + yp, 0:256], acc, ALU.add).then_inc(S("y_done"), 1)
                        else:
                            dve.tensor_tensor(acc, PS[:, 4 + yp, 0:256], ytmp, ALU.add).then_inc(S("y_done"), 1)
                        dve.wait_ge(S("y_done"), YU[w] + 1)
                    dve.wait_ge(S("st_ps"), w + 1)
                    link(dve.tensor_tensor(hp(state(dd)), hp(state(dd)), bc(etot3[:, t, 4 * dd:4 * dd + 4], (1, 4), (0, HD)), mul))
                    dve.tensor_tensor(state(dd), PS[:, 6 + w % 2, 0:256], state(dd), ALU.add).then_inc(S("state_done"), 1)
                    dve.wait_ge(S("state_done"), w + 1)

                w0 = 2 * NT * L
                for i in range(2 * NT + 1):
                    if i < 2 * NT:
                        front(w0 + i)
                    if i:
                        back(w0 + i - 1)
                t0 = ul[0]
                nt = NT - t0
                y = ot[:, t0:, 768:1024]
                link(dve.tensor_tensor(sc[:, 16:20], row("ssd_d", 0, 4), row("ssd_d", 4, 4), ALU.add))
                xs = xB[:, t0:, 0:256]
                tmp = ar(scr, nt * 256)
                link(dve.tensor_tensor(tmp.rearrange("p (t h d) -> p t h d", t=nt, h=4), heads(xs, 4),
                                       bc(sc[:, 16:20], (0, nt), (1, 4), (0, HD)), mul))
                tmp3 = tmp.rearrange("p (t d) -> p t d", t=nt)
                link(dve.tensor_tensor(y, y, tmp3, ALU.add))
                dve.wait_ge(S("z_silu"), L + 1)
                if t0:
                    dve.memset(ot[:, 0:t0, 512:1024], 0.0)
                dve.tensor_tensor(y, y, p[:, t0:, Z0:Z0 + GW], mul).then_inc(S("fin_in"), 1)
                dve.wait_ge(S("fin_sq"), L + 1)
                sq = ar(scr, 2 * NT * GW).rearrange("p (t d) -> p t d", t=NT)
                f3 = ss[:, 0:30].rearrange("p (t h) -> p t h", t=NT)
                dve.tensor_reduce(f3[:, :, 0:4], heads(sq[:, :, 0:256], 4), AX.X, ALU.add)
                link(dve.tensor_reduce(f3[:, :, 4], sq[:, :, 256:512], AX.X, ALU.add))
                dve.tensor_scalar(f3[:, :, 0:4], f3[:, :, 0:4], 1.0 / HD, EPS, mul, ALU.add)
                dve.tensor_scalar(f3[:, :, 4:5], f3[:, :, 4:5], 1.0 / GW, EPS, mul, ALU.add).then_inc(S("var_f"), 1)
                dve.wait_ge(S("sqrt_f"), L + 1)
                link(dve.reciprocal(ss[:, 0:30], ss[:, 0:30]))
                link(dve.tensor_scalar(f3[:, :, 0:4], f3[:, :, 0:4], 1.0 - LAM_INIT[L], None, mul))
                vd = heads(ot[:, :, 512:768], 4)
                dve.tensor_tensor(vd, vd, over(f3[:, :, 0:4], HD), mul)
                link(dve.tensor_tensor(ot[:, :, 768:1024], ot[:, :, 768:1024], bc(f3[:, :, 4], (5, NT), (0, 256)), mul))
                dve.tensor_tensor(vd, vd, gain("diff_g_sub", NT, 4), mul)
                dve.tensor_tensor(ot[:, :, 768:1024], ot[:, :, 768:1024], bc(row("ssd_g_norm"), (0, NT), (1, 256)), mul
                                  ).then_inc(S("mix_done"), 1)

            def out_proj(L):
                for i, t in enumerate(out_tiles(L)):
                    dve.wait_ge(S("oT_ps"), OT0[L] + i + 1)
                    dve.tensor_copy(oT[:, 4:8, t * P:(t + 1) * P],
                                    PS[:, 2 * (i % 2) + 1, :].rearrange("p (c n) -> p c n", c=4)).then_inc(S("oT_d"), 1)
                for m in range(DC):
                    dve.wait_ge(S("op_ps"), DC * L + m + 1)
                    parts = []
                    for bk, (a, b) in enumerate(segs(tok_lo(L))):
                        parts += [(bk, a, max(a, a2), min(b, b2), s) for s, a2, b2 in streams(tok_lo(L), N) if max(a, a2) < min(b, b2)]
                    for q, (bk, a, c0, c1, s) in enumerate(parts):
                        last = dve.scalar_tensor_tensor(out=hT[:, m, c0:c1], in0=PS[:, 4 + 2 * (m % 2) + bk, c0 - a:c1 - a],
                                                        scalar=mod4[:, L, 16 + m, s:s + 1], in1=hT[:, m, c0:c1], op0=mul, op1=ALU.add)
                    last.then_inc(S("op_ev"), 1)
                dve.wait_ge(S("op_ev"), DC * (L + 1))
                dve.memset(sc[:, 20:21], 0.0).then_inc(S("h_mid"), 1)

            def route(L):
                tl = out_tiles(L)
                t0, T = tl[0], len(tl)
                for i, t in enumerate(tl):
                    dve.wait_ge(S("ftok_ps"), OT0[L] + i + 1)
                    if cnt2(L, i):
                        dve.wait_ge(S(f"f_out{i % 2}"), 16 * cnt2(L, i))
                    dve.tensor_copy(ftok[:, i % 2, 512:], PS[:, 2 * (i % 2) + 1, :]).then_inc(S("ftok_d"), 1)
                dve.wait_ge(S("lg_ps"), L + 1)
                lg = r_lg[:, t0:]
                link(dve.tensor_tensor(lg, PS[:, 4, t0 * 20:NT * 20].rearrange("p (t n) -> p t n", t=T),
                                       bc(row("moe_b_group"), (0, T), (1, 20)), ALU.add))
                g4 = lg[:, :, 0:4]

                def v24(off):
                    return r_(off, 24).rearrange("p (t g) -> p t g", t=NT)[:, t0:]

                def v96(off):
                    return r_(off, 96).rearrange("p (t e) -> p t e", t=NT)[:, t0:]

                def s6(k):
                    return r6(k)[:, t0:]

                def first_max(v, w, mx, tmp, oh):
                    link(dve.tensor_reduce(mx, v, AX.X, ALU.max))
                    link(dve.tensor_tensor(tmp, v, bc(mx, (1, T), (0, w)), ALU.is_equal))
                    link(dve.tensor_tensor(tmp, tmp, bc(K[:, C_DEC:C_DEC + 1], (0, T), (1, w)), mul))
                    link(dve.tensor_reduce(s6(9), tmp, AX.X, ALU.max))
                    link(dve.tensor_tensor(oh, tmp, bc(s6(9), (1, T), (0, w)), ALU.is_equal))

                ohg = v24(144)
                first_max(g4, 4, s6(0), v24(120), ohg)
                if t0:
                    link(dve.memset(r_(120, 24), 0.0))
                    link(dve.memset(r6(4), 0.0))
                dve.tensor_tensor(v24(120), g4, bc(s6(0), (1, T), (0, 4)), ALU.subtract).then_inc(S("rt_g"), 1)
                dve.wait_ge(S("rt_ge"), L + 1)
                link(dve.tensor_reduce(s6(1), v24(120), AX.X, ALU.add))
                link(dve.reciprocal(s6(1), s6(1)))
                em = v96(228)
                em4 = em.rearrange("p t (g e) -> p t g e", g=GROUPS)
                ohg4 = bc(ohg, (4, T), (1, 4), (0, EPG))
                link(dve.tensor_tensor(em4, lg[:, :, 4:20].rearrange("p t (g e) -> p t g e", g=GROUPS), ohg4, mul))
                link(dve.tensor_scalar(v24(120), ohg, -1.0, BIG, ALU.add, mul))
                link(dve.tensor_tensor(em4, em4, bc(v24(120), (4, T), (1, 4), (0, EPG)), ALU.add))
                first_max(em, EXP, s6(2), v96(324), r_oh[0][:, t0:])
                link(dve.scalar_tensor_tensor(out=em, in0=r_oh[0][:, t0:], scalar=-3 * BIG, in1=em, op0=mul, op1=ALU.add))
                first_max(em, EXP, s6(3), v96(324), r_oh[1][:, t0:])
                dve.tensor_tensor(r_sel[:, t0:], r_oh[0][:, t0:], r_oh[1][:, t0:], ALU.add).then_inc(S("sel_done"), 1)
                dve.tensor_tensor(s6(4), s6(3), s6(2), ALU.subtract).then_inc(S("rt_m"), 1)
                dve.wait_ge(S("rt_me"), L + 1)
                link(dve.tensor_scalar(s6(5), s6(4), 1.0, None, ALU.add))
                link(dve.reciprocal(s6(5), s6(5)))
                link(dve.tensor_tensor(wtok[:, t0:NT], s6(5), s6(1), mul))
                link(dve.tensor_tensor(wtok[:, NT + t0:2 * NT], wtok[:, t0:NT], s6(4), mul))
                dve.wait_ge(S("rank_ps"), L + 1)
                dm = v96(708)
                dve.tensor_copy(dm, PS[:, 5, t0 * EXP:NT * EXP].rearrange("p (t e) -> p t e", t=T))
                cnt, blocks, pex = r_(804, EXP), r_(820, EXP), r_(836, EXP)
                link(dve.tensor_copy(cnt, PS[:, 5, NT * EXP:(NT + 1) * EXP]))
                c6 = r_(852, EXP * NT).rearrange("p (e j) -> p e j", e=EXP)
                link(dve.tensor_tensor(c6, bc(cnt, (1, EXP), (0, NT)), bc(K[:, C_THR:C_THR + 1], (0, EXP), (1, NT)), ALU.is_gt))
                link(dve.tensor_reduce(blocks, c6, AX.X, ALU.add))
                t16 = r_(852, EXP * EXP).rearrange("p (e j) -> p e j", e=EXP)
                link(dve.tensor_tensor(t16, K[:, C_TRI:C_TRI + EXP * EXP].rearrange("p (e j) -> p e j", e=EXP),
                                       bc(blocks, (0, EXP), (1, EXP)), mul))
                link(dve.tensor_reduce(pex, t16, AX.X, ALU.add))
                link(dve.tensor_tensor(cnt, pex, blocks, ALU.add))
                cb = r_(1108, NBMAX * EXP).rearrange("p (b e) -> p b e", b=NBMAX)
                link(dve.tensor_tensor(cb, bc(K[:, C_BLK:C_BLK + 1], (1, NBMAX), (0, EXP)), bc(cnt, (0, NBMAX), (1, EXP)), ALU.is_ge))
                link(dve.tensor_reduce(r_(852, NBMAX), cb, AX.X, ALU.add))
                dve.tensor_scalar(blk_e[:, :], r_(852, NBMAX), float(EXP - 1), None, ALU.min).then_inc(S("blk_ready"), 1)
                dve.wait_ge(S("blk_ready"), L + 1)
                link(dve.tensor_scalar(pex, pex, float(P), None, mul))
                link(dve.tensor_tensor(dm, dm, bc(pex, (0, T), (1, EXP)), ALU.add))
                for k in range(TOPK):
                    link(dve.tensor_tensor(v96(324), r_oh[k][:, t0:], dm, mul))
                    link(dve.tensor_reduce(s6(6 + k), v96(324), AX.X, ALU.add))
                    last = dve.tensor_copy(dest[:, k * NT + t0:(k + 1) * NT], s6(6 + k))
                last.then_inc(S("dest_ready"), 1)

            def experts(L):
                n0 = NB0[L]
                fl = L == 0

                def x_evac(i, par):
                    b = 2 * i + par
                    dve.wait_ge(S("xt_ps"), n0 + b + 1)
                    dve.tensor_copy(xT(par)[:, 512:], PS[:, 1, :]).then_inc(S("xT_d"), 1)

                def up(i, par):
                    b = 2 * i + par
                    dve.wait_ge(S("silu_done"), n0 + b + 1)
                    dve.tensor_tensor(hid(par), PS[:, 3, :], hid(par), mul).then_inc(S("h_done"), 1)

                def h_and_y(i, par, first=False):
                    b = 2 * i + par
                    dve.wait_ge(S("ht_ps"), n0 + b + 1)
                    dve.tensor_copy(hidT(par), PS[:, 4, :]).then_inc(S("hT_ev"), 1)
                    dve.wait_ge(S("dn_ps"), n0 + b + 1)
                    if not first:
                        dve.wait_ge(S(f"y_out{par}"), 16 * (n0 // 2) + 16 * i)
                    dve.tensor_copy(ysb(par)[:, 512:], PS[:, 6, :]).then_inc(S("y_d"), 1)

                half_n = NB[L] // 2
                x_evac(0, 0)
                up(0, 0)
                x_evac(0, 1)
                h_and_y(0, 0, fl)
                up(0, 1)
                x_evac(1, 0)
                h_and_y(0, 1, fl)
                with dve.Fori(1, half_n - 1) as i:
                    up(i, 0)
                    x_evac(i, 1)
                    h_and_y(i, 0)
                    up(i, 1)
                    x_evac(i + 1, 0)
                    h_and_y(i, 1)
                up(half_n - 1, 0)
                x_evac(half_n - 1, 1)
                h_and_y(half_n - 1, 0)
                up(half_n - 1, 1)
                h_and_y(half_n - 1, 1)

            def combine(L):
                for i, t in enumerate(out_tiles(L)):
                    dve.wait_ge(S(f"g_in{i % 2}"), 32 * (cnt2(L, i) + 1))
                    a, b = r12(i, 0), r12(i, 1)
                    link(dve.tensor_scalar(a, a, wtok[:, t:t + 1], None, mul))
                    dve.scalar_tensor_tensor(out=a, in0=b, scalar=wtok[:, NT + t:NT + t + 1], in1=a, op0=mul, op1=ALU.add
                                             ).then_inc(S("comb"), 1)
                    dve.wait_ge(S("comb_ps"), OT0[L] + i + 1)
                    s = 1 if t < CT else 0
                    for c in range(DC):
                        v = hT[:, c, t * P:(t + 1) * P]
                        last = dve.scalar_tensor_tensor(out=v, in0=PS[:, 2 * (i % 2) + c // 4, (c % 4) * P:(c % 4 + 1) * P],
                                                        scalar=mod4[:, L, 40 + c, s:s + 1], in1=v, op0=mul, op1=ALU.add)
                    last.then_inc(S("hup"), 1)
                dve.wait_ge(S("hup"), OT0[L] + OTN[L])
                dve.memset(sc[:, 21:22], 0.0).then_inc(S("h_final"), 1)

            for L in range(LAYERS):
                norm(L, 0)
                conv(L)
                stats(L)
                mla_prep(L)
                attention(L)
                scan(L)
                out_proj(L)
                norm(L, 1)
                route(L)
                experts(L)
                combine(L)
            for i, t in enumerate(out_tiles(1)):
                dve.wait_ge(S("res_ps"), i + 1)
                if i >= 2:
                    dve.wait_ge(S(f"res_out{i % 2}"), 16 * (i // 2))
                dve.tensor_copy(restok[:, i % 2, 512:], PS[:, 2 * (i % 2) + 1, :]).then_inc(S("res_d"), 1)

        @block.gpsimd
        def _(pool):
            pool.wait_ge(S("consts_in"), 16)
            for L in range(LAYERS):
                pool.wait_ge(S("rstd_done"), L + 1)
                pool.wait_ge(S("rows_in"), 16 * len(ROWS) * (L + 1))
                ss3 = ss[:, :].rearrange("p (t h) -> p t h", t=NT)
                v = p[:, :, NA0:NA0 + 512].rearrange("p t (h d) -> p t h d", h=8)
                pool.tensor_tensor(v, v, bc(ss3[:, :, 0:8], (26, NT), (1, 8), (0, HD)), ALU.mult).then_inc(S("na_r"), 1)
                pool.wait_ge(S("na_r"), L + 1)
                for q, nm in enumerate(("na_g_q", "na_g_k")):
                    last = pool.tensor_tensor(v[:, :, 4 * q:4 * q + 4], v[:, :, 4 * q:4 * q + 4],
                                              bc(row(nm), (0, NT), (0, 4), (1, HD)), ALU.mult)
                last.then_inc(S("na_norm"), 1)
                pool.wait_ge(S("bias_in"), 16 * 2 * HEADS * (L + 1))
                bv = bias4[:, :, 1:, :]
                pool.tensor_tensor(bv, bv, bc(K[:, C_MASK:C_MASK + 1], (0, HEADS), (0, ROFF - 1), (1, GRID)), ALU.add
                                   ).then_inc(S("bias_ready"), 1)
                if L == 0:
                    pool.wait_ge(S("h_mid"), 1)
                    pool.memset(zrow, 0.0).then_inc(S("zero_row"), 1)
                pool.memset(slots[:, :], N).then_inc(S("slots_fill"), 1)
                pool.wait_ge(S("dest_ready"), L + 1)
                pool.wait_ge(S("slots_init"), 16 * (L + 1))
                for t in out_tiles(L):
                    for k in range(TOPK):
                        pool.indirect_dma_start(
                            out=dram["slot_tok"], out_offset=bass.IndirectOffsetOnAxis(ap=dest[:, k * NT + t:k * NT + t + 1], axis=0),
                            in_=tokid[:, t:t + 1], in_offset=None).then_inc(S("slot_scat"), 16)
                pool.wait_ge(S("slots_in"), 16 * (L + 1))
                for q in range(2):
                    pool.wait_ge(S(f"f_out{q}"), 16 * (NT // 2 * L + OTN[L] // 2))
                pool.wait_ge(S("zrow_out"), 16)
                n0 = NB0[L]

                def gather(i, par, first=False):
                    b = 2 * i + par
                    if not first:
                        pool.wait_ge(S("xt_ps"), n0 + b - 1)
                        pool.wait_ge(S(f"xg_in{par}"), 16 * (n0 // 2) + 16 * i)
                    pool.tensor_copy(slot1[:, par:par + 1], slots[:, bass.ds(b, 1)]).then_inc(S("slot1_done"), 1)
                    pool.wait_ge(S("slot1_done"), n0 + b + 1)
                    pool.nop(nofuse=True)
                    pool.indirect_dma_start(
                        out=xg(par), out_offset=None, in_=dram["f_rows"],
                        in_offset=bass.IndirectOffsetOnAxis(ap=slot1[:, par:par + 1], axis=0)).then_inc(S(f"xg_in{par}"), 16)

                for par in range(2):
                    gather(0, par, True)
                with pool.Fori(1, NB[L] // 2) as i:
                    for par in range(2):
                        gather(i, par)
                for q in range(2):
                    pool.wait_ge(S(f"y_out{q}"), 16 * (NB0[L] + NB[L]) // 2)
                for i, t in enumerate(out_tiles(L)):
                    if i >= 2:
                        pool.wait_ge(S("hup"), OT0[L] + i - 1)
                    for k in range(TOPK):
                        pool.indirect_dma_start(
                            out=r12(i, k), out_offset=None, in_=dram["y_rows"],
                            in_offset=bass.IndirectOffsetOnAxis(ap=dest[:, k * NT + t:k * NT + t + 1], axis=0)
                        ).then_inc(S(f"g_in{i % 2}"), 16)


_INS = ["x", "c", "ctx", "c_ctx", "w_mod", "b_mod", "g_mix", "w_in", "w_out", "na_g_q", "na_g_k",
        "mla_g_qa", "mla_w_qb", "mla_g_kva", "mla_w_kvb", "mla_g_q", "mla_g_k", "diff_g_q", "diff_g_k", "diff_lambda",
        "diff_g_sub", "ssd_conv_w", "ssd_conv_b", "ssd_dt_bias", "ssd_a_log", "ssd_d", "ssd_g_norm", "g_ffn",
        "moe_w_group", "moe_b_group", "moe_w_expert", "moe_b_expert", "moe_w_gate", "moe_w_up", "moe_w_down"]


def kernel(**inputs):
    import numpy as _np
    import concourse.bacc as _bacc
    from concourse import mybir as _mybir
    from concourse.bass_utils import run_bass_kernel_spmd as _run

    nc = _bacc.Bacc("TRN2", target_bir_lowering=False, num_devices=1)
    arrays, io = {}, {}
    rel = _np.ascontiguousarray(inputs["na_rel_bias"]).reshape(LAYERS, -1)
    data = {k: _np.ascontiguousarray(inputs[k]) for k in _INS}
    data["rel_pad"] = _np.pad(rel, ((0, 0), (REL_PAD, REL_PAD)))
    data["consts"] = constants()
    for name, a in data.items():
        arrays[f"in_{name}"] = a
        io[name] = nc.dram_tensor(f"in_{name}", a.shape, _mybir.dt.from_np(a.dtype), kind="ExternalInput").ap()
    out = nc.dram_tensor("out", (1, SEQ, D), F32, kind="ExternalOutput").ap()
    build(nc, io, out)
    r = _run(nc, [arrays], core_ids=[0])
    return r.results[0]["out"]
```

```python
from contextlib import ExitStack
import math

import numpy as np
import concourse.bass as bass
from concourse import mybir

ALU = mybir.AluOpType
ACT = mybir.ActivationFunctionType
AX = mybir.AxisListType
F32 = mybir.dt.float32
I32 = mybir.dt.int32

P = 128
D = 1024
DC = D // P
LAYERS = 2
CTX = 256
SEQ = 512
N = CTX + SEQ
NT = N // P
CT = CTX // P
GRID = 64
NA_KH, NA_KW = 8, 16
ROFF = 2 * NA_KH - 1
COFF = 2 * NA_KW - 1
HEADS = 4
HD = 64
MLA_D = 96
DQK = 32
GW = 256
STATE = 128
CONV = 5
EPS = 1e-6
BIG = 1e30

NA0, MLA0, DIF0, Z0, XBC0, DT0, N_IN = 0, 768, 1184, 1952, 2208, 2976, 2984
PM, PDT, PNK, PNV, PDK, PDV, PNQ, PDQ, PZ, PW = 0, 416, 424, 680, 936, 1192, 1448, 1704, 1960, 2216
XBC = DT0 - XBC0
XM = XBC // P

REL_PAD = GRID
REL_W = HEADS * ROFF * COFF + 2 * REL_PAD

EXP, EPG, GROUPS, FF = 16, 4, 4, 512
FC = FF // P
TOPK = 2

C_ID, C_U, C_L, C_SU, C_ONE = 0, 128, 256, 384, 512
C_MASK = 640
C_COS = C_MASK + GRID
C_SIN = C_COS + 4 * 16
C_THR = C_SIN + 4 * 16
C_TRI = C_THR + NT
C_BLK = C_TRI + EXP * EXP
NBMAX = N * TOPK // P + EXP
C_DEC = C_BLK + NBMAX
C_TOK = C_DEC + EXP
C_W = C_TOK + NT

ROWS = [("na_g_q", 64), ("na_g_k", 64), ("mla_g_qa", 256), ("mla_g_kva", 128), ("mla_g_q", 96),
        ("mla_g_k", 96), ("diff_g_q", 32), ("diff_g_k", 32), ("diff_g_sub", 64), ("ssd_g_norm", 256),
        ("ssd_dt_bias", 8), ("ssd_a_log", 8), ("ssd_d", 8), ("diff_lambda", 128),
        ("moe_b_group", 4), ("moe_b_expert", 16)]
ROW_AT = {}
_at = 0
for _name, _w in ROWS:
    ROW_AT[_name] = (_at, _w)
    _at += _w
ROWS_W = _at

A_B = 0
A_C = A_B + DC * N
A_D = A_C + NT * PW
XW = N + 4
A_RAW = A_D + XM * XW
RAWW = XW + 4
A_E = A_RAW + 2 * RAWW
E_W = 8192
A_F = A_E + E_W
F_XB, F_KM, F_KN = 0, 3072, 6144
ARENA = A_F + 9216
M_W = A_B + DC * N
M_WSET = 2 * DC * FF + FC * D
M_X = 0
M_Y = M_W + 2 * M_WSET


LAM_INIT = [0.8 - 0.6 * math.exp(-0.3 * layer) for layer in range(LAYERS)]


def constants():
    c = np.zeros((P, C_W), np.float32)
    i = np.arange(P)
    c[:, C_ID:C_ID + P] = np.eye(P)
    c[:, C_U:C_U + P] = i[:, None] <= i[None, :]
    c[:, C_L:C_L + P] = i[:, None] >= i[None, :]
    c[:, C_SU:C_SU + P] = i[:, None] < i[None, :]
    c[:, C_ONE:C_ONE + P] = 1.0
    q, k = np.arange(GRID)[:, None], np.arange(GRID)[None, :]
    lo = np.clip(q - NA_KW // 2, 0, GRID - NA_KW)
    m = np.where((k >= lo) & (k < lo + NA_KW), 0.0, -BIG)
    c[:, C_MASK:C_MASK + GRID] = np.concatenate([m, m])
    inv = np.power(np.float32(10000.0), -np.arange(8, dtype=np.float32) / np.float32(8)).astype(np.float32)
    t = np.arange(SEQ)
    ang = np.concatenate([(t // GRID).astype(np.float32)[:, None] * inv,
                          (t % GRID).astype(np.float32)[:, None] * inv], axis=-1)
    c[:, C_COS:C_COS + 64] = np.cos(ang).astype(np.float32).reshape(4, P, 16).transpose(1, 0, 2).reshape(P, 64)
    c[:, C_SIN:C_SIN + 64] = np.sin(ang).astype(np.float32).reshape(4, P, 16).transpose(1, 0, 2).reshape(P, 64)
    c[:, C_THR:C_THR + NT] = P * np.arange(NT)
    e = np.arange(EXP)
    c[:, C_TRI:C_TRI + EXP * EXP] = (e[None, :] < e[:, None]).astype(np.float32).reshape(-1)
    c[:, C_BLK:C_BLK + NBMAX] = np.arange(NBMAX)
    c[:, C_DEC:C_DEC + EXP] = EXP - e
    c[:, C_TOK:C_TOK + NT] = i[:, None] + P * np.arange(NT)[None, :]
    return c


def bc(ap, *free):
    return bass.AP(ap.tensor, ap.offset, [list(ap.ap[0])] + [list(x) for x in free])


class Chain:

    def __init__(self, eng, sem):
        self.eng, self.sem, self.n = eng, sem, 0

    def __call__(self, ins):
        self.n += 1
        ins.then_inc(self.sem, 1)
        self.eng.wait_ge(self.sem, self.n)


def build(nc, io, out):
    st = ExitStack()
    with st:
        sems = {}

        def S(name):
            if name not in sems:
                sems[name] = st.enter_context(nc.semaphore(name))
            return sems[name]

        def sb(name, w, dt=F32):
            return st.enter_context(nc.sbuf_tensor(name, [P, w], dt))

        hT_ = sb("hT", DC * N)
        X = sb("arena", ARENA)
        K = sb("consts", C_W)
        rows = sb("rows", ROWS_W)
        modcol = sb("modcol", LAYERS * 48 * 2)
        acol = sb("acol", LAYERS * 2 * DC * 2)
        gcol = sb("gcol", LAYERS * 2 * DC)
        convw = sb("convw", LAYERS * XM * 6)
        ss = sb("ss", NT * 26)
        ss2 = sb("ss2", NT * 8)
        sc = sb("sc", 32)
        cc = sb("cc", 16)
        ssd = sb("ssd", 10 * 48)
        att = sb("att_small", 16)
        wtok = sb("wtok", NT * TOPK)
        dest = sb("dest", NT * TOPK, I32)
        tokid = sb("tokid", NT, I32)
        blk_e = sb("blk_e", NBMAX, I32)
        slots = sb("slots", NBMAX, I32)
        slot1 = sb("slot1", 2, I32)
        npair = sb("npair", 1, I32)

        PS = st.enter_context(nc.psum_tensor("ps", [P, 8, 512], F32))

        dram = {}
        for nm, shape, dt in (("slot_tok", (NBMAX * P, 1), I32), ("f_rows", (N + 1, D), F32),
                              ("y_rows", (NBMAX * P, D), F32), ("rel_rows", (LAYERS * GRID, REL_W), F32)):
            dram[nm] = nc.dram_tensor(nm, shape, dt).ap()

        hT = hT_[:, :].rearrange("p (c n) -> p c n", c=DC)

        def ar(off, n):
            return X[:, off:off + n]

        aT = ar(A_B, DC * N).rearrange("p (c n) -> p c n", c=DC)
        ot = ar(A_B, NT * D).rearrange("p (t d) -> p t d", t=NT)
        p = ar(A_C, NT * PW).rearrange("p (t d) -> p t d", t=NT)
        oT = ar(A_C, DC * N).rearrange("p (c n) -> p c n", c=DC)
        xbcT = ar(A_D, XM * XW).rearrange("p (m n) -> p m n", m=XM)
        raw = ar(A_RAW, 2 * RAWW).rearrange("p (b n) -> p b n", b=2)
        sq2 = ar(A_RAW, 2 * N).rearrange("p (b n) -> p b n", b=2)
        wbuf = ar(A_E, E_W).rearrange("p (b k n) -> p b k n", b=2, k=DC)
        kTm = ar(A_F + F_KM, 4 * N).rearrange("p (h n) -> p h n", h=4)
        kTn = ar(A_F + F_KN, 4 * N).rearrange("p (h n) -> p h n", h=4)
        xB = ar(A_F + F_XB, NT * 512).rearrange("p (t d) -> p t d", t=NT)
        ident = K[:, C_ID:C_ID + P]
        triU = K[:, C_U:C_U + P]
        triL = K[:, C_L:C_L + P]
        strictU = K[:, C_SU:C_SU + P]
        ones = K[:, C_ONE:C_ONE + P]
        mod4 = modcol[:, :].rearrange("p (l j s) -> p l j s", l=LAYERS, s=2)
        acol4 = acol[:, :].rearrange("p (l w c s) -> p l w c s", l=LAYERS, w=2, s=2)
        gcol3 = gcol[:, :].rearrange("p (l w c) -> p l w c", l=LAYERS, w=2)
        cw = convw[:, :].rearrange("p (l m j) -> p l m j", l=LAYERS, j=6)

        def row(name, off=0, n=None):
            a, w = ROW_AT[name]
            return rows[:, a + off:a + off + (n or w)]

        def xcol(t):
            return t * P if t < CT else t * P + 4

        def out_tiles(L):
            return list(range(NT)) if L < LAYERS - 1 else list(range(CT, NT))

        def streams(lo, hi):
            r = []
            if lo < CTX:
                r.append((1, lo, CTX))
            r.append((0, max(lo, CTX), hi))
            return r

        def tok_lo(L):
            return 0 if L < LAYERS - 1 else CTX

        def segs(lo):
            return [(0, 512), (512, N)] if lo == 0 else [(CTX, N)]

        MODN = 6 * D // 512
        mod_jobs = [(L, n) for L in range(LAYERS) for n in range(MODN)]
        CH = [("x", 0, 4), ("x", 4, 2),
              ("t", PM, 424, [(0, MLA0, 416), (416, DT0, 8)], False),
              ("t", PNK, 512, [(0, NA0 + 256, 512)], False),
              ("t", PDK, 512, [(0, DIF0 + 256, 512)], False),
              ("t", PNQ, 512, [(0, NA0, 256), (256, DIF0, 256)], True),
              ("t", PZ, 256, [(0, Z0, 256)], True)]
        NCH = len(CH)
        TCH = [j for j in range(NCH) if CH[j][0] == "t"]
        JOBS = [[(j, t) for j in TCH for t in (out_tiles(L) if CH[j][4] else range(NT))] for L in range(LAYERS)]
        PJ0 = [0, len(JOBS[0]), len(JOBS[0]) + len(JOBS[1])]
        XB_AT, CUM_AT, SCAN_AT = 0, 6, 7

        def units(L):
            r = []
            for g, nh in (("mla", 4), ("na", 4), ("dif", 8)):
                for t in out_tiles(L):
                    r += [(g, h, t) for h in range(nh)]
            return r

        UN = [units(L) for L in range(LAYERS)]
        U0 = [0, len(UN[0])]
        ALLU = UN[0] + UN[1]
        FULLS = [0]
        for _g, _h, _t in ALLU:
            FULLS.append(FULLS[-1] + (1 if _t >= CT else 0))
        PERJOB = {"mla": 1, "na": 2, "dif": 4}
        JOB = []
        jobs = []
        for _u, (_g, _h, _t) in enumerate(ALLU):
            if _h % PERJOB[_g] == 0:
                jobs.append((_u, _g, _h, _t))
            JOB.append(len(jobs) - 1)
        SU = []
        for L in range(LAYERS):
            o0, o1 = [0, 1, 2, 3, 4, 5], [1, 0, 5, 4, 3, 2]
            SU += [(L, dd, o[i]) for i in range(NT) for dd, o in ((0, o0), (1, o1))]
        YU = [0]
        for L, dd, t in SU:
            YU.append(YU[-1] + (1 if t in out_tiles(L) else 0))
        NB = [len(out_tiles(L)) * P * TOPK // P + EXP for L in range(LAYERS)]
        PAIRS = [n // 2 for n in NB]
        MINP = [len(out_tiles(L)) * TOPK // 2 for L in range(LAYERS)]
        NB0 = [0, NB[0] + 2]
        OT0 = [0, NT]
        OTN = [NT, NT - CT]

        modrow = ar(A_C, LAYERS * 6 * D)

        def mod_w(i):
            return ar(A_E + (i % 3) * 4096, 4096)

        rs = ar(A_F + 3264, N)
        cT = ar(A_E, 3 * N).rearrange("p (c n) -> p c n", c=3)
        wqb = ar(A_E + 2304, 768)
        wkvb = ar(A_E + 3072, 512)
        scr = A_E + 3584
        sca = A_F + F_KM
        scs = A_F + F_KM + 3328
        Pb = ar(A_E, 2 * N).rearrange("p (b n) -> p b n", b=2)
        PTb = ar(A_E + 2 * N, 2 * N).rearrange("p (b n) -> p b n", b=2)
        qT = ar(A_E + 4 * N, 2 * P).rearrange("p (b n) -> p b n", b=2)
        bias4 = ar(A_D, HEADS * ROFF * GRID).rearrange("p (h r c) -> p h r c", h=HEADS, r=ROFF)
        wo = ar(A_E, E_W)

        def sv(k):
            return ssd[:, k * 48:(k + 1) * 48].rearrange("p (t h) -> p t h", t=NT)

        def GMb(w):
            return ar(sca + 256 * (YU[w] % 2), 256)

        def Mall(w):
            return ar(sca + 512 + 512 * (YU[w] % 2), 512)

        def Mb(w, h):
            return Mall(w)[:, h * P:(h + 1) * P]

        def xdt(w):
            return ar(sca + 1536 + 256 * (w % 2), 256)

        def xdte(w):
            return ar(sca + 2048 + 256 * (w % 2), 256)

        def state(dd):
            return ar(sca + 2560 + 256 * dd, 256)

        ytmp = ar(sca + 3072, 256)
        yacc = ar(A_RAW, NT * GW).rearrange("p (t d) -> p t d", t=NT)
        ftok = ar(A_F, 2 * D).rearrange("p (b n) -> p b n", b=2)
        zrows = ar(A_F + 5 * D, D)
        YZ0 = N * TOPK // P
        wr = ar(A_F + 3 * D, DC * 20).rearrange("p (k n) -> p k n", k=DC)
        RT = A_F + 4 * D

        def r_(off, n):
            return ar(RT + off, n)

        r_lg = r_(0, 120).rearrange("p (t n) -> p t n", t=NT)
        r_oh = [r_(420, 96).rearrange("p (t e) -> p t e", t=NT), r_(516, 96).rearrange("p (t e) -> p t e", t=NT)]
        r_sel = r_(612, 96).rearrange("p (t e) -> p t e", t=NT)

        def r6(k):
            return r_(168 + 6 * k, 6)

        def xg(par):
            return ar(M_X + par * D, D)

        def xT(par):
            return ar(M_X + 2 * D + par * D, D)

        def hid(par):
            return ar(M_X + 4 * D + par * FF, FF)

        def hidT(par):
            return ar(M_X + 4 * D + 2 * FF + par * FF, FF)

        def ysb(par):
            return ar(M_Y + par * D, D)

        def moe_w(par):
            o = M_W + par * M_WSET
            return (ar(o, DC * FF).rearrange("p (k n) -> p k n", k=DC),
                    ar(o + DC * FF, DC * FF).rearrange("p (k n) -> p k n", k=DC),
                    ar(o + 2 * DC * FF, FC * D).rearrange("p (k n) -> p k n", k=FC))

        def r12(i, k):
            return ar(A_F + 4 * D + (2 * (i % 2) + k) * D, D)

        restok = ftok

        def win_loads(L, j):
            n = [sum(1 if CH[q][0] == "x" else len(CH[q][3]) for q in range(top) if q % 2 == j % 2) for top in (NCH, j + 1)]
            return 16 * (n[0] * L + n[1])

        def win_done(L, j):
            if CH[j][0] == "x":
                return S("xp_ps"), XM * L + CH[j][1] + CH[j][2]
            return S("pj_ps"), PJ0[L] + sum(1 for q, _ in JOBS[L] if q <= j)

        def last_pair(eng, L):
            eng.wait_ge(S("blk_ready"), L + 1)
            return eng.value_load(npair[0:1, 0:1], min_val=MINP[L] - 1, max_val=PAIRS[L] - 1)

        def cnt2(L, i):
            return NT // 2 * L + i // 2

        block = st.enter_context(nc.Block())

        @block.sync
        def _(sp):
            sp.dma_start(K[:, :], io["consts"]).then_inc(S("consts_in"), 16)
            with nc.allow_non_contiguous_dma(reason="small columns"):
                sp.dma_start(cc[:, 0:8], io["c"][0].rearrange("(k p) -> p k", p=P)).then_inc(S("cc_in"), 16)
                sp.dma_start(cc[:, 8:16], io["c_ctx"].rearrange("(k p) -> p k", p=P)).then_inc(S("cc_in"), 16)
            for t in range(NT):
                src = io["ctx"][0, t * P:(t + 1) * P, :] if t < CT else io["x"][0, (t - CT) * P:(t - CT + 1) * P, :]
                sp.dma_start(ar(A_B + t * D, D), src).then_inc(S("x_in"), 16)
            sp.dma_start(modrow[0:2, :],
                         io["b_mod"].rearrange("l n -> (l n)").partition_broadcast(2)).then_inc(S("bmod_in"), 16)
            for i, (L, n) in enumerate(mod_jobs):
                if i >= 3:
                    sp.wait_ge(S("wmod_used"), i - 2)
                sp.dma_start(mod_w(i).rearrange("p (k n) -> p k n", k=DC),
                             io["w_mod"][L].rearrange("(k p) n -> p k n", p=P)[:, :, n * 512:(n + 1) * 512]
                             ).then_inc(S(f"wmod_in{i % 3}"), 16)
                if i == MODN:
                    sp.wait_ge(S("zero_row"), 1)
                    sp.dma_start(dram["y_rows"].rearrange("(b p) n -> p b n", p=P)[:, YZ0:, :],
                                 bc(zrows, (0, NBMAX - YZ0), (1, D))).then_inc(S("y_zero"), 16)
                    sp.dma_start(dram["f_rows"][N:N + 1, :], zrows[0:1, :]).then_inc(S("y_zero"), 16)
                if i == 2:
                    with nc.allow_non_contiguous_dma(reason="small columns"):
                        for l2 in range(LAYERS):
                            for w, nm in ((0, "g_mix"), (1, "g_ffn")):
                                sp.dma_start(gcol3[:, l2, w, :], io[nm][l2].rearrange("(k p) -> p k", p=P)
                                             ).then_inc(S("cols_in"), 16)
                            for m in range(XM):
                                sp.dma_start(cw[:, l2, m, 0:CONV],
                                             io["ssd_conv_w"][l2, :, m * P:(m + 1) * P].rearrange("j p -> p j")
                                             ).then_inc(S("cols_in"), 16)
                            sp.dma_start(cw[:, l2, :, CONV], io["ssd_conv_b"][l2].rearrange("(m p) -> p m", p=P)
                                         ).then_inc(S("cols_in"), 16)
            for l2 in range(LAYERS):
                sp.dma_start(dram["rel_rows"][l2 * GRID:(l2 + 1) * GRID, :], io["rel_pad"][l2].partition_broadcast(GRID)
                             ).then_inc(S("rel_copied"), 16)
            for L in range(LAYERS):
                if L:
                    sp.wait_ge(S("h_final"), 1)
                for nm, w in ROWS:
                    src = io[nm][L]
                    if len(src.shape) == 2:
                        src = src.rearrange("a b -> (a b)")
                    sp.dma_start(row(nm), src.partition_broadcast(P)).then_inc(S("rows_in"), 16)
                if L == 0:
                    sp.wait_ge(S("wmod_used"), len(mod_jobs))
                for j, ch in enumerate(CH):
                    if j >= 2:
                        sp.wait_ge(*win_done(L, j - 2))
                    src = io["w_in"][L].rearrange("(k p) n -> p k n", p=P)
                    b = wbuf[:, j % 2]
                    if ch[0] == "x":
                        a, w = XBC0 + ch[1] * P, ch[2] * P
                        sp.dma_start(b[:, :, 0:w], src[:, :, a:a + w]).then_inc(S(f"win_in{j % 2}"), 16)
                    else:
                        with nc.allow_non_contiguous_dma(reason="dt columns"):
                            for o, a, w in ch[3]:
                                sp.dma_start(b[:, :, o:o + w], src[:, :, a:a + w]).then_inc(S(f"win_in{j % 2}"), 16)
                sp.wait_ge(S("scan_done"), L + 1)
                sp.wait_ge(S("rel_copied"), 16 * LAYERS)
                rb = dram["rel_rows"]
                for half in range(2):
                    base = rb.offset + L * GRID * REL_W + REL_PAD + (NA_KW - 1)
                    n_ro = ROFF - half
                    for h in range(HEADS):
                        dst = bias4[64 * half:64 * half + 64, h, half:ROFF, :]
                        src = bass.AP(rb.tensor, base + h * ROFF * COFF, [[REL_W - 1, GRID], [COFF, n_ro], [1, GRID]])
                        sp.dma_start(dst, src).then_inc(S("bias_in"), 16)
                sp.wait_ge(*win_done(L, NCH - 1))
                sp.dma_start(wqb.rearrange("p (k n) -> p k n", k=2),
                             io["mla_w_qb"][L].rearrange("(k p) n -> p k n", p=P)).then_inc(S("wmla_in"), 16)
                sp.dma_start(wkvb, io["mla_w_kvb"][L]).then_inc(S("wmla_in"), 16)
                sp.wait_ge(S("mix_done"), L + 1)
                sp.dma_start(wo.rearrange("p (k n) -> p k n", k=DC),
                             io["w_out"][L].rearrange("(k p) n -> p k n", p=P)).then_inc(S("wo_in"), 16)
                sp.wait_ge(S("h_mid"), L + 1)
                with nc.allow_non_contiguous_dma(reason="router columns"):
                    sp.dma_start(wr[:, :, 0:GROUPS], io["moe_w_group"][L].rearrange("(k p) n -> p k n", p=P)
                                 ).then_inc(S("wr_in"), 16)
                    sp.dma_start(wr[:, :, GROUPS:], io["moe_w_expert"][L].rearrange("(k p) n -> p k n", p=P)
                                 ).then_inc(S("wr_in"), 16)
                for i, t in enumerate(out_tiles(L)):
                    sp.wait_ge(S("ftok_a"), OT0[L] + i + 1)
                    sp.wait_ge(S("ftok_d"), OT0[L] + i + 1)
                    sp.dma_start(dram["f_rows"][t * P:(t + 1) * P, :], ftok[:, i % 2, :]).then_inc(S(f"f_out{i % 2}"), 16)
                wgv = io["moe_w_gate"][L].rearrange("e (k p) n -> e p k n", p=P)
                wuv = io["moe_w_up"][L].rearrange("e (k p) n -> e p k n", p=P)
                wdv = io["moe_w_down"][L].rearrange("e (k p) n -> e p k n", p=P)
                sp.wait_ge(S("blk_ready"), L + 1)

                def load_block(i, par, first):
                    b = 2 * i + par
                    e = sp.value_load(blk_e[0:1, bass.ds(b, 1)], min_val=0, max_val=EXP - 1)
                    if not first:
                        sp.wait_ge(S("dn_ps"), NB0[L] + b - 1)
                    wg, wu, wd = moe_w(par)
                    for dst, v in ((wg, wgv), (wu, wuv)):
                        sp.dma_start(dst, v[bass.ds(e, 1)].rearrange("e p k n -> p (e k) n")).then_inc(S(f"gu_in{par}"), 16)
                    sp.dma_start(wd, wdv[bass.ds(e, 1)].rearrange("e p k n -> p (e k) n")).then_inc(S(f"wd_in{par}"), 16)

                for par in range(2):
                    load_block(0, par, True)
                sp.wait_ge(S("slots_fill"), L + 1)
                sp.dma_start(dram["slot_tok"].rearrange("(p b) o -> p (b o)", p=P), slots[:, :]).then_inc(S("slots_init"), 16)
                sp.wait_ge(S("slot_scat"), 16 * TOPK * (OT0[L] + OTN[L]))
                with nc.allow_non_contiguous_dma(reason="slot columns"):
                    sp.dma_start(slots[:, :], dram["slot_tok"].rearrange("(b p) o -> p (b o)", p=P)).then_inc(S("slots_in"), 16)
                lastp = last_pair(sp, L)
                with sp.Fori(1, lastp + 1) as i:
                    for par in range(2):
                        load_block(i, par, False)
                for par in range(2):
                    sp.wait_ge(S(f"gu_in{par}"), 32 * lastp + 32 + 16 * NB0[L])
                    sp.wait_ge(S(f"wd_in{par}"), 16 * lastp + 16 + 8 * NB0[L])
                with sp.Fori(lastp + 1, PAIRS[L] + 1):
                    for par in range(2):
                        sp.sem_inc(S(f"gu_in{par}"), 32)
                        sp.sem_inc(S(f"wd_in{par}"), 16)
            for i in range(NT - CT):
                sp.wait_ge(S("res_a"), i + 1)
                sp.wait_ge(S("res_d"), i + 1)
                sp.dma_start(out[0, i * P:(i + 1) * P, :], restok[:, i % 2, :]).then_inc(S(f"res_out{i % 2}"), 16)
            for q in range(2):
                sp.wait_ge(S(f"res_out{q}"), 16 * ((NT - CT) // 2))

        @block.tensor
        def _(pe):
            pe.wait_ge(S("consts_in"), 16)
            pe.wait_ge(S("x_in"), 16 * NT)
            for t in range(NT):
                if t >= 2:
                    pe.wait_ge(S("x_ev_a"), t - 1)
                    pe.wait_ge(S("x_ev_d"), t - 1)
                for c in range(DC):
                    last = pe.transpose(PS[:, 2 * (t % 2) + c // 4, (c % 4) * P:(c % 4 + 1) * P],
                                        ar(A_B + t * D + c * P, P), ident)
                last.then_inc(S("x_ps"), 1)
            pe.wait_ge(S("cc_silu"), 1)
            for i in range(len(mod_jobs)):
                pe.wait_ge(S(f"wmod_in{i % 3}"), 16 * (i // 3 + 1))
                if i >= 2:
                    pe.wait_ge(S("mod_ev"), i - 1)
                for k in range(DC):
                    last = pe.matmul(PS[0:2, 4 + i % 2, :], bc(cc[:, k:k + 1], (8, 2)),
                                     mod_w(i)[:, k * 512:(k + 1) * 512], start=(k == 0), stop=(k == DC - 1))
                last.then_inc(S("wmod_used"), 1)
            pe.wait_ge(S("mod_ev"), len(mod_jobs))
            for j in range(LAYERS * 48):
                last = pe.transpose(PS[:, 6, 2 * j:2 * j + 2], modrow[0:2, j * P:(j + 1) * P], ident[0:2, 0:2])
            last.then_inc(S("modT_ps"), 1)

            def norm_sums(L, w):
                lo = 0 if w == 0 else tok_lo(L)
                base = (2 * L + w) * DC
                for c in range(DC):
                    pe.wait_ge(S("sq_done"), base + c + 1)
                    for bk, (a, b) in enumerate(segs(lo)):
                        last = pe.matmul(PS[:, bk, 0:b - a], ones, sq2[:, c % 2, a:b], start=(c == 0), stop=(c == DC - 1))
                    last.then_inc(S("sq_used"), 1)

            def in_proj(L):
                pe.wait_ge(S("aT_ready"), L + 1)
                k = 0
                for j, ch in enumerate(CH):
                    pe.wait_ge(S(f"win_in{j % 2}"), win_loads(L, j))
                    if ch[0] == "x":
                        for m in range(ch[1], ch[1] + ch[2]):
                            if m >= 2:
                                pe.wait_ge(S("raw_ready"), XM * L + m - 1)
                            mm = m - ch[1]
                            for bk, (a, b) in enumerate(segs(0)):
                                for c in range(DC):
                                    last = pe.matmul(PS[:, 2 * (m % 2) + bk, 0:b - a],
                                                     wbuf[:, j % 2, c, mm * P:(mm + 1) * P], aT[:, c, a:b],
                                                     start=(c == 0), stop=(c == DC - 1))
                            last.then_inc(S("xp_ps"), 1)
                        continue
                    for t in [tt for jj, tt in JOBS[L] if jj == j]:
                        if k >= 2:
                            pe.wait_ge(S("pj_ev"), PJ0[L] + k - 1)
                        for c in range(DC):
                            last = pe.matmul(PS[:, 4 + k % 2, 0:ch[2]], aT[:, c, t * P:(t + 1) * P],
                                             wbuf[:, j % 2, c, 0:ch[2]], start=(c == 0), stop=(c == DC - 1))
                        last.then_inc(S("pj_ps"), 1)
                        if XB_AT <= k < XB_AT + 2:
                            xb_transposes(L, k - XB_AT)
                        if k == CUM_AT:
                            scan_sums(L)
                        if SCAN_AT <= k <= SCAN_AT + 2 * NT:
                            scan_step(L, k - SCAN_AT)
                        k += 1

            def xb_transposes(L, half):
                if half == 0:
                    pe.wait_ge(S("xbc_ready"), XM * (L + 1))
                for t in range(3 * half, 3 * half + 3):
                    if t >= 2:
                        pe.wait_ge(S("xb_ev"), NT * L + t - 1)
                    for q in range(4):
                        last = pe.transpose(PS[:, 6 + t % 2, q * P:(q + 1) * P], xbcT[:, q, xcol(t):xcol(t) + P], ident)
                    last.then_inc(S("xb_ps"), 1)

            def mla_prep(L):
                pe.wait_ge(S("stats_done"), L + 1)
                for t in range(NT):
                    if t >= 2:
                        pe.wait_ge(S("cT_ev"), NT * L + t - 1)
                    for c in range(3):
                        last = pe.transpose(PS[:, t % 2, c * P:(c + 1) * P], p[:, t, PM + c * P:PM + (c + 1) * P], ident)
                    last.then_inc(S("cT_ps"), 1)
                pe.wait_ge(S("wmla_in"), 32 * (L + 1))
                for t in range(NT):
                    pe.wait_ge(S("cT_ev"), NT * L + t + 1)
                    if t >= 2:
                        pe.wait_ge(S("mq_ev"), NT * L + t - 1)
                        pe.wait_ge(S("mkv_ev"), NT * L + t - 1)
                    for c in range(2):
                        pe.matmul(PS[:, 2 + t % 2, 0:384], cT[:, c, t * P:(t + 1) * P], wqb[:, c * 384:(c + 1) * 384],
                                  start=(c == 0), stop=(c == 1))
                    last = pe.matmul(PS[:, 4 + t % 2, :], cT[:, 2, t * P:(t + 1) * P], wkvb, start=True, stop=True)
                    last.then_inc(S("mla_ps"), 1)

            def key_transposes(L):
                pe.wait_ge(S("na_norm"), L + 1)
                pe.wait_ge(S("dif_norm"), L + 1)
                for n in range(2 * NT):
                    kind, t = n // NT, n % NT
                    if n >= 2:
                        pe.wait_ge(S("kt_ev"), 2 * NT * L + n - 1)
                    if kind == 1 and t == 0:
                        pe.wait_ge(S("m_norm"), L + 1)
                    for q in range(4):
                        if kind == 0:
                            a = PNK + q * P if q < 2 else PDK + (q - 2) * P
                            src, rows_ = p[:, t, a:a + P], P
                        else:
                            a = 640 + MLA_D * q
                            src, rows_ = ot[:, t, a:a + MLA_D], MLA_D
                        last = pe.transpose(PS[0:rows_, 6 + n % 2, q * P:(q + 1) * P], src, ident)
                    last.then_inc(S("kt_ps"), 1)

            def attention(L):
                n, u0 = len(UN[L]), U0[L]
                pe.wait_ge(S("kt_ev"), 2 * NT * (L + 1))

                def q_transpose(j):
                    _, g, h, t = jobs[j]
                    if j:
                        pe.wait_ge(S("qT_ev"), j)
                    if g == "mla":
                        src, r = ot[:, t, 256 + MLA_D * h:256 + MLA_D * (h + 1)], MLA_D
                    elif g == "na":
                        src, r = p[:, t, PNQ + HD * h:PNQ + HD * h + P], P
                    else:
                        src, r = p[:, t, PDQ + DQK * h:PDQ + DQK * h + P], P
                    pe.transpose(PS[0:r, 7, 0:P], src, ident).then_inc(S("qT_ps"), 1)

                for i in range(n + 2):
                    if i < n:
                        u = u0 + i
                        g, h, t = ALLU[u]
                        if i == 0:
                            q_transpose(JOB[u])
                        if i + 1 < n and JOB[u + 1] != JOB[u]:
                            q_transpose(JOB[u + 1])
                        pe.wait_ge(S("qT_ev"), JOB[u] + 1)
                        if u >= 2:
                            pe.wait_ge(S("exp_done"), u - 1)
                        qb = qT[:, JOB[u] % 2]
                        if g == "mla":
                            lo, hi, kt = 0, MLA_D, kTm[:, h]
                        elif g == "na":
                            lo, hi, kt = HD * (h % 2), HD * (h % 2) + HD, kTn[:, h // 2]
                        else:
                            lo, hi, kt = DQK * (h % 4), DQK * (h % 4) + DQK, kTn[:, 2 + h // 4]
                        if g == "na" and t == CT:
                            pe.wait_ge(S("bias_ready"), L + 1)
                        b0 = 2 * (u % 2)
                        full = t >= CT
                        bias = g == "na" and full
                        last = pe.matmul(PS[:, b0, 0:(512 if full else CTX)], qb[lo:hi], kt[lo:hi, 0:(512 if full else CTX)],
                                         start=True, stop=not bias, skip_group_check=True)
                        if full:
                            last = pe.matmul(PS[:, b0 + 1, 0:256], qb[lo:hi], kt[lo:hi, 512:N], start=True,
                                             stop=not bias, skip_group_check=True)
                        if bias:
                            s0 = NA_KH - 1 - 2 * (t - CT)
                            pe.matmul(PS[:, b0, 256:512], ident, bias4[:, h, s0:s0 + 4, :], start=False, stop=True,
                                      skip_group_check=True)
                            last = pe.matmul(PS[:, b0 + 1, 0:256], ident, bias4[:, h, s0 + 4:s0 + 8, :], start=False,
                                             stop=True, skip_group_check=True)
                        last.then_inc(S("s_ps"), 1)
                    if 1 <= i <= n:
                        u = u0 + i - 1
                        t = ALLU[u][2]
                        pe.wait_ge(S("exp_done"), u + 1)
                        if u >= 1:
                            pe.wait_ge(S("pt_ev_a"), u)
                            if FULLS[u]:
                                pe.wait_ge(S("pt_ev_d"), FULLS[u])
                        for c in range(NT if t >= CT else CT):
                            last = pe.transpose(PS[:, 4 + c // 4, (c % 4) * P:(c % 4 + 1) * P],
                                                Pb[:, u % 2, c * P:(c + 1) * P], ident)
                        last.then_inc(S("t_ps"), 1)
                    if i >= 2:
                        u = u0 + i - 2
                        g, h, t = ALLU[u]
                        pe.wait_ge(S("pt_ev_a"), u + 1)
                        if FULLS[u + 1]:
                            pe.wait_ge(S("pt_ev_d"), FULLS[u + 1])
                        if u >= 1:
                            pe.wait_ge(S("o_ev"), u)
                        v0 = {"mla": PM + HD * h, "na": PNV + HD * h, "dif": PDV + HD * (h // 2)}[g]
                        nk = NT if t >= CT else CT
                        for c in range(nk):
                            last = pe.matmul(PS[:, 6, 0:HD], PTb[:, u % 2, c * P:(c + 1) * P], p[:, c, v0:v0 + HD],
                                             start=(c == 0), stop=(c == nk - 1))
                        last.then_inc(S("o_ps"), 1)

            def scan_sums(L):
                pe.wait_ge(S("xb_ev"), NT * (L + 1))
                pe.wait_ge(S("la_done"), L + 1)
                la = sv(0)
                pe.matmul(PS[:, 7, 0:24], triU, la[:, :, 0:4], start=True, stop=True)
                pe.matmul(PS[:, 7, 24:48], triL, la[:, :, 4:8], start=True, stop=True)
                pe.matmul(PS[:, 7, 48:96], ones, la, start=True, stop=True).then_inc(S("cum_ps"), 1)

            def scan_step(L, i):
                la = sv(0)
                n = 2 * NT
                if i == 0:
                    pe.wait_ge(S("cum_done"), L + 1)
                if i < n:
                    w = n * L + i
                    _, dd, t = SU[w]
                    if t in out_tiles(L):
                        if YU[w] >= 1:
                            pe.wait_ge(S("front_done"), YU[w])
                        yp = YU[w] % 2
                        tri = triU if dd == 0 else triL
                        for h in range(HEADS):
                            pe.matmul(PS[:, yp, h * P:(h + 1) * P], bc(la[:, t, dd * 4 + h:dd * 4 + h + 1], (0, P)), tri,
                                      start=True, stop=True)
                        x0 = xcol(t)
                        for g in range(2):
                            last = pe.matmul(PS[:, 2, g * P:(g + 1) * P], xbcT[:, 2 + g, x0:x0 + P],
                                             xbcT[:, 4 + g, x0:x0 + P], start=True, stop=True)
                        last.then_inc(S("rg_ps"), 1)
                if i >= 1:
                    w = n * L + i - 1
                    _, dd, t = SU[w]
                    pe.wait_ge(S("xdt_done"), w + 1)
                    if w >= 1:
                        pe.wait_ge(S("state_done"), w)
                    if t in out_tiles(L):
                        pe.wait_ge(S("m_done"), YU[w] + 1)
                        if YU[w] >= 1:
                            pe.wait_ge(S("y_done"), YU[w])
                        x0 = xcol(t)
                        for h in range(HEADS):
                            pe.matmul(PS[:, 3, h * HD:(h + 1) * HD], Mb(w, h), xdt(w)[:, h * HD:(h + 1) * HD],
                                      start=True, stop=True)
                        for g in range(2):
                            last = pe.matmul(PS[:, 3, 256 + g * P:256 + (g + 1) * P], xbcT[:, 4 + g, x0:x0 + P],
                                             state(dd)[:, g * P:(g + 1) * P], start=True, stop=True)
                        last.then_inc(S("y_ps"), 1)
                    for g in range(2):
                        last = pe.matmul(PS[:, 6, g * P:(g + 1) * P], xB[:, t, 256 + g * P:256 + (g + 1) * P],
                                         xdte(w)[:, g * P:(g + 1) * P], start=True, stop=True)
                    last.then_inc(S("st_ps"), 1)

            def out_proj(L):
                pe.wait_ge(S("mix_done"), L + 1)
                for i, t in enumerate(out_tiles(L)):
                    if i >= 2:
                        pe.wait_ge(S("oT_a"), OT0[L] + i - 1)
                        pe.wait_ge(S("oT_d"), OT0[L] + i - 1)
                    for c in range(DC):
                        f = {0: 2, 1: 3, 2: 0, 3: 1}.get(c, c)
                        last = pe.transpose(PS[:, 2 * (i % 2) + c // 4, (c % 4) * P:(c % 4 + 1) * P],
                                            ot[:, t, f * P:(f + 1) * P], ident)
                    last.then_inc(S("oT_ps"), 1)
                pe.wait_ge(S("oT_a"), OT0[L] + OTN[L])
                pe.wait_ge(S("oT_d"), OT0[L] + OTN[L])
                pe.wait_ge(S("wo_in"), 16 * (L + 1))
                for m in range(DC):
                    if m >= 2:
                        pe.wait_ge(S("op_ev"), DC * L + m - 1)
                    for bk, (a, b) in enumerate(segs(tok_lo(L))):
                        for c in range(DC):
                            last = pe.matmul(PS[:, 4 + 2 * (m % 2) + bk, 0:b - a], wo[:, c * D + m * P:c * D + (m + 1) * P],
                                             oT[:, c, a:b], start=(c == 0), stop=(c == DC - 1))
                    last.then_inc(S("op_ps"), 1)

            def route_and_rows(L):
                pe.wait_ge(S("fT_ready"), L + 1)
                pe.wait_ge(S("wr_in"), 32 * (L + 1))
                for t in out_tiles(L):
                    for c in range(DC):
                        last = pe.matmul(PS[:, 4, t * 20:(t + 1) * 20], aT[:, c, t * P:(t + 1) * P], wr[:, c, :],
                                         start=(c == 0), stop=(c == DC - 1))
                last.then_inc(S("lg_ps"), 1)
                for i, t in enumerate(out_tiles(L)):
                    if i >= 2:
                        pe.wait_ge(S("ftok_a"), OT0[L] + i - 1)
                        pe.wait_ge(S("ftok_d"), OT0[L] + i - 1)
                    for c in range(DC):
                        last = pe.transpose(PS[:, 2 * (i % 2) + c // 4, (c % 4) * P:(c % 4 + 1) * P],
                                            aT[:, c, t * P:(t + 1) * P], ident)
                    last.then_inc(S("ftok_ps"), 1)
                pe.wait_ge(S("sel_done"), L + 1)
                tl = out_tiles(L)
                for n_, t in enumerate(tl):
                    for j, t2 in enumerate(tl[:n_ + 1]):
                        pe.matmul(PS[:, 5, t * EXP:(t + 1) * EXP], strictU if t2 == t else ones, r_sel[:, t2, :],
                                  start=(j == 0), stop=(t2 == t))
                for j, t in enumerate(tl):
                    last = pe.matmul(PS[:, 5, NT * EXP:(NT + 1) * EXP], ones, r_sel[:, t, :], start=(j == 0),
                                     stop=(j == len(tl) - 1))
                last.then_inc(S("rank_ps"), 1)

            def experts(L):
                n0 = NB0[L]

                def x_transposes(i, par, first=False):
                    b = 2 * i + par
                    pe.wait_ge(S(f"xg_in{L}{par}"), 16 * (i + 1))
                    if not first:
                        pe.wait_ge(S("xT_a"), n0 + b)
                        pe.wait_ge(S("xT_d"), n0 + b)
                    for c in range(DC):
                        last = pe.transpose(PS[:, c // 4, (c % 4) * P:(c % 4 + 1) * P], xg(par)[:, c * P:(c + 1) * P], ident)
                    last.then_inc(S("xt_ps"), 1)

                def gate_up(i, par, first=False):
                    b = 2 * i + par
                    wg, wu, _ = moe_w(par)
                    pe.wait_ge(S(f"gu_in{par}"), 32 * (i + 1) + 32 * (n0 // 2))
                    pe.wait_ge(S("xT_a"), n0 + b + 1)
                    pe.wait_ge(S("xT_d"), n0 + b + 1)
                    if not first:
                        pe.wait_ge(S("h_done"), n0 + b)
                    for bk, w in ((2, wg), (3, wu)):
                        for c in range(DC):
                            last = pe.matmul(PS[:, bk, :], xT(par)[:, c * P:(c + 1) * P], w[:, c, :], start=(c == 0),
                                             stop=(c == DC - 1))
                    last.then_inc(S("gu_ps"), 1)

                def down(i, par, first=False):
                    b = 2 * i + par
                    pe.wait_ge(S("h_done"), n0 + b + 1)
                    if not first:
                        pe.wait_ge(S("hT_ev"), n0 + b)
                    for c in range(FC):
                        last = pe.transpose(PS[:, 4, c * P:(c + 1) * P], hid(par)[:, c * P:(c + 1) * P], ident)
                    last.then_inc(S("ht_ps"), 1)
                    _, _, wd = moe_w(par)
                    pe.wait_ge(S("hT_ev"), n0 + b + 1)
                    pe.wait_ge(S(f"wd_in{par}"), 16 * (i + 1) + 16 * (n0 // 2))
                    if not first:
                        pe.wait_ge(S("y_a"), n0 + b)
                        pe.wait_ge(S("y_d"), n0 + b)
                    for half in range(2):
                        for c in range(FC):
                            last = pe.matmul(PS[:, 5 + half, :], hidT(par)[:, c * P:(c + 1) * P],
                                             wd[:, c, half * 512:(half + 1) * 512], start=(c == 0), stop=(c == FC - 1))
                    last.then_inc(S("dn_ps"), 1)

                lastp = last_pair(pe, L)
                fl = L == 0
                x_transposes(0, 0, fl)
                gate_up(0, 0, fl)
                x_transposes(0, 1)
                down(0, 0, fl)
                gate_up(0, 1)
                x_transposes(1, 0)
                down(0, 1)
                with pe.Fori(1, lastp) as i:
                    gate_up(i, 0)
                    x_transposes(i, 1)
                    down(i, 0)
                    gate_up(i, 1)
                    x_transposes(i + 1, 0)
                    down(i, 1)
                gate_up(lastp, 0)
                x_transposes(lastp, 1)
                down(lastp, 0)
                gate_up(lastp, 1)
                down(lastp, 1)
                pe.drain()
                with pe.Fori(lastp + 1, PAIRS[L] + 1):
                    for nm in ("xt_ps", "gu_ps", "ht_ps", "dn_ps"):
                        pe.sem_inc(S(nm), 2)

            def combine(L):
                for i, t in enumerate(out_tiles(L)):
                    pe.wait_ge(S("comb"), OT0[L] + i + 1)
                    if i >= 2:
                        pe.wait_ge(S("hup"), OT0[L] + i - 1)
                    for c in range(DC):
                        last = pe.transpose(PS[:, 2 * (i % 2) + c // 4, (c % 4) * P:(c % 4 + 1) * P],
                                            r12(i, 0)[:, c * P:(c + 1) * P], ident)
                    last.then_inc(S("comb_ps"), 1)

            for L in range(LAYERS):
                norm_sums(L, 0)
                in_proj(L)
                mla_prep(L)
                key_transposes(L)
                attention(L)
                out_proj(L)
                norm_sums(L, 1)
                route_and_rows(L)
                experts(L)
                combine(L)
            pe.wait_ge(S("h_final"), LAYERS)
            for i, t in enumerate(out_tiles(1)):
                if i >= 2:
                    pe.wait_ge(S("res_a"), i - 1)
                    pe.wait_ge(S("res_d"), i - 1)
                for c in range(DC):
                    last = pe.transpose(PS[:, 2 * (i % 2) + c // 4, (c % 4) * P:(c % 4 + 1) * P],
                                        hT[:, c, t * P:(t + 1) * P], ident)
                last.then_inc(S("res_ps"), 1)

        @block.scalar
        def _(act):
            for t in range(NT):
                act.wait_ge(S("x_ps"), t + 1)
                act.activation(hT[:, 0:4, t * P:(t + 1) * P], PS[:, 2 * (t % 2), :].rearrange("p (c n) -> p c n", c=4),
                               ACT.Copy).then_inc(S("x_ev_a"), 1)
            act.wait_ge(S("cc_in"), 32)
            act.activation(cc[:, :], cc[:, :], ACT.Silu).then_inc(S("cc_silu"), 1)

            def norm(L, w):
                lo = 0 if w == 0 else tok_lo(L)
                base = (2 * L + w) * DC
                if w == 1:
                    act.wait_ge(S("h_mid"), L + 1)
                elif L:
                    act.wait_ge(S("h_final"), L)
                else:
                    act.wait_ge(S("x_ev_d"), NT)
                    act.wait_ge(S("x_ev_a"), NT)
                for c in range(DC):
                    if base + c >= 2:
                        act.wait_ge(S("sq_used"), base + c - 1)
                    act.activation(sq2[:, c % 2, lo:N], hT[:, c, lo:N], ACT.Square).then_inc(S("sq_done"), 1)
                act.wait_ge(S("var_done"), 2 * L + w + 1)
                act.activation(rs[:, lo:N], rs[:, lo:N], ACT.Sqrt).then_inc(S("sqrt_done"), 1)
                act.wait_ge(S("acol_ready"), 1)
                for c in range(DC):
                    act.wait_ge(S("nrm_x"), base + c + 1)
                    for s, a, b in streams(lo, N):
                        last = act.activation(aT[:, c, a:b], aT[:, c, a:b], ACT.Identity,
                                              scale=acol4[:, L, w, c, s:s + 1], bias=mod4[:, L, 24 * w + c, s:s + 1])
                last.then_inc(S("fT_ready" if w else "aT_ready"), 1)

            def in_proj(L):
                act.wait_ge(S("pads_ready"), L + 1)
                for m in range(XM + 1):
                    if m < XM:
                        act.wait_ge(S("xp_ps"), XM * L + m + 1)
                        if m >= 2:
                            act.wait_ge(S("conv_done"), XM * L + m - 1)
                        b0 = 2 * (m % 2)
                        act.activation(raw[:, m % 2, 2:2 + CTX], PS[:, b0, 0:CTX], ACT.Copy)
                        act.activation(raw[:, m % 2, 6 + CTX:6 + 512], PS[:, b0, CTX:512], ACT.Copy)
                        act.activation(raw[:, m % 2, 6 + 512:6 + N], PS[:, b0 + 1, 0:N - 512], ACT.Copy
                                       ).then_inc(S("raw_ready"), 1)
                    if m:
                        act.wait_ge(S("conv_done"), XM * L + m)
                        act.activation(xbcT[:, m - 1, :], xbcT[:, m - 1, :], ACT.Silu).then_inc(S("xbc_ready"), 1)
                for k, (j, t) in enumerate(JOBS[L]):
                    act.wait_ge(S("pj_ps"), PJ0[L] + k + 1)
                    a, w = CH[j][1], CH[j][2]
                    act.activation(p[:, t, a:a + w], PS[:, 4 + k % 2, 0:w], ACT.Copy).then_inc(S("pj_ev"), 1)
                    if XB_AT <= k < XB_AT + 2:
                        for t2 in range(3 * (k - XB_AT), 3 * (k - XB_AT) + 3):
                            act.wait_ge(S("xb_ps"), NT * L + t2 + 1)
                            act.activation(xB[:, t2, :], PS[:, 6 + t2 % 2, :], ACT.Copy).then_inc(S("xb_ev"), 1)
                    if k == CUM_AT - 1:
                        step_sizes(L)
                    if k == CUM_AT:
                        act.wait_ge(S("cum_in"), L + 1)
                        act.activation(ssd[:, 5 * 48:6 * 48], ssd[:, 2 * 48:3 * 48], ACT.Exp)
                        act.activation(ssd[:, 4 * 48:5 * 48], ssd[:, 4 * 48:5 * 48], ACT.Exp)
                        act.activation(ssd[:, 6 * 48:7 * 48], ssd[:, 3 * 48:4 * 48], ACT.Exp).then_inc(S("cum_exp"), 1)
                    if SCAN_AT <= k < SCAN_AT + 2 * NT:
                        w = 2 * NT * L + k - SCAN_AT
                        if SU[w][2] in out_tiles(L):
                            act.wait_ge(S("front_done"), YU[w] + 1)
                            act.activation(Mall(w), Mall(w), ACT.Exp).then_inc(S("seg_exp"), 1)
                    if k + 1 < len(JOBS[L]) and JOBS[L][k + 1][0] == NCH - 1 and j != NCH - 1:
                        stats(L)

            def step_sizes(L):
                act.wait_ge(S("pj_ev"), PJ0[L] + NT)
                act.wait_ge(S("sp_in"), L + 1)
                act.activation(ssd[:, 8 * 48:9 * 48], ssd[:, 8 * 48:9 * 48], ACT.Exp).then_inc(S("sp_u"), 1)
                act.wait_ge(S("sp_w"), L + 1)
                act.activation(ssd[:, 48:96], ssd[:, 9 * 48:10 * 48], ACT.Ln)
                act.activation(sc[:, 8:16], row("ssd_a_log"), ACT.Exp).then_inc(S("sp_ln"), 1)
                act.activation(ar(scs, NT * 384).rearrange("p (t d) -> p t d", t=NT), p[:, :, PM:PM + 384], ACT.Square
                               ).then_inc(S("sq_stats"), 1)
                ss3 = ss[:, :].rearrange("p (t h) -> p t h", t=NT)
                act.wait_ge(S("var_s"), 2 * L + 1)
                act.activation(ss3[:, :, 24:26], ss3[:, :, 24:26], ACT.Sqrt).then_inc(S("sqrt_s"), 1)

            def stats(L):
                t0 = out_tiles(L)[0]
                nt = NT - t0
                act.wait_ge(S("scan_done"), L + 1)
                act.wait_ge(S("pj_ev"), PJ0[L] + 3 * NT + nt)
                for q, a in enumerate((PNK, PDK)):
                    act.activation(ar(sca + q * NT * 256, NT * 256).rearrange("p (t d) -> p t d", t=NT), p[:, :, a:a + 256], ACT.Square)
                act.activation(ar(sca + NT * 512, nt * 512).rearrange("p (t d) -> p t d", t=nt), p[:, t0:, PNQ:PNQ + 512], ACT.Square
                               ).then_inc(S("sq_stats"), 1)
                ss3 = ss[:, :].rearrange("p (t h) -> p t h", t=NT)
                act.wait_ge(S("var_s"), 2 * L + 2)
                act.activation(ss3[:, :, 0:24], ss3[:, :, 0:24], ACT.Sqrt).then_inc(S("sqrt_s"), 1)

            def mla_prep(L):
                for t in range(NT):
                    act.wait_ge(S("cT_ps"), NT * L + t + 1)
                    act.activation(cT[:, :, t * P:(t + 1) * P], PS[:, t % 2, 0:384].rearrange("p (c n) -> p c n", c=3),
                                   ACT.Copy).then_inc(S("cT_ev"), 1)
                for t in range(NT):
                    act.wait_ge(S("mla_ps"), NT * L + t + 1)
                    act.activation(ot[:, t, 256:640], PS[:, 2 + t % 2, 0:384], ACT.Copy).then_inc(S("mq_ev"), 1)
                act.wait_ge(S("mq_ev"), NT * (L + 1))
                act.wait_ge(S("mkv_ev"), NT * (L + 1))
                act.activation(ar(scr, NT * 768).rearrange("p (t d) -> p t d", t=NT), ot[:, :, 256:1024], ACT.Square
                               ).then_inc(S("sq_m"), 1)
                act.wait_ge(S("var_m"), L + 1)
                act.activation(ss2[:, :], ss2[:, :], ACT.Sqrt).then_inc(S("sqrt_m"), 1)
                for n in range(2 * NT):
                    kind, t = n // NT, n % NT
                    act.wait_ge(S("kt_ps"), 2 * NT * L + n + 1)
                    src = PS[:, 6 + n % 2, :].rearrange("p (q n) -> p q n", q=4)
                    if kind == 0:
                        act.activation(kTn[:, :, t * P:(t + 1) * P], src, ACT.Copy).then_inc(S("kt_ev"), 1)
                    else:
                        act.activation(kTm[0:MLA_D, :, t * P:(t + 1) * P], src[0:MLA_D], ACT.Copy).then_inc(S("kt_ev"), 1)

            def attention(L):
                n, u0 = len(UN[L]), U0[L]
                act.wait_ge(S("lam_in"), L + 1)
                act.activation(sc[:, 0:2], sc[:, 0:2], ACT.Exp).then_inc(S("lam_exp"), 1)

                def q_evac(j):
                    act.wait_ge(S("qT_ps"), j + 1)
                    r = MLA_D if jobs[j][1] == "mla" else P
                    act.activation(qT[0:r, j % 2], PS[0:r, 7, 0:P], ACT.Copy).then_inc(S("qT_ev"), 1)

                for i in range(n + 1):
                    if i < n:
                        u = u0 + i
                        t = ALLU[u][2]
                        if i == 0:
                            q_evac(JOB[u])
                        if i + 1 < n and JOB[u + 1] != JOB[u]:
                            q_evac(JOB[u + 1])
                        act.wait_ge(S("nm_done"), u + 1)
                        if u >= 2:
                            act.wait_ge(S("t_ps"), u - 1)
                            if u >= 4:
                                act.wait_ge(S("o_ev"), u - 3)
                        w = N if t >= CT else CTX
                        act.activation(Pb[:, u % 2, 0:w], PS[:, 2 * (u % 2):2 * (u % 2) + 2, :].rearrange("p b n -> p (b n)")[:, 0:w],
                                       ACT.Exp, bias=att[:, 4 + u % 4:5 + u % 4],
                                       accum_out=att[:, 8 + u % 4:9 + u % 4]).then_inc(S("exp_done"), 1)
                    if i >= 1:
                        u = u0 + i - 1
                        t = ALLU[u][2]
                        act.wait_ge(S("t_ps"), u + 1)
                        if u >= 2:
                            act.wait_ge(S("o_ps"), u - 1)
                        w = 512 if t >= CT else CTX
                        act.activation(PTb[:, u % 2, 0:w], PS[:, 4, 0:w], ACT.Copy).then_inc(S("pt_ev_a"), 1)

            def finish(L):
                zt = p[:, out_tiles(L)[0]:, PZ:PZ + GW]
                act.activation(zt, zt, ACT.Silu).then_inc(S("z_silu"), 1)
                act.wait_ge(S("fin_in"), L + 1)
                act.activation(ar(scr, 2 * NT * GW).rearrange("p (t d) -> p t d", t=NT), ot[:, :, 512:1024], ACT.Square
                               ).then_inc(S("fin_sq"), 1)
                act.wait_ge(S("var_f"), L + 1)
                act.activation(ss[:, 0:30], ss[:, 0:30], ACT.Sqrt).then_inc(S("sqrt_f"), 1)

            def out_proj(L):
                for i, t in enumerate(out_tiles(L)):
                    act.wait_ge(S("oT_ps"), OT0[L] + i + 1)
                    act.activation(oT[:, 0:4, t * P:(t + 1) * P], PS[:, 2 * (i % 2), :].rearrange("p (c n) -> p c n", c=4),
                                   ACT.Copy).then_inc(S("oT_a"), 1)

            def rows_and_route(L):
                def f_evac():
                    for i, t in enumerate(out_tiles(L)):
                        act.wait_ge(S("ftok_ps"), OT0[L] + i + 1)
                        if cnt2(L, i):
                            act.wait_ge(S(f"f_out{i % 2}"), 16 * cnt2(L, i))
                        act.activation(ftok[:, i % 2, 0:512], PS[:, 2 * (i % 2), :], ACT.Copy).then_inc(S("ftok_a"), 1)
                f_evac()
                act.wait_ge(S("rt_g"), L + 1)
                act.activation(r_(120, 24), r_(120, 24), ACT.Exp).then_inc(S("rt_ge"), 1)
                act.wait_ge(S("rt_m"), L + 1)
                act.activation(r6(4), r6(4), ACT.Exp).then_inc(S("rt_me"), 1)

            def experts(L):
                n0 = NB0[L]
                fl = L == 0

                def x_evac(i, par):
                    b = 2 * i + par
                    act.wait_ge(S("xt_ps"), n0 + b + 1)
                    act.activation(xT(par)[:, 0:512], PS[:, 0, :], ACT.Copy).then_inc(S("xT_a"), 1)

                def gate(i, par):
                    b = 2 * i + par
                    act.wait_ge(S("gu_ps"), n0 + b + 1)
                    act.activation(hid(par), PS[:, 2, :], ACT.Silu).then_inc(S("silu_done"), 1)

                def y_store(i, par, first=False):
                    b = 2 * i + par
                    act.wait_ge(S("dn_ps"), n0 + b + 1)
                    if not first:
                        act.wait_ge(S(f"y_out{par}"), 16 * (n0 // 2) + 16 * i)
                    act.activation(ysb(par)[:, 0:512], PS[:, 5, :], ACT.Copy).then_inc(S("y_a"), 1)
                    act.wait_ge(S("y_a"), n0 + b + 1)
                    act.wait_ge(S("y_d"), n0 + b + 1)
                    act.dma_start(dram["y_rows"].rearrange("(b p) n -> b p n", p=P)[bass.ds(b, 1)].rearrange("b p n -> p (b n)"),
                                  ysb(par)).then_inc(S(f"y_out{par}"), 16)

                lastp = last_pair(act, L)
                x_evac(0, 0)
                gate(0, 0)
                x_evac(0, 1)
                y_store(0, 0, fl)
                gate(0, 1)
                x_evac(1, 0)
                y_store(0, 1, fl)
                with act.Fori(1, lastp) as i:
                    gate(i, 0)
                    x_evac(i, 1)
                    y_store(i, 0)
                    gate(i, 1)
                    x_evac(i + 1, 0)
                    y_store(i, 1)
                gate(lastp, 0)
                x_evac(lastp, 1)
                y_store(lastp, 0)
                gate(lastp, 1)
                y_store(lastp, 1)
                act.drain()
                for par in range(2):
                    act.wait_ge(S(f"y_out{par}"), 16 * lastp + 16 + 8 * n0)
                with act.Fori(lastp + 1, PAIRS[L] + 1):
                    for nm in ("xT_a", "silu_done", "y_a"):
                        act.sem_inc(S(nm), 2)
                    for par in range(2):
                        act.sem_inc(S(f"y_out{par}"), 16)

            for L in range(LAYERS):
                norm(L, 0)
                in_proj(L)
                mla_prep(L)
                attention(L)
                finish(L)
                out_proj(L)
                norm(L, 1)
                rows_and_route(L)
                experts(L)
            for i, t in enumerate(out_tiles(1)):
                act.wait_ge(S("res_ps"), i + 1)
                if i >= 2:
                    act.wait_ge(S(f"res_out{i % 2}"), 16 * (i // 2))
                act.activation(restok[:, i % 2, 0:512], PS[:, 2 * (i % 2), :], ACT.Copy).then_inc(S("res_a"), 1)

        @block.vector
        def _(dve):
            link = Chain(dve, S("dve_chain"))
            dve.wait_ge(S("consts_in"), 16)
            link(dve.tensor_copy(tokid[:, :], K[:, C_TOK:C_TOK + NT]))
            mul = ALU.mult
            for t in range(NT):
                dve.wait_ge(S("x_ps"), t + 1)
                dve.tensor_copy(hT[:, 4:8, t * P:(t + 1) * P],
                                PS[:, 2 * (t % 2) + 1, :].rearrange("p (c n) -> p c n", c=4)).then_inc(S("x_ev_d"), 1)
            dve.wait_ge(S("bmod_in"), 16)
            for i in range(len(mod_jobs)):
                dve.wait_ge(S("wmod_used"), i + 1)
                mr = modrow[0:2, i * 512:(i + 1) * 512]
                dve.tensor_tensor(mr, PS[0:2, 4 + i % 2, :], mr, ALU.add).then_inc(S("mod_ev"), 1)
            dve.wait_ge(S("modT_ps"), 1)
            link(dve.tensor_copy(modcol[:, :], PS[:, 6, 0:LAYERS * 96]))
            dve.wait_ge(S("cols_in"), 16 * LAYERS * (3 + XM))
            for l2 in range(LAYERS):
                for w in range(2):
                    g = gcol3[:, l2, w, :]
                    last = dve.scalar_tensor_tensor(out=acol4[:, l2, w], in0=mod4[:, l2, 24 * w + 8:24 * w + 16, :], scalar=1.0,
                                                    in1=bc(g, (1, DC), (0, 2)), op0=ALU.add, op1=mul)
            last.then_inc(S("acol_ready"), 1)

            def norm(L, w):
                lo = 0 if w == 0 else tok_lo(L)
                base = (2 * L + w) * DC
                dve.wait_ge(S("sq_used"), base + DC)
                for bk, (a, b) in enumerate(segs(lo)):
                    last = dve.tensor_scalar(rs[:, a:b], PS[:, bk, 0:b - a], 1.0 / D, EPS, mul, ALU.add)
                last.then_inc(S("var_done"), 1)
                if w == 0:
                    dve.memset(raw[:, :, 0:2], 0.0)
                    dve.memset(raw[:, :, 2 + CTX:6 + CTX], 0.0)
                    dve.memset(raw[:, :, RAWW - 2:RAWW], 0.0).then_inc(S("pads_ready"), 1)
                dve.wait_ge(S("sqrt_done"), 2 * L + w + 1)
                link(dve.reciprocal(rs[:, lo:N], rs[:, lo:N]))
                for c in range(DC):
                    dve.tensor_tensor(aT[:, c, lo:N], hT[:, c, lo:N], rs[:, lo:N], mul).then_inc(S("nrm_x"), 1)

            def conv(L):
                for m in range(XM):
                    dve.wait_ge(S("raw_ready"), XM * L + m + 1)
                    o = xbcT[:, m, :]
                    link(dve.tensor_scalar(o, raw[:, m % 2, 0:XW], cw[:, L, m, 0:1], cw[:, L, m, 5:6], mul, ALU.add))
                    for j in range(1, CONV):
                        ins = dve.scalar_tensor_tensor(out=o, in0=raw[:, m % 2, j:j + XW], scalar=cw[:, L, m, j:j + 1],
                                                       in1=o, op0=mul, op1=ALU.add)
                        if j < CONV - 1:
                            link(ins)
                    ins.then_inc(S("conv_done"), 1)

            ss3 = ss[:, :].rearrange("p (t h) -> p t h", t=NT)
            ss23 = ss2[:, :].rearrange("p (t h) -> p t h", t=NT)

            def heads(v, h):
                return v.rearrange("p t (h d) -> p t h d", h=h)

            def over(a3, d):
                return bc(a3, list(a3.ap[1]), list(a3.ap[2]), (0, d))

            def gain(name, t, h):
                g = row(name)
                return bc(g, (0, t), (0, h), (1, ROW_AT[name][1]))

            def rotate(v, tmp, nh):
                x1, x2 = v[:, :, :, 0:16], v[:, :, :, 16:32]
                cosb = bc(K[:, C_COS:C_COS + 1], (16, 4), (0, nh), (1, 16))
                sinb = bc(K[:, C_SIN:C_SIN + 1], (16, 4), (0, nh), (1, 16))
                n = 4 * nh * 16
                tm = [ar(tmp + q * n, n).rearrange("p (t h d) -> p t h d", t=4, h=nh) for q in range(4)]
                dve.tensor_tensor(tm[0], x1, cosb, mul)
                dve.tensor_tensor(tm[1], x2, sinb, mul)
                dve.tensor_tensor(tm[2], x1, sinb, mul)
                link(dve.tensor_tensor(tm[3], x2, cosb, mul))
                dve.tensor_tensor(x1, tm[0], tm[1], ALU.subtract)
                return dve.tensor_tensor(x2, tm[2], tm[3], ALU.add)

            def latent_stats(L):
                dve.wait_ge(S("sq_stats"), 2 * L + 1)
                m2 = ar(scs, NT * 384).rearrange("p (t d) -> p t d", t=NT)
                dve.tensor_reduce(ss3[:, :, 24], m2[:, :, 0:256], AX.X, ALU.add)
                link(dve.tensor_reduce(ss3[:, :, 25], m2[:, :, 256:384], AX.X, ALU.add))
                dve.tensor_scalar(ss3[:, :, 24:25], ss3[:, :, 24:25], 1.0 / 256, EPS, mul, ALU.add)
                dve.tensor_scalar(ss3[:, :, 25:26], ss3[:, :, 25:26], 1.0 / 128, EPS, mul, ALU.add).then_inc(S("var_s"), 1)
                dve.wait_ge(S("sqrt_s"), 2 * L + 1)
                link(dve.reciprocal(ss3[:, :, 24:26], ss3[:, :, 24:26]))
                cq, ckv = p[:, :, PM:PM + 256], p[:, :, PM + 256:PM + 384]
                dve.tensor_tensor(cq, cq, bc(ss3[:, :, 24], (26, NT), (0, 256)), mul)
                link(dve.tensor_tensor(ckv, ckv, bc(ss3[:, :, 25], (26, NT), (0, 128)), mul))
                dve.tensor_tensor(cq, cq, bc(row("mla_g_qa"), (0, NT), (1, 256)), mul)
                dve.tensor_tensor(ckv, ckv, bc(row("mla_g_kva"), (0, NT), (1, 128)), mul).then_inc(S("stats_done"), 1)

            def stats(L):
                t0 = out_tiles(L)[0]
                nt = NT - t0
                dve.wait_ge(S("sq_stats"), 2 * L + 2)

                def sq(off, tiles, width, h, a, n):
                    v = ar(sca + off, tiles * width).rearrange("p (t d) -> p t d", t=tiles)[:, :, a:a + n]
                    return heads(v, h)
                dve.tensor_reduce(ss3[:, :, 0:4], sq(0, NT, 256, 4, 0, 256), AX.X, ALU.add)
                dve.tensor_reduce(ss3[:, :, 8:16], sq(NT * 256, NT, 256, 8, 0, 256), AX.X, ALU.add)
                dve.tensor_reduce(ss3[:, t0:, 4:8], sq(NT * 512, nt, 512, 4, 0, 256), AX.X, ALU.add)
                link(dve.tensor_reduce(ss3[:, t0:, 16:24], sq(NT * 512, nt, 512, 8, 256, 256), AX.X, ALU.add))
                dve.tensor_scalar(ss3[:, :, 0:8], ss3[:, :, 0:8], 1.0 / HD, EPS, mul, ALU.add)
                dve.tensor_scalar(ss3[:, :, 8:24], ss3[:, :, 8:24], 1.0 / DQK, EPS, mul, ALU.add).then_inc(S("var_s"), 1)
                dve.wait_ge(S("sqrt_s"), 2 * L + 2)
                link(dve.reciprocal(ss3[:, :, 0:24], ss3[:, :, 0:24]))
                dve.tensor_scalar(ss3[:, :, 4:8], ss3[:, :, 4:8], HD ** -0.5, None, mul)
                dve.tensor_scalar(ss3[:, :, 16:24], ss3[:, :, 16:24], DQK ** -0.5, None, mul).then_inc(S("rstd_done"), 1)
                dve.wait_ge(S("rstd_done"), L + 1)
                vk, vq = heads(p[:, :, PDK:PDK + 256], 8), heads(p[:, t0:, PDQ:PDQ + 256], 8)
                dve.tensor_tensor(vk, vk, over(ss3[:, :, 8:16], DQK), mul)
                link(dve.tensor_tensor(vq, vq, over(ss3[:, t0:, 16:24], DQK), mul))
                dve.tensor_tensor(vk, vk, gain("diff_g_k", NT, 8), mul)
                link(dve.tensor_tensor(vq, vq, gain("diff_g_q", nt, 8), mul))
                link(rotate(vk[:, CT:], A_F + F_XB, 8))
                rotate(vq[:, CT - t0:], A_F + F_XB, 8).then_inc(S("dif_norm"), 1)

            def mla_prep(L):
                for t in range(NT):
                    dve.wait_ge(S("mla_ps"), NT * L + t + 1)
                    kv = PS[:, 4 + t % 2, :].rearrange("p (h d) -> p h d", h=HEADS)
                    mk = ot[:, t, 640:1024].rearrange("p (h d) -> p h d", h=HEADS)
                    dve.tensor_copy(mk[:, :, 0:HD], kv[:, :, 0:HD])
                    dve.tensor_copy(p[:, t, PM:PM + 256].rearrange("p (h d) -> p h d", h=HEADS), kv[:, :, HD:2 * HD])
                    dve.tensor_copy(mk[:, :, HD:MLA_D], bc(p[:, t, PM + 384:PM + 385], (0, HEADS), (1, 32))
                                    ).then_inc(S("mkv_ev"), 1)
                dve.wait_ge(S("sq_m"), L + 1)
                link(dve.tensor_reduce(ss23, ar(scr, NT * 768).rearrange("p (t h d) -> p t h d", t=NT, h=8), AX.X, ALU.add))
                dve.tensor_scalar(ss2[:, :], ss2[:, :], 1.0 / MLA_D, EPS, mul, ALU.add).then_inc(S("var_m"), 1)
                dve.wait_ge(S("sqrt_m"), L + 1)
                link(dve.reciprocal(ss2[:, :], ss2[:, :]))
                link(dve.tensor_scalar(ss23[:, :, 0:4], ss23[:, :, 0:4], MLA_D ** -0.5, None, mul))
                v = heads(ot[:, :, 256:1024], 8)
                link(dve.tensor_tensor(v, v, over(ss23, MLA_D), mul))
                dve.tensor_tensor(v[:, :, 0:4], v[:, :, 0:4], gain("mla_g_q", NT, 4), mul)
                link(dve.tensor_tensor(v[:, :, 4:8], v[:, :, 4:8], gain("mla_g_k", NT, 4), mul))
                rotate(v[:, CT:, :, HD:MLA_D], scr, 8).then_inc(S("m_norm"), 1)

            def attention(L):
                n, u0 = len(UN[L]), U0[L]
                lv = row("diff_lambda")
                lt = ssd[:, 0:64].rearrange("p (a d) -> p a d", a=2)
                link(dve.tensor_tensor(lt, bc(lv, (64, 2), (1, 32)), bc(row("diff_lambda", 32, 96), (64, 2), (1, 32)), mul))
                dve.tensor_reduce(sc[:, 0:2], lt, AX.X, ALU.add).then_inc(S("lam_in"), 1)
                dve.wait_ge(S("lam_exp"), L + 1)
                link(dve.tensor_tensor(sc[:, 2:3], sc[:, 1:2], sc[:, 0:1], ALU.subtract))
                link(dve.tensor_scalar(sc[:, 3:4], sc[:, 2:3], -LAM_INIT[L], None, ALU.add))

                for i in range(n + 2):
                    if i < n:
                        u = u0 + i
                        w = N if ALLU[u][2] >= CT else CTX
                        dve.wait_ge(S("s_ps"), u + 1)
                        link(dve.tensor_reduce(att[:, u % 4:u % 4 + 1],
                                               PS[:, 2 * (u % 2):2 * (u % 2) + 2, :].rearrange("p b n -> p (b n)")[:, 0:w],
                                               AX.X, ALU.max))
                        dve.tensor_scalar(att[:, 4 + u % 4:5 + u % 4], att[:, u % 4:u % 4 + 1], -1.0, None, mul
                                          ).then_inc(S("nm_done"), 1)
                    if 1 <= i <= n:
                        u = u0 + i - 1
                        if ALLU[u][2] >= CT:
                            dve.wait_ge(S("t_ps"), u + 1)
                            if u >= 2:
                                dve.wait_ge(S("o_ps"), u - 1)
                            dve.tensor_copy(PTb[:, u % 2, 512:N], PS[:, 5, 0:N - 512]).then_inc(S("pt_ev_d"), 1)
                    if i >= 2:
                        u = u0 + i - 2
                        g, h, t = ALLU[u]
                        dve.wait_ge(S("o_ps"), u + 1)
                        link(dve.reciprocal(att[:, 12:13], att[:, 8 + u % 4:9 + u % 4]))
                        o = PS[:, 6, 0:HD]
                        c0 = {"mla": HD * h, "na": 256 + HD * h, "dif": 512 + HD * (h // 2)}[g]
                        dst = ot[:, t, c0:c0 + HD]
                        if g == "dif" and h % 2:
                            link(dve.tensor_tensor(att[:, 13:14], att[:, 12:13], sc[:, 3:4], mul))
                            dve.scalar_tensor_tensor(out=dst, in0=o, scalar=att[:, 13:14], in1=dst, op0=mul, op1=ALU.add
                                                     ).then_inc(S("o_ev"), 1)
                        else:
                            dve.tensor_scalar(dst, o, att[:, 12:13], None, mul).then_inc(S("o_ev"), 1)
                        dve.wait_ge(S("o_ev"), u + 1)

            def scan(L):
                la, dt, cum, tot, toend, ecum, etot, x_, u_, w_ = [ssd[:, k * 48:(k + 1) * 48] for k in range(10)]
                la3, dt3, cum3, tot3, toend3, ecum3, etot3 = [sv(k) for k in range(7)]
                ul = out_tiles(L)
                dve.wait_ge(S("rows_in"), 16 * len(ROWS) * (L + 1))
                dve.wait_ge(S("pj_ev"), PJ0[L] + NT)
                link(dve.tensor_tensor(sv(7), p[:, :, PDT:PDT + 8], bc(row("ssd_dt_bias"), (0, NT), (1, 8)), ALU.add))
                link(dve.tensor_scalar(u_, x_, -1.0, None, mul))
                dve.tensor_tensor(u_, u_, x_, ALU.min).then_inc(S("sp_in"), 1)
                dve.wait_ge(S("sp_u"), L + 1)
                dve.tensor_scalar(w_, u_, 1.0, None, ALU.add).then_inc(S("sp_w"), 1)
                dve.wait_ge(S("sp_ln"), L + 1)
                link(dve.tensor_scalar(cum, w_, -1.0, 1e-7, ALU.add, ALU.max))
                link(dve.reciprocal(cum, cum))
                link(dve.tensor_tensor(cum, cum, u_, mul))
                link(dve.tensor_tensor(dt, dt, cum, mul))
                link(dve.tensor_scalar(w_, w_, 1.0, None, ALU.is_equal))
                link(dve.tensor_tensor(w_, w_, u_, mul))
                link(dve.tensor_tensor(dt, dt, w_, ALU.max))
                link(dve.tensor_scalar(x_, x_, 0.0, None, ALU.max))
                link(dve.tensor_tensor(dt, dt, x_, ALU.add))
                link(dve.tensor_tensor(la3, dt3, bc(sc[:, 8:16], (0, NT), (1, 8)), mul))
                dve.tensor_scalar(la, la, -1.0, None, mul).then_inc(S("la_done"), 1)
                if L == 0:
                    dve.wait_ge(S("y_zero"), 32)
                for dd in range(2):
                    last = dve.memset(state(dd), 0.0)
                link(last)
                latent_stats(L)
                dve.wait_ge(S("cum_ps"), L + 1)
                pc = PS[:, 7, 0:96]
                for dd in range(2):
                    dve.tensor_copy(cum3[:, :, 4 * dd:4 * dd + 4], pc[:, 24 * dd:24 * dd + 24].rearrange("p (t h) -> p t h", t=NT))
                link(dve.tensor_copy(tot, pc[:, 48:96]))
                dve.tensor_tensor(toend, tot, cum, ALU.subtract).then_inc(S("cum_in"), 1)
                dve.wait_ge(S("cum_exp"), L + 1)
                dve.tensor_copy(w_, cum).then_inc(S("cum_done"), 1)
                dve.wait_ge(S("cum_done"), L + 1)

                def hp(v2):
                    return v2.rearrange("p (h d) -> p h d", h=HEADS)

                def front(w):
                    _, dd, t = SU[w]
                    if t in ul:
                        dve.wait_ge(S("rg_ps"), YU[w] + 1)
                        yp = YU[w] % 2
                        tri = triU if dd == 0 else triL
                        if YU[w] >= 2:
                            dve.wait_ge(S("y_ps"), YU[w] - 1)
                        dve.tensor_tensor(GMb(w).rearrange("p (g n) -> p g n", g=2), PS[:, 2, 0:256].rearrange("p (g n) -> p g n", g=2),
                                          bc(tri, (0, 2), (1, P)), mul)
                        for h in range(HEADS):
                            last = dve.tensor_scalar(Mb(w, h), PS[:, yp, h * P:(h + 1) * P],
                                                     cum3[:, t, 4 * dd + h:4 * dd + h + 1], 0.0, ALU.subtract, ALU.min)
                        last.then_inc(S("front_done"), 1)
                    if w >= 2:
                        dve.wait_ge(S("st_ps"), w - 1)
                    link(dve.tensor_tensor(hp(xdt(w)), hp(xB[:, t, 0:256]), bc(dt3[:, t, 4 * dd:4 * dd + 4], (1, 4), (0, HD)), mul))
                    dve.tensor_tensor(hp(xdte(w)), hp(xdt(w)), bc(toend3[:, t, 4 * dd:4 * dd + 4], (1, 4), (0, HD)), mul
                                      ).then_inc(S("xdt_done"), 1)
                    if t in ul:
                        dve.wait_ge(S("seg_exp"), YU[w] + 1)
                        dve.wait_ge(S("xdt_done"), w + 1)
                        m4 = Mall(w).rearrange("p (g h n) -> p g h n", g=2, h=2)
                        dve.tensor_tensor(m4, m4, bc(GMb(w), (P, 2), (0, 2), (1, P)), mul).then_inc(S("m_done"), 1)

                def back(w):
                    _, dd, t = SU[w]
                    if t in ul:
                        dve.wait_ge(S("y_ps"), YU[w] + 1)
                        yp = YU[w] % 2
                        link(dve.tensor_tensor(hp(ytmp), hp(PS[:, 3, 256:512]), bc(ecum3[:, t, 4 * dd:4 * dd + 4], (1, 4), (0, HD)), mul))
                        acc = yacc[:, t]
                        if (L, 1 - dd, t) in SU[2 * NT * L:w]:
                            link(dve.tensor_tensor(acc, acc, ytmp, ALU.add))
                            dve.tensor_tensor(acc, PS[:, 3, 0:256], acc, ALU.add).then_inc(S("y_done"), 1)
                        else:
                            dve.tensor_tensor(acc, PS[:, 3, 0:256], ytmp, ALU.add).then_inc(S("y_done"), 1)
                        dve.wait_ge(S("y_done"), YU[w] + 1)
                    dve.wait_ge(S("st_ps"), w + 1)
                    link(dve.tensor_tensor(hp(state(dd)), hp(state(dd)), bc(etot3[:, t, 4 * dd:4 * dd + 4], (1, 4), (0, HD)), mul))
                    dve.tensor_tensor(state(dd), PS[:, 6, 0:256], state(dd), ALU.add).then_inc(S("state_done"), 1)
                    dve.wait_ge(S("state_done"), w + 1)

                w0 = 2 * NT * L
                for i in range(2 * NT + 1):
                    if i < 2 * NT:
                        front(w0 + i)
                    if i:
                        back(w0 + i - 1)
                t0 = ul[0]
                nt = NT - t0
                y = yacc[:, t0:]
                link(dve.tensor_tensor(sc[:, 16:20], row("ssd_d", 0, 4), row("ssd_d", 4, 4), ALU.add))
                xs = xB[:, t0:, 0:256]
                tmp = ar(sca, nt * 256)
                link(dve.tensor_tensor(tmp.rearrange("p (t h d) -> p t h d", t=nt, h=4), heads(xs, 4),
                                       bc(sc[:, 16:20], (0, nt), (1, 4), (0, HD)), mul))
                tmp3 = tmp.rearrange("p (t d) -> p t d", t=nt)
                dve.tensor_tensor(y, y, tmp3, ALU.add).then_inc(S("scan_done"), 1)

            def finish(L):
                t0 = out_tiles(L)[0]
                dve.wait_ge(S("z_silu"), L + 1)
                if t0:
                    dve.memset(ot[:, 0:t0, 512:1024], 0.0)
                dve.tensor_tensor(ot[:, t0:, 768:1024], yacc[:, t0:], p[:, t0:, PZ:PZ + GW], mul).then_inc(S("fin_in"), 1)
                dve.wait_ge(S("fin_sq"), L + 1)
                sq = ar(scr, 2 * NT * GW).rearrange("p (t d) -> p t d", t=NT)
                f3 = ss[:, 0:30].rearrange("p (t h) -> p t h", t=NT)
                dve.tensor_reduce(f3[:, :, 0:4], heads(sq[:, :, 0:256], 4), AX.X, ALU.add)
                link(dve.tensor_reduce(f3[:, :, 4], sq[:, :, 256:512], AX.X, ALU.add))
                dve.tensor_scalar(f3[:, :, 0:4], f3[:, :, 0:4], 1.0 / HD, EPS, mul, ALU.add)
                dve.tensor_scalar(f3[:, :, 4:5], f3[:, :, 4:5], 1.0 / GW, EPS, mul, ALU.add).then_inc(S("var_f"), 1)
                dve.wait_ge(S("sqrt_f"), L + 1)
                link(dve.reciprocal(ss[:, 0:30], ss[:, 0:30]))
                link(dve.tensor_scalar(f3[:, :, 0:4], f3[:, :, 0:4], 1.0 - LAM_INIT[L], None, mul))
                vd = heads(ot[:, :, 512:768], 4)
                dve.tensor_tensor(vd, vd, over(f3[:, :, 0:4], HD), mul)
                link(dve.tensor_tensor(ot[:, :, 768:1024], ot[:, :, 768:1024], bc(f3[:, :, 4], (5, NT), (0, 256)), mul))
                dve.tensor_tensor(vd, vd, gain("diff_g_sub", NT, 4), mul)
                dve.tensor_tensor(ot[:, :, 768:1024], ot[:, :, 768:1024], bc(row("ssd_g_norm"), (0, NT), (1, 256)), mul
                                  ).then_inc(S("mix_done"), 1)

            def out_proj(L):
                for i, t in enumerate(out_tiles(L)):
                    dve.wait_ge(S("oT_ps"), OT0[L] + i + 1)
                    dve.tensor_copy(oT[:, 4:8, t * P:(t + 1) * P],
                                    PS[:, 2 * (i % 2) + 1, :].rearrange("p (c n) -> p c n", c=4)).then_inc(S("oT_d"), 1)
                for m in range(DC):
                    dve.wait_ge(S("op_ps"), DC * L + m + 1)
                    parts = []
                    for bk, (a, b) in enumerate(segs(tok_lo(L))):
                        parts += [(bk, a, max(a, a2), min(b, b2), s) for s, a2, b2 in streams(tok_lo(L), N) if max(a, a2) < min(b, b2)]
                    for q, (bk, a, c0, c1, s) in enumerate(parts):
                        last = dve.scalar_tensor_tensor(out=hT[:, m, c0:c1], in0=PS[:, 4 + 2 * (m % 2) + bk, c0 - a:c1 - a],
                                                        scalar=mod4[:, L, 16 + m, s:s + 1], in1=hT[:, m, c0:c1], op0=mul, op1=ALU.add)
                    last.then_inc(S("op_ev"), 1)
                dve.wait_ge(S("op_ev"), DC * (L + 1))
                dve.memset(sc[:, 20:21], 0.0).then_inc(S("h_mid"), 1)

            def route(L):
                tl = out_tiles(L)
                t0, T = tl[0], len(tl)
                for i, t in enumerate(tl):
                    dve.wait_ge(S("ftok_ps"), OT0[L] + i + 1)
                    if cnt2(L, i):
                        dve.wait_ge(S(f"f_out{i % 2}"), 16 * cnt2(L, i))
                    dve.tensor_copy(ftok[:, i % 2, 512:], PS[:, 2 * (i % 2) + 1, :]).then_inc(S("ftok_d"), 1)
                dve.wait_ge(S("lg_ps"), L + 1)
                lg = r_lg[:, t0:]
                link(dve.tensor_tensor(lg, PS[:, 4, t0 * 20:NT * 20].rearrange("p (t n) -> p t n", t=T),
                                       bc(row("moe_b_group"), (0, T), (1, 20)), ALU.add))
                g4 = lg[:, :, 0:4]

                def v24(off):
                    return r_(off, 24).rearrange("p (t g) -> p t g", t=NT)[:, t0:]

                def v96(off):
                    return r_(off, 96).rearrange("p (t e) -> p t e", t=NT)[:, t0:]

                def s6(k):
                    return r6(k)[:, t0:]

                def first_max(v, w, mx, tmp, oh):
                    link(dve.tensor_reduce(mx, v, AX.X, ALU.max))
                    link(dve.tensor_tensor(tmp, v, bc(mx, (1, T), (0, w)), ALU.is_equal))
                    link(dve.tensor_tensor(tmp, tmp, bc(K[:, C_DEC:C_DEC + 1], (0, T), (1, w)), mul))
                    link(dve.tensor_reduce(s6(9), tmp, AX.X, ALU.max))
                    link(dve.tensor_tensor(oh, tmp, bc(s6(9), (1, T), (0, w)), ALU.is_equal))

                ohg = v24(144)
                first_max(g4, 4, s6(0), v24(120), ohg)
                if t0:
                    link(dve.memset(r_(120, 24), 0.0))
                    link(dve.memset(r6(4), 0.0))
                dve.tensor_tensor(v24(120), g4, bc(s6(0), (1, T), (0, 4)), ALU.subtract).then_inc(S("rt_g"), 1)
                dve.wait_ge(S("rt_ge"), L + 1)
                link(dve.tensor_reduce(s6(1), v24(120), AX.X, ALU.add))
                link(dve.reciprocal(s6(1), s6(1)))
                em = v96(228)
                em4 = em.rearrange("p t (g e) -> p t g e", g=GROUPS)
                ohg4 = bc(ohg, (4, T), (1, 4), (0, EPG))
                link(dve.tensor_tensor(em4, lg[:, :, 4:20].rearrange("p t (g e) -> p t g e", g=GROUPS), ohg4, mul))
                link(dve.tensor_scalar(v24(120), ohg, -1.0, BIG, ALU.add, mul))
                link(dve.tensor_tensor(em4, em4, bc(v24(120), (4, T), (1, 4), (0, EPG)), ALU.add))
                first_max(em, EXP, s6(2), v96(324), r_oh[0][:, t0:])
                link(dve.scalar_tensor_tensor(out=em, in0=r_oh[0][:, t0:], scalar=-3 * BIG, in1=em, op0=mul, op1=ALU.add))
                first_max(em, EXP, s6(3), v96(324), r_oh[1][:, t0:])
                dve.tensor_tensor(r_sel[:, t0:], r_oh[0][:, t0:], r_oh[1][:, t0:], ALU.add).then_inc(S("sel_done"), 1)
                dve.tensor_tensor(s6(4), s6(3), s6(2), ALU.subtract).then_inc(S("rt_m"), 1)
                dve.wait_ge(S("rt_me"), L + 1)
                link(dve.tensor_scalar(s6(5), s6(4), 1.0, None, ALU.add))
                link(dve.reciprocal(s6(5), s6(5)))
                link(dve.tensor_tensor(wtok[:, t0:NT], s6(5), s6(1), mul))
                link(dve.tensor_tensor(wtok[:, NT + t0:2 * NT], wtok[:, t0:NT], s6(4), mul))
                dve.wait_ge(S("rank_ps"), L + 1)
                dm = v96(708)
                dve.tensor_copy(dm, PS[:, 5, t0 * EXP:NT * EXP].rearrange("p (t e) -> p t e", t=T))
                cnt, blocks, pex = r_(804, EXP), r_(820, EXP), r_(836, EXP)
                link(dve.tensor_copy(cnt, PS[:, 5, NT * EXP:(NT + 1) * EXP]))
                c6 = r_(852, EXP * NT).rearrange("p (e j) -> p e j", e=EXP)
                link(dve.tensor_tensor(c6, bc(cnt, (1, EXP), (0, NT)), bc(K[:, C_THR:C_THR + 1], (0, EXP), (1, NT)), ALU.is_gt))
                link(dve.tensor_reduce(blocks, c6, AX.X, ALU.add))
                t16 = r_(852, EXP * EXP).rearrange("p (e j) -> p e j", e=EXP)
                link(dve.tensor_tensor(t16, K[:, C_TRI:C_TRI + EXP * EXP].rearrange("p (e j) -> p e j", e=EXP),
                                       bc(blocks, (0, EXP), (1, EXP)), mul))
                link(dve.tensor_reduce(pex, t16, AX.X, ALU.add))
                link(dve.tensor_tensor(cnt, pex, blocks, ALU.add))
                cb = r_(1108, NBMAX * EXP).rearrange("p (b e) -> p b e", b=NBMAX)
                link(dve.tensor_tensor(cb, bc(K[:, C_BLK:C_BLK + 1], (1, NBMAX), (0, EXP)), bc(cnt, (0, NBMAX), (1, EXP)), ALU.is_ge))
                link(dve.tensor_reduce(r_(852, NBMAX), cb, AX.X, ALU.add))
                link(dve.tensor_scalar(blk_e[:, :], r_(852, NBMAX), float(EXP - 1), None, ALU.min))
                pj = r_(852, PAIRS[L])
                link(dve.tensor_scalar(pj, K[:, C_BLK:C_BLK + PAIRS[L]], 2.0, cnt[:, EXP - 1:EXP], mul, ALU.is_lt))
                link(dve.tensor_reduce(r_(900, 1), pj, AX.X, ALU.add))
                dve.tensor_scalar(npair[:, :], r_(900, 1), -1.0, None, ALU.add).then_inc(S("blk_ready"), 1)
                dve.wait_ge(S("blk_ready"), L + 1)
                link(dve.tensor_scalar(pex, pex, float(P), None, mul))
                link(dve.tensor_tensor(dm, dm, bc(pex, (0, T), (1, EXP)), ALU.add))
                for k in range(TOPK):
                    link(dve.tensor_tensor(v96(324), r_oh[k][:, t0:], dm, mul))
                    link(dve.tensor_reduce(s6(6 + k), v96(324), AX.X, ALU.add))
                    last = dve.tensor_copy(dest[:, k * NT + t0:(k + 1) * NT], s6(6 + k))
                last.then_inc(S("dest_ready"), 1)

            def experts(L):
                n0 = NB0[L]
                fl = L == 0

                def x_evac(i, par):
                    b = 2 * i + par
                    dve.wait_ge(S("xt_ps"), n0 + b + 1)
                    dve.tensor_copy(xT(par)[:, 512:], PS[:, 1, :]).then_inc(S("xT_d"), 1)

                def up(i, par):
                    b = 2 * i + par
                    dve.wait_ge(S("silu_done"), n0 + b + 1)
                    dve.tensor_tensor(hid(par), PS[:, 3, :], hid(par), mul).then_inc(S("h_done"), 1)

                def h_and_y(i, par, first=False):
                    b = 2 * i + par
                    dve.wait_ge(S("ht_ps"), n0 + b + 1)
                    dve.tensor_copy(hidT(par), PS[:, 4, :]).then_inc(S("hT_ev"), 1)
                    dve.wait_ge(S("dn_ps"), n0 + b + 1)
                    if not first:
                        dve.wait_ge(S(f"y_out{par}"), 16 * (n0 // 2) + 16 * i)
                    dve.tensor_copy(ysb(par)[:, 512:], PS[:, 6, :]).then_inc(S("y_d"), 1)

                lastp = last_pair(dve, L)
                x_evac(0, 0)
                up(0, 0)
                x_evac(0, 1)
                h_and_y(0, 0, fl)
                up(0, 1)
                x_evac(1, 0)
                h_and_y(0, 1, fl)
                with dve.Fori(1, lastp) as i:
                    up(i, 0)
                    x_evac(i, 1)
                    h_and_y(i, 0)
                    up(i, 1)
                    x_evac(i + 1, 0)
                    h_and_y(i, 1)
                up(lastp, 0)
                x_evac(lastp, 1)
                h_and_y(lastp, 0)
                up(lastp, 1)
                h_and_y(lastp, 1)
                dve.drain()
                with dve.Fori(lastp + 1, PAIRS[L] + 1):
                    for nm in ("xT_d", "h_done", "hT_ev", "y_d"):
                        dve.sem_inc(S(nm), 2)

            def combine(L):
                for i, t in enumerate(out_tiles(L)):
                    dve.wait_ge(S(f"g_in{i % 2}"), 32 * (cnt2(L, i) + 1))
                    a, b = r12(i, 0), r12(i, 1)
                    link(dve.tensor_scalar(a, a, wtok[:, t:t + 1], None, mul))
                    dve.scalar_tensor_tensor(out=a, in0=b, scalar=wtok[:, NT + t:NT + t + 1], in1=a, op0=mul, op1=ALU.add
                                             ).then_inc(S("comb"), 1)
                    dve.wait_ge(S("comb_ps"), OT0[L] + i + 1)
                    s = 1 if t < CT else 0
                    for c in range(DC):
                        v = hT[:, c, t * P:(t + 1) * P]
                        last = dve.scalar_tensor_tensor(out=v, in0=PS[:, 2 * (i % 2) + c // 4, (c % 4) * P:(c % 4 + 1) * P],
                                                        scalar=mod4[:, L, 40 + c, s:s + 1], in1=v, op0=mul, op1=ALU.add)
                    last.then_inc(S("hup"), 1)
                dve.wait_ge(S("hup"), OT0[L] + OTN[L])
                dve.memset(sc[:, 21:22], 0.0).then_inc(S("h_final"), 1)

            for L in range(LAYERS):
                norm(L, 0)
                conv(L)
                scan(L)
                stats(L)
                mla_prep(L)
                attention(L)
                finish(L)
                out_proj(L)
                norm(L, 1)
                route(L)
                experts(L)
                combine(L)
            for i, t in enumerate(out_tiles(1)):
                dve.wait_ge(S("res_ps"), i + 1)
                if i >= 2:
                    dve.wait_ge(S(f"res_out{i % 2}"), 16 * (i // 2))
                dve.tensor_copy(restok[:, i % 2, 512:], PS[:, 2 * (i % 2) + 1, :]).then_inc(S("res_d"), 1)

        @block.gpsimd
        def _(pool):
            pool.wait_ge(S("consts_in"), 16)
            pool.memset(zrows, 0.0).then_inc(S("zero_row"), 1)
            for L in range(LAYERS):
                pool.wait_ge(S("rstd_done"), L + 1)
                pool.wait_ge(S("rows_in"), 16 * len(ROWS) * (L + 1))
                ss3 = ss[:, :].rearrange("p (t h) -> p t h", t=NT)
                t0 = out_tiles(L)[0]
                vk = p[:, :, PNK:PNK + 256].rearrange("p t (h d) -> p t h d", h=HEADS)
                vq = p[:, t0:, PNQ:PNQ + 256].rearrange("p t (h d) -> p t h d", h=HEADS)
                pool.tensor_tensor(vk, vk, bc(ss3[:, :, 0:4], (26, NT), (1, 4), (0, HD)), ALU.mult)
                pool.tensor_tensor(vq, vq, bc(ss3[:, t0:, 4:8], (26, NT - t0), (1, 4), (0, HD)), ALU.mult).then_inc(S("na_r"), 1)
                pool.wait_ge(S("na_r"), L + 1)
                pool.tensor_tensor(vk, vk, bc(row("na_g_k"), (0, NT), (0, 4), (1, HD)), ALU.mult)
                pool.tensor_tensor(vq, vq, bc(row("na_g_q"), (0, NT - t0), (0, 4), (1, HD)), ALU.mult).then_inc(S("na_norm"), 1)
                pool.wait_ge(S("bias_in"), 16 * 2 * HEADS * (L + 1))
                bv = bias4[:, :, 1:, :]
                pool.tensor_tensor(bv, bv, bc(K[:, C_MASK:C_MASK + 1], (0, HEADS), (0, ROFF - 1), (1, GRID)), ALU.add
                                   ).then_inc(S("bias_ready"), 1)
                pool.memset(slots[:, :], N).then_inc(S("slots_fill"), 1)
                pool.wait_ge(S("dest_ready"), L + 1)
                pool.wait_ge(S("slots_init"), 16 * (L + 1))
                for t in out_tiles(L):
                    for k in range(TOPK):
                        pool.indirect_dma_start(
                            out=dram["slot_tok"], out_offset=bass.IndirectOffsetOnAxis(ap=dest[:, k * NT + t:k * NT + t + 1], axis=0),
                            in_=tokid[:, t:t + 1], in_offset=None).then_inc(S("slot_scat"), 16)
                pool.wait_ge(S("slots_in"), 16 * (L + 1))
                for q in range(2):
                    pool.wait_ge(S(f"f_out{q}"), 16 * (NT // 2 * L + OTN[L] // 2))
                pool.wait_ge(S("y_zero"), 32)
                n0 = NB0[L]

                def gather(i, par, first=False):
                    b = 2 * i + par
                    if not first:
                        pool.wait_ge(S("xt_ps"), n0 + b - 1)
                        pool.wait_ge(S(f"xg_in{L}{par}"), 16 * i)
                    pool.tensor_copy(slot1[:, par:par + 1], slots[:, bass.ds(b, 1)]).then_inc(S("slot1_done"), 1)
                    pool.wait_ge(S("slot1_done"), n0 + b + 1)
                    pool.nop(nofuse=True)
                    pool.indirect_dma_start(
                        out=xg(par), out_offset=None, in_=dram["f_rows"],
                        in_offset=bass.IndirectOffsetOnAxis(ap=slot1[:, par:par + 1], axis=0)).then_inc(S(f"xg_in{L}{par}"), 16)

                for par in range(2):
                    gather(0, par, True)
                lastp = last_pair(pool, L)
                with pool.Fori(1, lastp + 1) as i:
                    for par in range(2):
                        gather(i, par)
                pool.drain()
                with pool.Fori(lastp + 1, PAIRS[L] + 1):
                    pool.sem_inc(S("slot1_done"), 2)
                for q in range(2):
                    pool.wait_ge(S(f"y_out{q}"), 8 * (NB0[L] + NB[L] + 2))
                for i, t in enumerate(out_tiles(L)):
                    if i >= 2:
                        pool.wait_ge(S("hup"), OT0[L] + i - 1)
                    for k in range(TOPK):
                        pool.indirect_dma_start(
                            out=r12(i, k), out_offset=None, in_=dram["y_rows"],
                            in_offset=bass.IndirectOffsetOnAxis(ap=dest[:, k * NT + t:k * NT + t + 1], axis=0)
                        ).then_inc(S(f"g_in{i % 2}"), 16)


_INS = ["x", "c", "ctx", "c_ctx", "w_mod", "b_mod", "g_mix", "w_in", "w_out", "na_g_q", "na_g_k",
        "mla_g_qa", "mla_w_qb", "mla_g_kva", "mla_w_kvb", "mla_g_q", "mla_g_k", "diff_g_q", "diff_g_k", "diff_lambda",
        "diff_g_sub", "ssd_conv_w", "ssd_conv_b", "ssd_dt_bias", "ssd_a_log", "ssd_d", "ssd_g_norm", "g_ffn",
        "moe_w_group", "moe_b_group", "moe_w_expert", "moe_b_expert", "moe_w_gate", "moe_w_up", "moe_w_down"]


def kernel(**inputs):
    import numpy as _np
    import concourse.bacc as _bacc
    from concourse import mybir as _mybir
    from concourse.bass_utils import run_bass_kernel_spmd as _run

    nc = _bacc.Bacc("TRN2", target_bir_lowering=False, num_devices=1)
    arrays, io = {}, {}
    rel = _np.ascontiguousarray(inputs["na_rel_bias"]).reshape(LAYERS, -1)
    data = {k: _np.ascontiguousarray(inputs[k]) for k in _INS}
    data["rel_pad"] = _np.pad(rel, ((0, 0), (REL_PAD, REL_PAD)))
    data["consts"] = constants()
    for name, a in data.items():
        arrays[f"in_{name}"] = a
        io[name] = nc.dram_tensor(f"in_{name}", a.shape, _mybir.dt.from_np(a.dtype), kind="ExternalInput").ap()
    out = nc.dram_tensor("out", (1, SEQ, D), F32, kind="ExternalOutput").ap()
    build(nc, io, out)
    r = _run(nc, [arrays], core_ids=[0])
    return r.results[0]["out"]
```

```python
from contextlib import ExitStack
import math

import numpy as np
import concourse.bass as bass
from concourse import mybir

ALU = mybir.AluOpType
ACT = mybir.ActivationFunctionType
AX = mybir.AxisListType
F32 = mybir.dt.float32
I32 = mybir.dt.int32

P = 128
D = 1024
DC = D // P
LAYERS = 2
CTX = 256
SEQ = 512
N = CTX + SEQ
NT = N // P
CT = CTX // P
GRID = 64
NA_KH, NA_KW = 8, 16
ROFF = 2 * NA_KH - 1
COFF = 2 * NA_KW - 1
HEADS = 4
HD = 64
MLA_D = 96
DQK = 32
GW = 256
STATE = 128
CONV = 5
EPS = 1e-6
BIG = 1e30

NA0, MLA0, DIF0, Z0, XBC0, DT0, N_IN = 0, 768, 1184, 1952, 2208, 2976, 2984
PM, PDT, PNK, PNV, PDK, PDV, PNQ, PDQ, PZ, PW = 0, 416, 424, 680, 936, 1192, 1448, 1704, 1960, 2216
XBC = DT0 - XBC0
XM = XBC // P

REL_PAD = GRID
REL_W = HEADS * ROFF * COFF + 2 * REL_PAD

EXP, EPG, GROUPS, FF = 16, 4, 4, 512
FC = FF // P
TOPK = 2

C_ID, C_U, C_L, C_SU, C_ONE = 0, 128, 256, 384, 512
C_MASK = 640
C_COS = C_MASK + GRID
C_SIN = C_COS + 4 * 16
C_THR = C_SIN + 4 * 16
C_TRI = C_THR + NT
C_BLK = C_TRI + EXP * EXP
NBMAX = N * TOPK // P + EXP
C_DEC = C_BLK + NBMAX
C_TOK = C_DEC + EXP
C_IOTA = C_TOK + NT
C_SEL = C_IOTA + P
C_W = C_SEL + 2

ROWS = [("na_g_q", 64), ("na_g_k", 64), ("mla_g_qa", 256), ("mla_g_kva", 128), ("mla_g_q", 96),
        ("mla_g_k", 96), ("diff_g_q", 32), ("diff_g_k", 32), ("diff_g_sub", 64), ("ssd_g_norm", 256),
        ("ssd_dt_bias", 8), ("ssd_a_log", 8), ("ssd_d", 8), ("diff_lambda", 128),
        ("moe_b_group", 4), ("moe_b_expert", 16)]
ROW_AT = {}
_at = 0
for _name, _w in ROWS:
    ROW_AT[_name] = (_at, _w)
    _at += _w
ROWS_W = _at

A_B = 0
A_C = A_B + DC * N
A_D = A_C + NT * PW
XW = N + 4
A_RAW = A_D + XM * XW
RAWW = XW + 4
A_E = A_RAW + 2 * RAWW
E_W = 8192
A_F = A_E + E_W
F_XB, F_KM, F_KN = 0, 3072, 6144
ARENA = A_F + 9216
M_W = A_B + DC * N
M_WSET = 2 * DC * FF + FC * D
M_X = 0
M_Y = M_W + 2 * M_WSET


LAM_INIT = [0.8 - 0.6 * math.exp(-0.3 * layer) for layer in range(LAYERS)]


def constants():
    c = np.zeros((P, C_W), np.float32)
    i = np.arange(P)
    c[:, C_ID:C_ID + P] = np.eye(P)
    c[:, C_U:C_U + P] = i[:, None] <= i[None, :]
    c[:, C_L:C_L + P] = i[:, None] >= i[None, :]
    c[:, C_SU:C_SU + P] = i[:, None] < i[None, :]
    c[:, C_ONE:C_ONE + P] = 1.0
    q, k = np.arange(GRID)[:, None], np.arange(GRID)[None, :]
    lo = np.clip(q - NA_KW // 2, 0, GRID - NA_KW)
    m = np.where((k >= lo) & (k < lo + NA_KW), 0.0, -BIG)
    c[:, C_MASK:C_MASK + GRID] = np.concatenate([m, m])
    inv = np.power(np.float32(10000.0), -np.arange(8, dtype=np.float32) / np.float32(8)).astype(np.float32)
    t = np.arange(SEQ)
    ang = np.concatenate([(t // GRID).astype(np.float32)[:, None] * inv,
                          (t % GRID).astype(np.float32)[:, None] * inv], axis=-1)
    c[:, C_COS:C_COS + 64] = np.cos(ang).astype(np.float32).reshape(4, P, 16).transpose(1, 0, 2).reshape(P, 64)
    c[:, C_SIN:C_SIN + 64] = np.sin(ang).astype(np.float32).reshape(4, P, 16).transpose(1, 0, 2).reshape(P, 64)
    c[:, C_THR:C_THR + NT] = P * np.arange(NT)
    e = np.arange(EXP)
    c[:, C_TRI:C_TRI + EXP * EXP] = (e[None, :] < e[:, None]).astype(np.float32).reshape(-1)
    c[:, C_BLK:C_BLK + NBMAX] = np.arange(NBMAX)
    c[:, C_DEC:C_DEC + EXP] = EXP - e
    c[:, C_TOK:C_TOK + NT] = i[:, None] + P * np.arange(NT)[None, :] - N
    c[:, C_IOTA:C_IOTA + P] = i
    c[:, C_SEL:C_SEL + 2] = (i[:, None] % 32) == np.arange(2)[None, :]
    return c


def bc(ap, *free):
    return bass.AP(ap.tensor, ap.offset, [list(ap.ap[0])] + [list(x) for x in free])


class Chain:

    def __init__(self, eng, sem):
        self.eng, self.sem, self.n = eng, sem, 0

    def __call__(self, ins):
        self.n += 1
        ins.then_inc(self.sem, 1)
        self.eng.wait_ge(self.sem, self.n)


def build(nc, io, out):
    st = ExitStack()
    with st:
        sems = {}

        def S(name):
            if name not in sems:
                sems[name] = st.enter_context(nc.semaphore(name))
            return sems[name]

        def sb(name, w, dt=F32):
            return st.enter_context(nc.sbuf_tensor(name, [P, w], dt))

        hT_ = sb("hT", DC * N)
        X = sb("arena", ARENA)
        K = sb("consts", C_W)
        rows = sb("rows", ROWS_W)
        modcol = sb("modcol", LAYERS * 48 * 2)
        acol = sb("acol", LAYERS * 2 * DC * 2)
        gcol = sb("gcol", LAYERS * 2 * DC)
        convw = sb("convw", LAYERS * XM * 6)
        ss = sb("ss", NT * 26)
        ss2 = sb("ss2", NT * 8)
        sc = sb("sc", 32)
        cc = sb("cc", 16)
        ssd = sb("ssd", 10 * 48)
        att = sb("att_small", 56)
        wtok = sb("wtok", NT * TOPK)
        dest = sb("dest", NT * TOPK, I32)
        blk_e = sb("blk_e", NBMAX, I32)
        slots = sb("slots", NBMAX, I32)
        slot1 = sb("slot1", 2, I32)
        npair = sb("npair", 1, I32)

        PS = st.enter_context(nc.psum_tensor("ps", [P, 8, 512], F32))

        dram = {}
        for nm, shape, dt in (("f_rows", (N + 1, D), F32),
                              ("y_rows", (NBMAX * P, D), F32), ("rel_rows", (LAYERS * GRID, REL_W), F32)):
            dram[nm] = nc.dram_tensor(nm, shape, dt).ap()

        hT = hT_[:, :].rearrange("p (c n) -> p c n", c=DC)

        def ar(off, n):
            return X[:, off:off + n]

        aT = ar(A_B, DC * N).rearrange("p (c n) -> p c n", c=DC)
        ot = ar(A_B, NT * D).rearrange("p (t d) -> p t d", t=NT)
        p = ar(A_C, NT * PW).rearrange("p (t d) -> p t d", t=NT)
        oT = ar(A_C, DC * N).rearrange("p (c n) -> p c n", c=DC)
        xbcT = ar(A_D, XM * XW).rearrange("p (m n) -> p m n", m=XM)
        raw = ar(A_RAW, 2 * RAWW).rearrange("p (b n) -> p b n", b=2)
        sq2 = ar(A_RAW, 2 * N).rearrange("p (b n) -> p b n", b=2)
        wbuf = ar(A_E, E_W).rearrange("p (b k n) -> p b k n", b=2, k=DC)
        kTm = ar(A_F + F_KM, 4 * N).rearrange("p (h n) -> p h n", h=4)
        kTn = ar(A_F + F_KN, 4 * N).rearrange("p (h n) -> p h n", h=4)
        xB = ar(A_F + F_XB, NT * 512).rearrange("p (t d) -> p t d", t=NT)
        ident = K[:, C_ID:C_ID + P]
        triU = K[:, C_U:C_U + P]
        triL = K[:, C_L:C_L + P]
        strictU = K[:, C_SU:C_SU + P]
        ones = K[:, C_ONE:C_ONE + P]
        mod4 = modcol[:, :].rearrange("p (l j s) -> p l j s", l=LAYERS, s=2)
        acol4 = acol[:, :].rearrange("p (l w c s) -> p l w c s", l=LAYERS, w=2, s=2)
        gcol3 = gcol[:, :].rearrange("p (l w c) -> p l w c", l=LAYERS, w=2)
        cw = convw[:, :].rearrange("p (l m j) -> p l m j", l=LAYERS, j=6)

        def row(name, off=0, n=None):
            a, w = ROW_AT[name]
            return rows[:, a + off:a + off + (n or w)]

        def xcol(t):
            return t * P if t < CT else t * P + 4

        def out_tiles(L):
            return list(range(NT)) if L < LAYERS - 1 else list(range(CT, NT))

        def streams(lo, hi):
            r = []
            if lo < CTX:
                r.append((1, lo, CTX))
            r.append((0, max(lo, CTX), hi))
            return r

        def tok_lo(L):
            return 0 if L < LAYERS - 1 else CTX

        def segs(lo):
            return [(0, 512), (512, N)] if lo == 0 else [(CTX, N)]

        MODN = 6 * D // 512
        mod_jobs = [(L, n) for L in range(LAYERS) for n in range(MODN)]
        CH = [("x", 0, 4), ("x", 4, 2),
              ("t", PM, 424, [(0, MLA0, 416), (416, DT0, 8)], False),
              ("t", PNK, 512, [(0, NA0 + 256, 512)], False),
              ("t", PDK, 512, [(0, DIF0 + 256, 512)], False),
              ("t", PNQ, 512, [(0, NA0, 256), (256, DIF0, 256)], True),
              ("t", PZ, 256, [(0, Z0, 256)], True)]
        NCH = len(CH)
        TCH = [j for j in range(NCH) if CH[j][0] == "t"]
        JOBS = [[(j, t) for j in TCH for t in (out_tiles(L) if CH[j][4] else range(NT))] for L in range(LAYERS)]
        PJ0 = [0, len(JOBS[0]), len(JOBS[0]) + len(JOBS[1])]
        XB_AT, CUM_AT, SCAN_AT = 0, 6, 7

        QUAD = 4

        def at(k, w):
            return (k % 2) * 2 + k // 2 if w > 1 else 0

        def dif_quads(u):
            return sum(1 for g, _, _, w in ALLU[:u] if g == "dif" and w > 1)

        def units(L):
            groups = (("mla", 4), ("na", 4), ("dif", 8))
            return ([(g, h, t, QUAD) for t in out_tiles(L) if t < CT for g, nh in groups for h in range(0, nh, QUAD)]
                    + [(g, h, t, 1) for g, nh in groups for t in range(CT, NT) for h in range(nh)])

        UN = [units(L) for L in range(LAYERS)]
        U0 = [0, len(UN[0])]
        ALLU = UN[0] + UN[1]
        JOB = []
        jobs = []
        for _g, _h, _t, _w in ALLU:
            if _h % QUAD == 0:
                jobs.append((_g, _h, _t))
            JOB.append(len(jobs) - 1)
        QCOLS = {"mla": QUAD * P, "na": 2 * P, "dif": P}

        SU = []
        for L in range(LAYERS):
            o0, o1 = [0, 1, 2, 3, 4, 5], [1, 0, 5, 4, 3, 2]
            SU += [(L, dd, o[i]) for i in range(NT) for dd, o in ((0, o0), (1, o1))]
        YU = [0]
        for L, dd, t in SU:
            YU.append(YU[-1] + (1 if t in out_tiles(L) else 0))
        NB = [len(out_tiles(L)) * P * TOPK // P + EXP for L in range(LAYERS)]
        PAIRS = [n // 2 for n in NB]
        MINP = [len(out_tiles(L)) * TOPK // 2 for L in range(LAYERS)]
        NB0 = [0, NB[0] + 2]
        OT0 = [0, NT]
        OTN = [NT, NT - CT]

        modrow = ar(A_C, LAYERS * 6 * D)
        silu_c = ar(A_D, 32 * DC)

        def mod_w(i):
            return ar(A_E + (i % 3) * 4096, 4096)

        rs = ar(A_F + 3264, N)
        cT = ar(A_E, 3 * N).rearrange("p (c n) -> p c n", c=3)
        wqb = ar(A_E + 2304, 768)
        wkvb = ar(A_E + 3072, 512)
        scr = A_E + 3584
        sca = A_F + F_KM
        scs = A_F + F_KM + 3328
        Pb = ar(A_E, 2 * 1024).rearrange("p (b n) -> p b n", b=2)
        PTb = ar(A_E + 2 * 1024, 2 * 1024).rearrange("p (b n) -> p b n", b=2)
        qT = ar(A_E + 4 * 1024, 2 * QUAD * P).rearrange("p (b n) -> p b n", b=2)

        def att_cols(k, u, n=1):
            a = 16 * k + QUAD * (u % 4)
            return att[:, a:a + n]

        recip, recip_l = att[:, 48:52], att[:, 52:54]
        sq_dif = ar(scr, NT * GW).rearrange("p (t d) -> p t d", t=NT)
        sq_scan = ar(A_E + 5 * 1024 + 256, NT * GW).rearrange("p (t d) -> p t d", t=NT)
        bias4 = ar(A_D, HEADS * ROFF * GRID).rearrange("p (h r c) -> p h r c", h=HEADS, r=ROFF)
        wo = ar(A_E, E_W)

        def sv(k):
            return ssd[:, k * 48:(k + 1) * 48].rearrange("p (t h) -> p t h", t=NT)

        def GMb(w):
            return ar(sca + 256 * (YU[w] % 2), 256)

        def Mall(w):
            return ar(sca + 512 + 512 * (YU[w] % 2), 512)

        def Mb(w, h):
            return Mall(w)[:, h * P:(h + 1) * P]

        def xdt(w):
            return ar(sca + 1536 + 256 * (w % 2), 256)

        def xdte(w):
            return ar(sca + 2048 + 256 * (w % 2), 256)

        def state(dd):
            return ar(sca + 2560 + 256 * dd, 256)

        ytmp = ar(sca + 3072, 256)
        yacc = ar(A_RAW, NT * GW).rearrange("p (t d) -> p t d", t=NT)
        ftok = ar(A_F, 2 * D).rearrange("p (b n) -> p b n", b=2)
        zrows = ar(A_F + 5 * D, D)
        YZ0 = N * TOPK // P
        wr = ar(A_F + 3 * D, DC * 20).rearrange("p (k n) -> p k n", k=DC)
        RT = A_F + 4 * D

        def r_(off, n):
            return ar(RT + off, n)

        r_lg = r_(0, 120).rearrange("p (t n) -> p t n", t=NT)
        r_oh = [r_(420, 96).rearrange("p (t e) -> p t e", t=NT), r_(516, 96).rearrange("p (t e) -> p t e", t=NT)]
        r_pre = r_(852, (NT + 1) * EXP).rearrange("p (t e) -> p t e", t=NT + 1)
        lgT = ar(A_F + 6 * D, N)
        oh_row = ar(A_F + 6 * D, TOPK * NT * P).rearrange("p (k t n) -> p k t n", k=TOPK, t=NT)
        oh_blk = ar(A_F + 6 * D + TOPK * NT * P, TOPK * NT * NBMAX).rearrange("p (k t n) -> p k t n", k=TOPK, t=NT)
        r_sel = r_(612, 96).rearrange("p (t e) -> p t e", t=NT)

        def r6(k):
            return r_(168 + 6 * k, 6)

        def xg(par):
            return ar(M_X + par * D, D)

        def xT(par):
            return ar(M_X + 2 * D + par * D, D)

        def hid(par):
            return ar(M_X + 4 * D + par * FF, FF)

        def hidT(par):
            return ar(M_X + 4 * D + 2 * FF + par * FF, FF)

        def ysb(par):
            return ar(M_Y + par * D, D)

        def moe_w(par):
            o = M_W + par * M_WSET
            return (ar(o, DC * FF).rearrange("p (k n) -> p k n", k=DC),
                    ar(o + DC * FF, DC * FF).rearrange("p (k n) -> p k n", k=DC),
                    ar(o + 2 * DC * FF, FC * D).rearrange("p (k n) -> p k n", k=FC))

        def r12(i, k):
            return ar(A_F + 4 * D + (2 * (i % 2) + k) * D, D)

        restok = ftok

        def win_loads(L, j):
            n = [sum(1 if CH[q][0] == "x" else len(CH[q][3]) for q in range(top) if q % 2 == j % 2) for top in (NCH, j + 1)]
            return 16 * (n[0] * L + n[1])

        def win_done(L, j):
            if CH[j][0] == "x":
                return S("xp_ps"), XM * L + CH[j][1] + CH[j][2]
            return S("pj_ps"), PJ0[L] + sum(1 for q, _ in JOBS[L] if q <= j)

        def last_pair(eng, L):
            eng.wait_ge(S("blk_ready"), L + 1)
            before = eng.value_load(npair[0:1, 0:1], min_val=MINP[L] - 2, max_val=PAIRS[L] - 2)
            return before, before + 1

        def cnt2(L, i):
            return NT // 2 * L + i // 2

        block = st.enter_context(nc.Block())

        @block.sync
        def _(sp):
            sp.dma_start(K[:, :], io["consts"]).then_inc(S("consts_in"), 16)
            with nc.allow_non_contiguous_dma(reason="small columns"):
                sp.dma_start(cc[:, 0:8], io["c"][0].rearrange("(k p) -> p k", p=P)).then_inc(S("cc_in"), 16)
                sp.dma_start(cc[:, 8:16], io["c_ctx"].rearrange("(k p) -> p k", p=P)).then_inc(S("cc_in"), 16)
            for t in range(NT):
                src = io["ctx"][0, t * P:(t + 1) * P, :] if t < CT else io["x"][0, (t - CT) * P:(t - CT + 1) * P, :]
                sp.dma_start(ar(A_B + t * D, D), src).then_inc(S("x_in"), 16)
            sp.wait_ge(S("zeros"), 1)
            sp.dma_start(modrow[0:2, :],
                         io["b_mod"].rearrange("l n -> (l n)").partition_broadcast(2)).then_inc(S("bmod_in"), 16)
            for i, (L, n) in enumerate(mod_jobs):
                if i >= 3:
                    sp.wait_ge(S("wmod_used"), 4 * (i - 2))
                sp.dma_start(mod_w(i).rearrange("p (k n) -> p k n", k=DC),
                             io["w_mod"][L].rearrange("(k p) n -> p k n", p=P)[:, :, n * 512:(n + 1) * 512]
                             ).then_inc(S(f"wmod_in{i % 3}"), 16)
                if i == 2:
                    with nc.allow_non_contiguous_dma(reason="small columns"):
                        for l2 in range(LAYERS):
                            for w, nm in ((0, "g_mix"), (1, "g_ffn")):
                                sp.dma_start(gcol3[:, l2, w, :], io[nm][l2].rearrange("(k p) -> p k", p=P)
                                             ).then_inc(S("cols_in"), 16)
                            for m in range(XM):
                                sp.dma_start(cw[:, l2, m, 0:CONV],
                                             io["ssd_conv_w"][l2, :, m * P:(m + 1) * P].rearrange("j p -> p j")
                                             ).then_inc(S("cols_in"), 16)
                            sp.dma_start(cw[:, l2, :, CONV], io["ssd_conv_b"][l2].rearrange("(m p) -> p m", p=P)
                                         ).then_inc(S("cols_in"), 16)
            for l2 in range(LAYERS):
                sp.dma_start(dram["rel_rows"][l2 * GRID:(l2 + 1) * GRID, :], io["rel_pad"][l2].partition_broadcast(GRID)
                             ).then_inc(S("rel_copied"), 16)
            for L in range(LAYERS):
                if L:
                    sp.wait_ge(S("h_final"), 1)
                for nm, w in ROWS:
                    src = io[nm][L]
                    if len(src.shape) == 2:
                        src = src.rearrange("a b -> (a b)")
                    sp.dma_start(row(nm), src.partition_broadcast(P)).then_inc(S("rows_in"), 16)
                if L == 0:
                    sp.wait_ge(S("wmod_used"), 4 * len(mod_jobs))
                for j, ch in enumerate(CH):
                    if j >= 2:
                        sp.wait_ge(*win_done(L, j - 2))
                    src = io["w_in"][L].rearrange("(k p) n -> p k n", p=P)
                    b = wbuf[:, j % 2]
                    if ch[0] == "x":
                        a, w = XBC0 + ch[1] * P, ch[2] * P
                        sp.dma_start(b[:, :, 0:w], src[:, :, a:a + w]).then_inc(S(f"win_in{j % 2}"), 16)
                    else:
                        with nc.allow_non_contiguous_dma(reason="dt columns"):
                            for o, a, w in ch[3]:
                                sp.dma_start(b[:, :, o:o + w], src[:, :, a:a + w]).then_inc(S(f"win_in{j % 2}"), 16)
                    if L == 0 and j == 1:
                        sp.wait_ge(S("zeros"), 2)
                        for par in range(2):
                            sp.dma_start(dram["y_rows"].rearrange("(b q p) n -> q p b n", p=P, q=2)[par, :, YZ0 // 2:, :],
                                         bc(zrows, (0, (NBMAX - YZ0) // 2), (1, D))).then_inc(S(f"y_out{par}"), 16)
                        sp.dma_start(dram["f_rows"][N:N + 1, :], zrows[0:1, :]).then_inc(S("f_zero"), 16)
                sp.wait_ge(S("scan_done"), L + 1)
                sp.wait_ge(S("rel_copied"), 16 * LAYERS)
                rb = dram["rel_rows"]
                for half in range(2):
                    base = rb.offset + L * GRID * REL_W + REL_PAD + (NA_KW - 1)
                    n_ro = ROFF - half
                    for h in range(HEADS):
                        dst = bias4[64 * half:64 * half + 64, h, half:ROFF, :]
                        src = bass.AP(rb.tensor, base + h * ROFF * COFF, [[REL_W - 1, GRID], [COFF, n_ro], [1, GRID]])
                        sp.dma_start(dst, src).then_inc(S("bias_in"), 16)
                sp.wait_ge(*win_done(L, NCH - 1))
                sp.dma_start(wqb.rearrange("p (k n) -> p k n", k=2),
                             io["mla_w_qb"][L].rearrange("(k p) n -> p k n", p=P)).then_inc(S("wmla_in"), 16)
                sp.dma_start(wkvb, io["mla_w_kvb"][L]).then_inc(S("wmla_in"), 16)
                sp.wait_ge(S("mix_done"), L + 1)
                sp.dma_start(wo.rearrange("p (k n) -> p k n", k=DC),
                             io["w_out"][L].rearrange("(k p) n -> p k n", p=P)).then_inc(S("wo_in"), 16)
                sp.wait_ge(S("h_mid"), L + 1)
                with nc.allow_non_contiguous_dma(reason="router columns"):
                    sp.dma_start(wr[:, :, 0:GROUPS], io["moe_w_group"][L].rearrange("(k p) n -> p k n", p=P)
                                 ).then_inc(S("wr_in"), 16)
                    sp.dma_start(wr[:, :, GROUPS:], io["moe_w_expert"][L].rearrange("(k p) n -> p k n", p=P)
                                 ).then_inc(S("wr_in"), 16)
                for i, t in enumerate(out_tiles(L)):
                    sp.wait_ge(S("ftok_a"), OT0[L] + i + 1)
                    sp.dma_start(dram["f_rows"][t * P:(t + 1) * P, :], ftok[:, i % 2, :]).then_inc(S(f"f_out{i % 2}"), 16)
                wgv = io["moe_w_gate"][L].rearrange("e (k p) n -> e p k n", p=P)
                wuv = io["moe_w_up"][L].rearrange("e (k p) n -> e p k n", p=P)
                wdv = io["moe_w_down"][L].rearrange("e (k p) n -> e p k n", p=P)
                sp.wait_ge(S("blk_ready"), L + 1)

                def load_block(i, par, first=False):
                    b = 2 * i + par
                    e = sp.value_load(blk_e[0:1, bass.ds(b, 1)], min_val=0, max_val=EXP - 1)
                    wg, wu, wd = moe_w(par)
                    if not first:
                        sp.wait_ge(S("gu_ps"), NB0[L] + b - 1)
                    for dst, v in ((wg, wgv), (wu, wuv)):
                        sp.dma_start(dst, v[bass.ds(e, 1)].rearrange("e p k n -> p (e k) n")).then_inc(S(f"gu_in{par}"), 16)
                    if not first:
                        sp.wait_ge(S("dn_ps"), NB0[L] + b - 1)
                    sp.dma_start(wd, wdv[bass.ds(e, 1)].rearrange("e p k n -> p (e k) n")).then_inc(S(f"wd_in{par}"), 16)

                load_block(0, 0, True)
                for par in range(2):
                    sp.wait_ge(S(f"xg_in{L}{par}"), 16)
                load_block(0, 1, True)
                _, lastp = last_pair(sp, L)
                with sp.Fori(1, lastp + 1) as i:
                    for par in range(2):
                        load_block(i, par)
                for par in range(2):
                    sp.wait_ge(S(f"gu_in{par}"), 32 * lastp + 32 + 16 * NB0[L])
                    sp.wait_ge(S(f"wd_in{par}"), 16 * lastp + 16 + 8 * NB0[L])
                with sp.Fori(lastp + 1, PAIRS[L] + 1):
                    for par in range(2):
                        sp.sem_inc(S(f"gu_in{par}"), 32)
                        sp.sem_inc(S(f"wd_in{par}"), 16)
            for i in range(NT - CT):
                sp.wait_ge(S("res_a"), i + 1)
                sp.wait_ge(S("res_d"), i + 1)
                sp.dma_start(out[0, i * P:(i + 1) * P, :], restok[:, i % 2, :]).then_inc(S(f"res_out{i % 2}"), 16)
            for q in range(2):
                sp.wait_ge(S(f"res_out{q}"), 16 * ((NT - CT) // 2))

        @block.tensor
        def _(pe):
            pe.wait_ge(S("consts_in"), 16)
            pe.wait_ge(S("x_in"), 16 * NT)
            for t in range(NT):
                if t >= 2:
                    pe.wait_ge(S("x_ev_a"), t - 1)
                    pe.wait_ge(S("x_ev_d"), t - 1)
                for c in range(DC):
                    last = pe.transpose(PS[:, 2 * (t % 2) + c // 4, (c % 4) * P:(c % 4 + 1) * P],
                                        ar(A_B + t * D + c * P, P), ident)
                last.then_inc(S("x_ps"), 1)
            def mod_columns(i):
                pe.wait_ge(S("mod_ev"), i + 1)
                for j in range(4 * i, 4 * i + 4):
                    last = pe.matmul(PS[:, 6, 2 * j:2 * j + 2], modrow[:, j * P:(j + 1) * P], K[:, C_SEL:C_SEL + 2],
                                     start=True, stop=True)
                return last

            pe.wait_ge(S("cc_silu"), 1)
            for i in range(len(mod_jobs)):
                pe.wait_ge(S(f"wmod_in{i % 3}"), 16 * (i // 3 + 1))
                if i >= 2:
                    pe.wait_ge(S("mod_ev"), i - 1)
                for k in range(DC // 4):
                    for g in range(4):
                        kk = 2 * g + k
                        last = pe.matmul(PS[32 * g:32 * g + 32, 4 + i % 2, :], silu_c[:, 32 * kk:32 * kk + 32],
                                         mod_w(i)[:, kk * 512:(kk + 1) * 512], start=(k == 0), stop=(k == DC // 4 - 1))
                        if k == DC // 4 - 1:
                            last.then_inc(S("wmod_used"), 1)
                if i >= 1:
                    mod_columns(i - 1)
            mod_columns(len(mod_jobs) - 1).then_inc(S("modT_ps"), 1)

            def norm_sums(L, w):
                lo = 0 if w == 0 else tok_lo(L)
                base = (2 * L + w) * DC
                for c in range(DC):
                    pe.wait_ge(S("sq_done"), base + c + 1)
                    for bk, (a, b) in enumerate(segs(lo)):
                        last = pe.matmul(PS[:, bk, 0:b - a], ones, sq2[:, c % 2, a:b], start=(c == 0), stop=(c == DC - 1))
                    last.then_inc(S("sq_used"), 1)

            def in_proj(L):
                pe.wait_ge(S("aT_ready"), DC * (L + 1))
                k = 0
                for j, ch in enumerate(CH):
                    pe.wait_ge(S(f"win_in{j % 2}"), win_loads(L, j))
                    if ch[0] == "x":
                        for m in range(ch[1], ch[1] + ch[2]):
                            if m >= 2:
                                pe.wait_ge(S("raw_ready"), XM * L + m - 1)
                            mm = m - ch[1]
                            for bk, (a, b) in enumerate(segs(0)):
                                for c in range(DC):
                                    last = pe.matmul(PS[:, 2 * (m % 2) + bk, 0:b - a],
                                                     wbuf[:, j % 2, c, mm * P:(mm + 1) * P], aT[:, c, a:b],
                                                     start=(c == 0), stop=(c == DC - 1))
                            last.then_inc(S("xp_ps"), 1)
                        continue
                    for t in [tt for jj, tt in JOBS[L] if jj == j]:
                        if k >= 2:
                            pe.wait_ge(S("pj_ev"), PJ0[L] + k - 1)
                        for c in range(DC):
                            last = pe.matmul(PS[:, 4 + k % 2, 0:ch[2]], aT[:, c, t * P:(t + 1) * P],
                                             wbuf[:, j % 2, c, 0:ch[2]], start=(c == 0), stop=(c == DC - 1))
                        last.then_inc(S("pj_ps"), 1)
                        if XB_AT <= k < XB_AT + 2:
                            xb_transposes(L, k - XB_AT)
                        if k == CUM_AT:
                            scan_sums(L)
                        if SCAN_AT <= k <= SCAN_AT + 2 * NT:
                            scan_step(L, k - SCAN_AT)
                        k += 1

            def xb_transposes(L, half):
                if half == 0:
                    pe.wait_ge(S("xbc_ready"), XM * (L + 1))
                for t in range(3 * half, 3 * half + 3):
                    if t >= 2:
                        pe.wait_ge(S("xb_ev"), NT * L + t - 1)
                    for q in range(4):
                        last = pe.transpose(PS[:, 6 + t % 2, q * P:(q + 1) * P], xbcT[:, q, xcol(t):xcol(t) + P], ident)
                    last.then_inc(S("xb_ps"), 1)

            def mla_prep(L):
                pe.wait_ge(S("stats_done"), L + 1)
                for t in range(NT):
                    if t >= 2:
                        pe.wait_ge(S("cT_ev"), NT * L + t - 1)
                    for c in range(3):
                        last = pe.transpose(PS[:, t % 2, c * P:(c + 1) * P], p[:, t, PM + c * P:PM + (c + 1) * P], ident)
                    last.then_inc(S("cT_ps"), 1)
                pe.wait_ge(S("wmla_in"), 32 * (L + 1))
                for t in range(NT):
                    pe.wait_ge(S("cT_ev"), NT * L + t + 1)
                    if t >= 2:
                        pe.wait_ge(S("mq_ev"), NT * L + t - 1)
                        pe.wait_ge(S("mkv_ev"), NT * L + t - 1)
                    for c in range(2):
                        pe.matmul(PS[:, 2 + t % 2, 0:384], cT[:, c, t * P:(t + 1) * P], wqb[:, c * 384:(c + 1) * 384],
                                  start=(c == 0), stop=(c == 1))
                    last = pe.matmul(PS[:, 4 + t % 2, :], cT[:, 2, t * P:(t + 1) * P], wkvb, start=True, stop=True)
                    last.then_inc(S("mla_ps"), 1)

            def key_transposes(L):
                pe.wait_ge(S("na_norm"), L + 1)
                pe.wait_ge(S("dif_norm"), L + 1)
                for n in range(2 * NT):
                    kind, t = n // NT, n % NT
                    if n >= 2:
                        pe.wait_ge(S("kt_ev"), 2 * NT * L + n - 1)
                    if kind == 1 and t == 0:
                        pe.wait_ge(S("m_norm"), L + 1)
                    for q in range(4):
                        if kind == 0:
                            a = PNK + q * P if q < 2 else PDK + (q - 2) * P
                            src, rows_ = p[:, t, a:a + P], P
                        else:
                            a = 640 + MLA_D * q
                            src, rows_ = ot[:, t, a:a + MLA_D], MLA_D
                        last = pe.transpose(PS[0:rows_, 6 + n % 2, q * P:(q + 1) * P], src, ident)
                    last.then_inc(S("kt_ps"), 1)

            def attention(L):
                n, u0 = len(UN[L]), U0[L]
                pe.wait_ge(S("kt_ev"), 2 * NT * (L + 1))

                def q_transpose(j):
                    g, h, t = jobs[j]
                    if j:
                        pe.wait_ge(S("qT_ev"), j)
                    for q in range(QCOLS[g] // P):
                        if g == "mla":
                            src, r = ot[:, t, 256 + MLA_D * (h + q):256 + MLA_D * (h + q + 1)], MLA_D
                        elif g == "na":
                            src, r = p[:, t, PNQ + HD * h + P * q:PNQ + HD * h + P * (q + 1)], P
                        else:
                            src, r = p[:, t, PDQ + DQK * h:PDQ + DQK * h + P], P
                        last = pe.transpose(PS[0:r, 7, q * P:(q + 1) * P], src, ident)
                    last.then_inc(S("qT_ps"), 1)

                def q_and_k(g, h, j):
                    if g == "mla":
                        lo, hi, kt, q = 0, MLA_D, kTm[:, h], h
                    elif g == "na":
                        lo, hi, kt, q = HD * (h % 2), HD * (h % 2) + HD, kTn[:, h // 2], h // 2
                    else:
                        lo, hi, kt, q = DQK * (h % 4), DQK * (h % 4) + DQK, kTn[:, 2 + h // 4], 0
                    return qT[lo:hi, j % 2, q * P:(q + 1) * P], kt[lo:hi]

                def scores(u):
                    g, h0, t, w = ALLU[u]
                    if u == u0:
                        q_transpose(JOB[u])
                    if u + 1 < u0 + n and JOB[u + 1] != JOB[u]:
                        q_transpose(JOB[u + 1])
                    pe.wait_ge(S("qT_ev"), JOB[u] + 1)
                    if u >= 2:
                        pe.wait_ge(S("exp_done"), u - 1)
                    b0 = 2 * (u % 2)
                    if t < CT:
                        for k in range(w):
                            qh, kh = q_and_k(g, h0 + k, JOB[u])
                            if g == "dif" and k == 2:
                                pe.wait_ge(S("s_half"), 2 * dif_quads(u) + 2)
                            last = pe.matmul(PS[:, b0 + k % 2, (k // 2) * CTX:(k // 2 + 1) * CTX], qh, kh[:, 0:CTX],
                                             start=True, stop=True, skip_group_check=True)
                            if g == "dif" and k < 2:
                                last.then_inc(S("s_half"), 1)
                        last.then_inc(S("s_ps"), 1)
                        return
                    if g == "na" and t == CT:
                        pe.wait_ge(S("bias_ready"), L + 1)
                    bias = g == "na"
                    qh, kh = q_and_k(g, h0, JOB[u])
                    pe.matmul(PS[:, b0, :], qh, kh[:, 0:512], start=True, stop=not bias, skip_group_check=True)
                    last = pe.matmul(PS[:, b0 + 1, 0:256], qh, kh[:, 512:N], start=True, stop=not bias, skip_group_check=True)
                    if bias:
                        s0 = NA_KH - 1 - 2 * (t - CT)
                        pe.matmul(PS[:, b0, 256:512], ident, bias4[:, h0, s0:s0 + 4, :], start=False, stop=True,
                                  skip_group_check=True)
                        last = pe.matmul(PS[:, b0 + 1, 0:256], ident, bias4[:, h0, s0 + 4:s0 + 8, :], start=False,
                                         stop=True, skip_group_check=True)
                    last.then_inc(S("s_ps"), 1)

                def prob_transposes(u):
                    _, _, t, w = ALLU[u]
                    pe.wait_ge(S("exp_done"), u + 1)
                    if u >= 1:
                        pe.wait_ge(S("pt_ev_a"), u)
                        pe.wait_ge(S("pt_ev_d"), u)
                    for c in range(NT if t >= CT else CT * w):
                        last = pe.transpose(PS[:, 4 + c // 4, (c % 4) * P:(c % 4 + 1) * P],
                                            Pb[:, u % 2, c * P:(c + 1) * P], ident)
                    last.then_inc(S("t_ps"), 1)

                def values(u):
                    g, h0, t, w = ALLU[u]
                    pe.wait_ge(S("pt_ev_a"), u + 1)
                    pe.wait_ge(S("pt_ev_d"), u + 1)
                    if u >= 1:
                        pe.wait_ge(S("o_ev"), u)
                    nk = NT if t >= CT else CT
                    for k in range(w):
                        h = h0 + k
                        v0 = {"mla": PM + HD * h, "na": PNV + HD * h, "dif": PDV + HD * (h // 2)}[g]
                        a = at(k, w)
                        for c in range(nk):
                            last = pe.matmul(PS[:, 6, a * HD:(a + 1) * HD], PTb[:, u % 2, (a * nk + c) * P:(a * nk + c + 1) * P],
                                             p[:, c, v0:v0 + HD], start=(c == 0), stop=(c == nk - 1))
                    last.then_inc(S("o_ps"), 1)

                for u in range(u0, u0 + n + 2):
                    if u < u0 + n:
                        scores(u)
                    if u0 < u <= u0 + n:
                        prob_transposes(u - 1)
                    if u >= u0 + 2:
                        values(u - 2)

            def scan_sums(L):
                pe.wait_ge(S("xb_ev"), NT * (L + 1))
                pe.wait_ge(S("la_done"), L + 1)
                la = sv(0)
                pe.matmul(PS[:, 7, 0:24], triU, la[:, :, 0:4], start=True, stop=True)
                pe.matmul(PS[:, 7, 24:48], triL, la[:, :, 4:8], start=True, stop=True)
                pe.matmul(PS[:, 7, 48:96], ones, la, start=True, stop=True).then_inc(S("cum_ps"), 1)

            def scan_step(L, i):
                la = sv(0)
                n = 2 * NT
                if i == 0:
                    pe.wait_ge(S("cum_done"), L + 1)
                if i < n:
                    w = n * L + i
                    _, dd, t = SU[w]
                    if t in out_tiles(L):
                        if YU[w] >= 1:
                            pe.wait_ge(S("front_done"), YU[w])
                        yp = YU[w] % 2
                        tri = triU if dd == 0 else triL
                        for h in range(HEADS):
                            pe.matmul(PS[:, yp, h * P:(h + 1) * P], bc(la[:, t, dd * 4 + h:dd * 4 + h + 1], (0, P)), tri,
                                      start=True, stop=True)
                        x0 = xcol(t)
                        for g in range(2):
                            last = pe.matmul(PS[:, 2, g * P:(g + 1) * P], xbcT[:, 2 + g, x0:x0 + P],
                                             xbcT[:, 4 + g, x0:x0 + P], start=True, stop=True)
                        last.then_inc(S("rg_ps"), 1)
                if i >= 1:
                    w = n * L + i - 1
                    _, dd, t = SU[w]
                    pe.wait_ge(S("xdt_done"), w + 1)
                    if w >= 1:
                        pe.wait_ge(S("state_done"), w)
                    if t in out_tiles(L):
                        pe.wait_ge(S("m_done"), YU[w] + 1)
                        if YU[w] >= 1:
                            pe.wait_ge(S("y_done"), YU[w])
                        x0 = xcol(t)
                        for h in range(HEADS):
                            pe.matmul(PS[:, 3, h * HD:(h + 1) * HD], Mb(w, h), xdt(w)[:, h * HD:(h + 1) * HD],
                                      start=True, stop=True)
                        for g in range(2):
                            last = pe.matmul(PS[:, 3, 256 + g * P:256 + (g + 1) * P], xbcT[:, 4 + g, x0:x0 + P],
                                             state(dd)[:, g * P:(g + 1) * P], start=True, stop=True)
                        last.then_inc(S("y_ps"), 1)
                    for g in range(2):
                        last = pe.matmul(PS[:, 6, g * P:(g + 1) * P], xB[:, t, 256 + g * P:256 + (g + 1) * P],
                                         xdte(w)[:, g * P:(g + 1) * P], start=True, stop=True)
                    last.then_inc(S("st_ps"), 1)

            def out_proj(L):
                pe.wait_ge(S("mix_done"), L + 1)
                for i, t in enumerate(out_tiles(L)):
                    if i >= 2:
                        pe.wait_ge(S("oT_a"), OT0[L] + i - 1)
                        pe.wait_ge(S("oT_d"), OT0[L] + i - 1)
                    for c in range(DC):
                        f = {0: 2, 1: 3, 2: 0, 3: 1}.get(c, c)
                        last = pe.transpose(PS[:, 2 * (i % 2) + c // 4, (c % 4) * P:(c % 4 + 1) * P],
                                            ot[:, t, f * P:(f + 1) * P], ident)
                    last.then_inc(S("oT_ps"), 1)
                pe.wait_ge(S("oT_a"), OT0[L] + OTN[L])
                pe.wait_ge(S("oT_d"), OT0[L] + OTN[L])
                pe.wait_ge(S("wo_in"), 16 * (L + 1))
                for m in range(DC):
                    if m >= 2:
                        pe.wait_ge(S("op_ev"), DC * L + m - 1)
                    for bk, (a, b) in enumerate(segs(tok_lo(L))):
                        for c in range(DC):
                            last = pe.matmul(PS[:, 4 + 2 * (m % 2) + bk, 0:b - a], wo[:, c * D + m * P:c * D + (m + 1) * P],
                                             oT[:, c, a:b], start=(c == 0), stop=(c == DC - 1))
                    last.then_inc(S("op_ps"), 1)

            def route_and_rows(L):
                tl = out_tiles(L)
                t0, T = tl[0], len(tl)
                pe.wait_ge(S("wr_in"), 32 * (L + 1))
                for c in range(DC):
                    pe.wait_ge(S("fT_ready"), DC * L + c + 1)
                    for bk, (a, b) in enumerate(segs(tok_lo(L))):
                        last = pe.matmul(PS[0:20, 4 + bk, 0:b - a], wr[:, c, :], aT[:, c, a:b], start=(c == 0), stop=(c == DC - 1))
                last.then_inc(S("lgT_ps"), 1)
                pe.wait_ge(S("lgT_ev"), L + 1)
                for t in tl:
                    last = pe.transpose(PS[:, 6, t * 20:(t + 1) * 20], lgT[0:20, t * P:(t + 1) * P], ident[0:20, 0:20])
                last.then_inc(S("lg_ps"), 1)
                for i, t in enumerate(tl):
                    if i >= 2:
                        pe.wait_ge(S("ftok_a"), OT0[L] + i - 1)
                    for c in range(DC):
                        last = pe.transpose(PS[:, 2 * (i % 2) + c // 4, (c % 4) * P:(c % 4 + 1) * P],
                                            aT[:, c, t * P:(t + 1) * P], ident)
                    last.then_inc(S("ftok_ps"), 1)
                pe.wait_ge(S("sel_done"), L + 1)
                pe.matmul(PS[:, 5, t0 * EXP:NT * EXP], strictU, r_sel[:, t0:, :], start=True, stop=False, skip_group_check=True)
                pe.matmul(PS[:, 5, t0 * EXP:NT * EXP], ones, r_pre[:, 0:T, :], start=False, stop=True, skip_group_check=True)
                pe.matmul(PS[:, 5, NT * EXP:(NT + 1) * EXP], ones, r_pre[:, T, :], start=True, stop=True).then_inc(S("rank_ps"), 1)
                pe.wait_ge(S("oh_ready"), L + 1)
                jobs_ = [(k, t) for k in range(TOPK) for t in range(T)]
                for n_, (k, t) in enumerate(jobs_):
                    last = pe.matmul(PS[:, 6, 0:NBMAX], oh_row[:, k, t, :], oh_blk[:, k, t, :], start=(n_ == 0),
                                     stop=(n_ == len(jobs_) - 1))
                last.then_inc(S("slot_ps"), 1)

            def experts(L):
                n0 = NB0[L]

                def x_transposes(i, par, first=False):
                    b = 2 * i + par
                    pe.wait_ge(S(f"xg_in{L}{par}"), 16 * (i + 1))
                    if not first:
                        pe.wait_ge(S("xT_a"), n0 + b)
                        pe.wait_ge(S("xT_d"), n0 + b)
                    for c in range(DC):
                        last = pe.transpose(PS[:, c // 4, (c % 4) * P:(c % 4 + 1) * P], xg(par)[:, c * P:(c + 1) * P], ident)
                    last.then_inc(S("xt_ps"), 1)

                def gate_up(i, par, first=False):
                    b = 2 * i + par
                    wg, wu, _ = moe_w(par)
                    pe.wait_ge(S(f"gu_in{par}"), 32 * (i + 1) + 32 * (n0 // 2))
                    pe.wait_ge(S("xT_a"), n0 + b + 1)
                    pe.wait_ge(S("xT_d"), n0 + b + 1)
                    if not first:
                        pe.wait_ge(S("h_done"), n0 + b)
                    for bk, w in ((2, wg), (3, wu)):
                        for c in range(DC):
                            last = pe.matmul(PS[:, bk, :], xT(par)[:, c * P:(c + 1) * P], w[:, c, :], start=(c == 0),
                                             stop=(c == DC - 1))
                    last.then_inc(S("gu_ps"), 1)

                def h_transposes(i, par, first=False):
                    b = 2 * i + par
                    pe.wait_ge(S("h_done"), n0 + b + 1)
                    if not first:
                        pe.wait_ge(S("hT_ev"), n0 + b)
                    for c in range(FC):
                        last = pe.transpose(PS[:, 4, c * P:(c + 1) * P], hid(par)[:, c * P:(c + 1) * P], ident)
                    last.then_inc(S("ht_ps"), 1)

                def down(i, par, first=False, back=0):
                    b = 2 * i + (par - 2 * back)
                    _, _, wd = moe_w(par)
                    pe.wait_ge(S("hT_ev"), b + (n0 + 1))
                    pe.wait_ge(S(f"wd_in{par}"), 16 * i + (16 - 16 * back + 16 * (n0 // 2)))
                    if not first:
                        pe.wait_ge(S("y_a"), b + n0)
                        pe.wait_ge(S("y_d"), b + n0)
                    for half in range(2):
                        for c in range(FC):
                            last = pe.matmul(PS[:, 5 + half, :], hidT(par)[:, c * P:(c + 1) * P],
                                             wd[:, c, half * 512:(half + 1) * 512], start=(c == 0), stop=(c == FC - 1))
                    last.then_inc(S("dn_ps"), 1)

                before, lastp = last_pair(pe, L)
                fl = L == 0
                x_transposes(0, 0, fl)
                gate_up(0, 0, fl)
                x_transposes(0, 1)
                h_transposes(0, 0, fl)
                gate_up(0, 1)
                x_transposes(1, 0)
                down(0, 0, fl)
                h_transposes(0, 1)
                with pe.Fori(1, lastp) as i:
                    gate_up(i, 0)
                    x_transposes(i, 1)
                    down(i, 1, back=1)
                    h_transposes(i, 0)
                    gate_up(i, 1)
                    x_transposes(i + 1, 0)
                    down(i, 0)
                    h_transposes(i, 1)
                gate_up(lastp, 0)
                x_transposes(lastp, 1)
                down(before, 1)
                h_transposes(lastp, 0)
                gate_up(lastp, 1)
                down(lastp, 0)
                h_transposes(lastp, 1)
                down(lastp, 1)
                pe.drain()
                with pe.Fori(lastp + 1, PAIRS[L] + 1):
                    for nm in ("xt_ps", "gu_ps", "ht_ps", "dn_ps"):
                        pe.sem_inc(S(nm), 2)

            def combine(L):
                for i, t in enumerate(out_tiles(L)):
                    pe.wait_ge(S("comb"), OT0[L] + i + 1)
                    if i >= 2:
                        pe.wait_ge(S("hup"), OT0[L] + i - 1)
                    for c in range(DC):
                        last = pe.transpose(PS[:, 2 * (i % 2) + c // 4, (c % 4) * P:(c % 4 + 1) * P],
                                            r12(i, 0)[:, c * P:(c + 1) * P], ident)
                    last.then_inc(S("comb_ps"), 1)

            for L in range(LAYERS):
                norm_sums(L, 0)
                in_proj(L)
                mla_prep(L)
                key_transposes(L)
                attention(L)
                out_proj(L)
                norm_sums(L, 1)
                route_and_rows(L)
                experts(L)
                combine(L)
            pe.wait_ge(S("h_final"), LAYERS)
            for i, t in enumerate(out_tiles(1)):
                if i >= 2:
                    pe.wait_ge(S("res_a"), i - 1)
                    pe.wait_ge(S("res_d"), i - 1)
                for c in range(DC):
                    last = pe.transpose(PS[:, 2 * (i % 2) + c // 4, (c % 4) * P:(c % 4 + 1) * P],
                                        hT[:, c, t * P:(t + 1) * P], ident)
                last.then_inc(S("res_ps"), 1)

        @block.scalar
        def _(act):
            for t in range(NT):
                act.wait_ge(S("x_ps"), t + 1)
                act.activation(hT[:, 0:4, t * P:(t + 1) * P], PS[:, 2 * (t % 2), :].rearrange("p (c n) -> p c n", c=4),
                               ACT.Copy).then_inc(S("x_ev_a"), 1)
            act.wait_ge(S("cc_in"), 32)
            act.activation(silu_c.rearrange("p (k r s) -> p k r s", k=DC, s=2), bc(cc[:, 0:1], (1, DC), (0, 16), (8, 2)),
                           ACT.Silu).then_inc(S("cc_silu"), 1)

            def norm(L, w):
                lo = 0 if w == 0 else tok_lo(L)
                base = (2 * L + w) * DC
                if w == 1:
                    act.wait_ge(S("h_mid"), L + 1)
                elif L:
                    act.wait_ge(S("h_final"), L)
                else:
                    act.wait_ge(S("x_ev_d"), NT)
                    act.wait_ge(S("x_ev_a"), NT)
                for c in range(DC):
                    if base + c >= 2:
                        act.wait_ge(S("sq_used"), base + c - 1)
                    act.activation(sq2[:, c % 2, lo:N], hT[:, c, lo:N], ACT.Square).then_inc(S("sq_done"), 1)
                act.wait_ge(S("var_done"), 2 * L + w + 1)
                act.activation(rs[:, lo:N], rs[:, lo:N], ACT.Sqrt).then_inc(S("sqrt_done"), 1)
                act.wait_ge(S("acol_ready"), 1)
                for c in range(DC):
                    act.wait_ge(S("nrm_x"), base + c + 1)
                    for s, a, b in streams(lo, N):
                        last = act.activation(aT[:, c, a:b], aT[:, c, a:b], ACT.Identity,
                                              scale=acol4[:, L, w, c, s:s + 1], bias=mod4[:, L, 24 * w + c, s:s + 1])
                    last.then_inc(S("fT_ready" if w else "aT_ready"), 1)

            def in_proj(L):
                act.wait_ge(S("pads_ready"), L + 1)
                for m in range(XM + 1):
                    if m < XM:
                        act.wait_ge(S("xp_ps"), XM * L + m + 1)
                        if m >= 2:
                            act.wait_ge(S("conv_done"), XM * L + m - 1)
                        b0 = 2 * (m % 2)
                        act.activation(raw[:, m % 2, 2:2 + CTX], PS[:, b0, 0:CTX], ACT.Copy)
                        act.activation(raw[:, m % 2, 6 + CTX:6 + 512], PS[:, b0, CTX:512], ACT.Copy)
                        act.activation(raw[:, m % 2, 6 + 512:6 + N], PS[:, b0 + 1, 0:N - 512], ACT.Copy
                                       ).then_inc(S("raw_ready"), 1)
                    if m:
                        act.wait_ge(S("conv_done"), XM * L + m)
                        act.activation(xbcT[:, m - 1, :], xbcT[:, m - 1, :], ACT.Silu).then_inc(S("xbc_ready"), 1)
                for k, (j, t) in enumerate(JOBS[L]):
                    act.wait_ge(S("pj_ps"), PJ0[L] + k + 1)
                    a, w = CH[j][1], CH[j][2]
                    act.activation(p[:, t, a:a + w], PS[:, 4 + k % 2, 0:w], ACT.Copy).then_inc(S("pj_ev"), 1)
                    if XB_AT <= k < XB_AT + 2:
                        for t2 in range(3 * (k - XB_AT), 3 * (k - XB_AT) + 3):
                            act.wait_ge(S("xb_ps"), NT * L + t2 + 1)
                            act.activation(xB[:, t2, :], PS[:, 6 + t2 % 2, :], ACT.Copy).then_inc(S("xb_ev"), 1)
                    if k == CUM_AT - 1:
                        step_sizes(L)
                    if k == CUM_AT:
                        act.wait_ge(S("cum_in"), L + 1)
                        act.activation(ssd[:, 5 * 48:6 * 48], ssd[:, 2 * 48:3 * 48], ACT.Exp)
                        act.activation(ssd[:, 4 * 48:5 * 48], ssd[:, 4 * 48:5 * 48], ACT.Exp)
                        act.activation(ssd[:, 6 * 48:7 * 48], ssd[:, 3 * 48:4 * 48], ACT.Exp).then_inc(S("cum_exp"), 1)
                    if SCAN_AT <= k < SCAN_AT + 2 * NT:
                        w = 2 * NT * L + k - SCAN_AT
                        if SU[w][2] in out_tiles(L):
                            act.wait_ge(S("front_done"), YU[w] + 1)
                            act.activation(Mall(w), Mall(w), ACT.Exp).then_inc(S("seg_exp"), 1)
                    if k + 1 < len(JOBS[L]) and JOBS[L][k + 1][0] == NCH - 1 and j != NCH - 1:
                        stats(L)

            def step_sizes(L):
                act.wait_ge(S("pj_ev"), PJ0[L] + NT)
                act.wait_ge(S("sp_in"), L + 1)
                act.activation(ssd[:, 8 * 48:9 * 48], ssd[:, 8 * 48:9 * 48], ACT.Exp).then_inc(S("sp_u"), 1)
                act.wait_ge(S("sp_w"), L + 1)
                act.activation(ssd[:, 48:96], ssd[:, 9 * 48:10 * 48], ACT.Ln)
                act.activation(sc[:, 8:16], row("ssd_a_log"), ACT.Exp).then_inc(S("sp_ln"), 1)
                act.activation(ar(scs, NT * 384).rearrange("p (t d) -> p t d", t=NT), p[:, :, PM:PM + 384], ACT.Square
                               ).then_inc(S("sq_stats"), 1)
                ss3 = ss[:, :].rearrange("p (t h) -> p t h", t=NT)
                act.wait_ge(S("var_s"), 2 * L + 1)
                act.activation(ss3[:, :, 24:26], ss3[:, :, 24:26], ACT.Sqrt).then_inc(S("sqrt_s"), 1)

            def stats(L):
                t0 = out_tiles(L)[0]
                nt = NT - t0
                act.wait_ge(S("scan_done"), L + 1)
                act.wait_ge(S("pj_ev"), PJ0[L] + 3 * NT + nt)
                for q, a in enumerate((PNK, PDK)):
                    act.activation(ar(sca + q * NT * 256, NT * 256).rearrange("p (t d) -> p t d", t=NT), p[:, :, a:a + 256], ACT.Square)
                act.activation(ar(sca + NT * 512, nt * 512).rearrange("p (t d) -> p t d", t=nt), p[:, t0:, PNQ:PNQ + 512], ACT.Square
                               ).then_inc(S("sq_stats"), 1)
                ss3 = ss[:, :].rearrange("p (t h) -> p t h", t=NT)
                act.wait_ge(S("var_s"), 2 * L + 2)
                act.activation(ss3[:, :, 0:24], ss3[:, :, 0:24], ACT.Sqrt).then_inc(S("sqrt_s"), 1)

            def mla_prep(L):
                for t in range(NT):
                    act.wait_ge(S("cT_ps"), NT * L + t + 1)
                    act.activation(cT[:, :, t * P:(t + 1) * P], PS[:, t % 2, 0:384].rearrange("p (c n) -> p c n", c=3),
                                   ACT.Copy).then_inc(S("cT_ev"), 1)
                for t in range(NT):
                    act.wait_ge(S("mla_ps"), NT * L + t + 1)
                    act.activation(ot[:, t, 256:640], PS[:, 2 + t % 2, 0:384], ACT.Copy).then_inc(S("mq_ev"), 1)
                act.wait_ge(S("mq_ev"), NT * (L + 1))
                act.wait_ge(S("mkv_ev"), NT * (L + 1))
                act.activation(ar(scr, NT * 768).rearrange("p (t d) -> p t d", t=NT), ot[:, :, 256:1024], ACT.Square
                               ).then_inc(S("sq_m"), 1)
                act.wait_ge(S("var_m"), L + 1)
                act.activation(ss2[:, :], ss2[:, :], ACT.Sqrt).then_inc(S("sqrt_m"), 1)
                for n in range(2 * NT):
                    kind, t = n // NT, n % NT
                    if n == NT:
                        zt = p[:, out_tiles(L)[0]:, PZ:PZ + GW]
                        act.activation(zt, zt, ACT.Silu).then_inc(S("z_silu"), 1)
                    act.wait_ge(S("kt_ps"), 2 * NT * L + n + 1)
                    src = PS[:, 6 + n % 2, :].rearrange("p (q n) -> p q n", q=4)
                    if kind == 0:
                        act.activation(kTn[:, :, t * P:(t + 1) * P], src, ACT.Copy).then_inc(S("kt_ev"), 1)
                    else:
                        act.activation(kTm[0:MLA_D, :, t * P:(t + 1) * P], src[0:MLA_D], ACT.Copy).then_inc(S("kt_ev"), 1)

            def attention(L):
                n, u0 = len(UN[L]), U0[L]
                act.wait_ge(S("lam_in"), L + 1)
                act.activation(sc[:, 0:2], sc[:, 0:2], ACT.Exp).then_inc(S("lam_exp"), 1)

                def q_evac(j):
                    act.wait_ge(S("qT_ps"), j + 1)
                    g = jobs[j][0]
                    r = MLA_D if g == "mla" else P
                    act.activation(qT[0:r, j % 2, 0:QCOLS[g]], PS[0:r, 7, 0:QCOLS[g]], ACT.Copy).then_inc(S("qT_ev"), 1)

                def exps(u):
                    _, _, t, w = ALLU[u]
                    if u == u0:
                        q_evac(JOB[u])
                    if u + 1 < u0 + n and JOB[u + 1] != JOB[u]:
                        q_evac(JOB[u + 1])
                    act.wait_ge(S("nm_done"), u + 1)
                    if u >= 2:
                        act.wait_ge(S("t_ps"), u - 1)
                        if u >= 4:
                            act.wait_ge(S("o_ev"), u - 3)
                    sp_ = PS[:, 2 * (u % 2):2 * (u % 2) + 2, :].rearrange("p b n -> p (b n)")
                    kw = N if t >= CT else CTX
                    for k in range(w):
                        last = act.activation(Pb[:, u % 2, k * kw:(k + 1) * kw], sp_[:, k * kw:(k + 1) * kw], ACT.Exp,
                                              bias=att_cols(1, u, w)[:, k:k + 1], accum_out=att_cols(2, u, w)[:, k:k + 1])
                    last.then_inc(S("exp_done"), 1)

                def probs_evac(u):
                    act.wait_ge(S("t_ps"), u + 1)
                    if u >= 2:
                        act.wait_ge(S("o_ps"), u - 1)
                    act.activation(PTb[:, u % 2, 0:512], PS[:, 4, :], ACT.Copy).then_inc(S("pt_ev_a"), 1)

                for u in range(u0, u0 + n + 1):
                    if u < u0 + n:
                        exps(u)
                    if u > u0:
                        probs_evac(u - 1)

            def finish(L):
                t0 = out_tiles(L)[0]
                act.wait_ge(S("o_ev"), U0[L] + len(UN[L]))
                act.activation(sq_dif[:, t0:], ot[:, t0:, 512:768], ACT.Square).then_inc(S("fin_sq"), 1)
                act.wait_ge(S("var_f"), L + 1)
                act.activation(ss[:, 5 * t0:30], ss[:, 5 * t0:30], ACT.Sqrt).then_inc(S("sqrt_f"), 1)

            def out_proj(L):
                for i, t in enumerate(out_tiles(L)):
                    act.wait_ge(S("oT_ps"), OT0[L] + i + 1)
                    act.activation(oT[:, 0:4, t * P:(t + 1) * P], PS[:, 2 * (i % 2), :].rearrange("p (c n) -> p c n", c=4),
                                   ACT.Copy).then_inc(S("oT_a"), 1)

            def rows_and_route(L):
                n = OTN[L]
                for i in range(n):
                    act.wait_ge(S("ftok_ps"), OT0[L] + i + 1)
                    if cnt2(L, i):
                        act.wait_ge(S(f"f_out{i % 2}"), 16 * cnt2(L, i))
                    act.activation(ftok[:, i % 2, :], PS[:, 2 * (i % 2):2 * (i % 2) + 2, :].rearrange("p b n -> p (b n)"),
                                   ACT.Copy).then_inc(S("ftok_a"), 1)
                    if i == 1:
                        act.wait_ge(S("rt_g"), L + 1)
                        act.activation(r_(120, 24), r_(120, 24), ACT.Exp).then_inc(S("rt_ge"), 1)
                act.wait_ge(S("rt_m"), L + 1)
                act.activation(r6(4), r6(4), ACT.Exp).then_inc(S("rt_me"), 1)

            def experts(L):
                n0 = NB0[L]

                def x_evac(i, par):
                    b = 2 * i + par
                    act.wait_ge(S("xt_ps"), n0 + b + 1)
                    act.activation(xT(par)[:, 0:512], PS[:, 0, :], ACT.Copy).then_inc(S("xT_a"), 1)

                def gate(i, par):
                    b = 2 * i + par
                    act.wait_ge(S("gu_ps"), n0 + b + 1)
                    act.activation(hid(par), PS[:, 2, :], ACT.Silu).then_inc(S("silu_done"), 1)

                def y_store(i, par, back=0):
                    b = 2 * i + (par - 2 * back)
                    act.wait_ge(S("dn_ps"), n0 + b + 1)
                    act.wait_ge(S(f"y_out{par}"), 16 * i + (16 * (n0 // 2) + 16 - 16 * back))
                    act.activation(ysb(par)[:, 0:512], PS[:, 5, :], ACT.Copy).then_inc(S("y_a"), 1)
                    act.wait_ge(S("y_a"), n0 + b + 1)
                    act.wait_ge(S("y_d"), n0 + b + 1)
                    act.dma_start(dram["y_rows"].rearrange("(b p) n -> b p n", p=P)[bass.ds(b, 1)].rearrange("b p n -> p (b n)"),
                                  ysb(par)).then_inc(S(f"y_out{par}"), 16)

                before, lastp = last_pair(act, L)
                x_evac(0, 0)
                gate(0, 0)
                x_evac(0, 1)
                gate(0, 1)
                x_evac(1, 0)
                y_store(0, 0)
                with act.Fori(1, lastp) as i:
                    gate(i, 0)
                    x_evac(i, 1)
                    y_store(i, 1, back=1)
                    gate(i, 1)
                    x_evac(i + 1, 0)
                    y_store(i, 0)
                gate(lastp, 0)
                x_evac(lastp, 1)
                y_store(before, 1)
                gate(lastp, 1)
                y_store(lastp, 0)
                y_store(lastp, 1)
                act.drain()
                for par in range(2):
                    act.wait_ge(S(f"y_out{par}"), 16 * lastp + 32 + 8 * n0)
                with act.Fori(lastp + 1, PAIRS[L] + 1):
                    for nm in ("xT_a", "silu_done", "y_a"):
                        act.sem_inc(S(nm), 2)
                    for par in range(2):
                        act.sem_inc(S(f"y_out{par}"), 16)

            for L in range(LAYERS):
                norm(L, 0)
                in_proj(L)
                mla_prep(L)
                attention(L)
                finish(L)
                out_proj(L)
                norm(L, 1)
                rows_and_route(L)
                experts(L)
            for i, t in enumerate(out_tiles(1)):
                act.wait_ge(S("res_ps"), i + 1)
                if i >= 2:
                    act.wait_ge(S(f"res_out{i % 2}"), 16 * (i // 2))
                act.activation(restok[:, i % 2, 0:512], PS[:, 2 * (i % 2), :], ACT.Copy).then_inc(S("res_a"), 1)

        @block.vector
        def _(dve):
            link = Chain(dve, S("dve_chain"))
            dve.wait_ge(S("consts_in"), 16)
            mul = ALU.mult
            for t in range(NT):
                dve.wait_ge(S("x_ps"), t + 1)
                dve.tensor_copy(hT[:, 4:8, t * P:(t + 1) * P],
                                PS[:, 2 * (t % 2) + 1, :].rearrange("p (c n) -> p c n", c=4)).then_inc(S("x_ev_d"), 1)
            dve.wait_ge(S("bmod_in"), 16)
            for i in range(len(mod_jobs)):
                dve.wait_ge(S("wmod_used"), 4 * (i + 1))
                mr = modrow[:, i * 512:(i + 1) * 512]
                dve.tensor_tensor(mr, PS[:, 4 + i % 2, :], mr, ALU.add).then_inc(S("mod_ev"), 1)
            dve.wait_ge(S("modT_ps"), 1)
            link(dve.tensor_copy(modcol[:, :], PS[:, 6, 0:LAYERS * 96]))
            dve.wait_ge(S("cols_in"), 16 * LAYERS * (3 + XM))
            for l2 in range(LAYERS):
                for w in range(2):
                    g = gcol3[:, l2, w, :]
                    last = dve.scalar_tensor_tensor(out=acol4[:, l2, w], in0=mod4[:, l2, 24 * w + 8:24 * w + 16, :], scalar=1.0,
                                                    in1=bc(g, (1, DC), (0, 2)), op0=ALU.add, op1=mul)
            last.then_inc(S("acol_ready"), 1)

            def norm(L, w):
                lo = 0 if w == 0 else tok_lo(L)
                base = (2 * L + w) * DC
                dve.wait_ge(S("sq_used"), base + DC)
                for bk, (a, b) in enumerate(segs(lo)):
                    last = dve.tensor_scalar(rs[:, a:b], PS[:, bk, 0:b - a], 1.0 / D, EPS, mul, ALU.add)
                last.then_inc(S("var_done"), 1)
                if w == 0:
                    dve.memset(raw[:, :, 0:2], 0.0)
                    dve.memset(raw[:, :, 2 + CTX:6 + CTX], 0.0)
                    dve.memset(raw[:, :, RAWW - 2:RAWW], 0.0).then_inc(S("pads_ready"), 1)
                dve.wait_ge(S("sqrt_done"), 2 * L + w + 1)
                link(dve.reciprocal(rs[:, lo:N], rs[:, lo:N]))
                for c in range(DC):
                    dve.tensor_tensor(aT[:, c, lo:N], hT[:, c, lo:N], rs[:, lo:N], mul).then_inc(S("nrm_x"), 1)

            def conv(L):
                for m in range(XM):
                    dve.wait_ge(S("raw_ready"), XM * L + m + 1)
                    o = xbcT[:, m, :]
                    link(dve.tensor_scalar(o, raw[:, m % 2, 0:XW], cw[:, L, m, 0:1], cw[:, L, m, 5:6], mul, ALU.add))
                    for j in range(1, CONV):
                        ins = dve.scalar_tensor_tensor(out=o, in0=raw[:, m % 2, j:j + XW], scalar=cw[:, L, m, j:j + 1],
                                                       in1=o, op0=mul, op1=ALU.add)
                        if j < CONV - 1:
                            link(ins)
                    ins.then_inc(S("conv_done"), 1)

            ss3 = ss[:, :].rearrange("p (t h) -> p t h", t=NT)
            ss23 = ss2[:, :].rearrange("p (t h) -> p t h", t=NT)

            def heads(v, h):
                return v.rearrange("p t (h d) -> p t h d", h=h)

            def over(a3, d):
                return bc(a3, list(a3.ap[1]), list(a3.ap[2]), (0, d))

            def gain(name, t, h):
                g = row(name)
                return bc(g, (0, t), (0, h), (1, ROW_AT[name][1]))

            def rotate(v, tmp, nh):
                x1, x2 = v[:, :, :, 0:16], v[:, :, :, 16:32]
                cosb = bc(K[:, C_COS:C_COS + 1], (16, 4), (0, nh), (1, 16))
                sinb = bc(K[:, C_SIN:C_SIN + 1], (16, 4), (0, nh), (1, 16))
                n = 4 * nh * 16
                tm = [ar(tmp + q * n, n).rearrange("p (t h d) -> p t h d", t=4, h=nh) for q in range(4)]
                dve.tensor_tensor(tm[0], x1, cosb, mul)
                dve.tensor_tensor(tm[1], x2, sinb, mul)
                dve.tensor_tensor(tm[2], x1, sinb, mul)
                link(dve.tensor_tensor(tm[3], x2, cosb, mul))
                dve.tensor_tensor(x1, tm[0], tm[1], ALU.subtract)
                return dve.tensor_tensor(x2, tm[2], tm[3], ALU.add)

            def latent_stats(L):
                dve.wait_ge(S("sq_stats"), 2 * L + 1)
                m2 = ar(scs, NT * 384).rearrange("p (t d) -> p t d", t=NT)
                dve.tensor_reduce(ss3[:, :, 24], m2[:, :, 0:256], AX.X, ALU.add)
                link(dve.tensor_reduce(ss3[:, :, 25], m2[:, :, 256:384], AX.X, ALU.add))
                dve.tensor_scalar(ss3[:, :, 24:25], ss3[:, :, 24:25], 1.0 / 256, EPS, mul, ALU.add)
                dve.tensor_scalar(ss3[:, :, 25:26], ss3[:, :, 25:26], 1.0 / 128, EPS, mul, ALU.add).then_inc(S("var_s"), 1)
                dve.wait_ge(S("sqrt_s"), 2 * L + 1)
                link(dve.reciprocal(ss3[:, :, 24:26], ss3[:, :, 24:26]))
                cq, ckv = p[:, :, PM:PM + 256], p[:, :, PM + 256:PM + 384]
                dve.tensor_tensor(cq, cq, bc(ss3[:, :, 24], (26, NT), (0, 256)), mul)
                link(dve.tensor_tensor(ckv, ckv, bc(ss3[:, :, 25], (26, NT), (0, 128)), mul))
                dve.tensor_tensor(cq, cq, bc(row("mla_g_qa"), (0, NT), (1, 256)), mul)
                dve.tensor_tensor(ckv, ckv, bc(row("mla_g_kva"), (0, NT), (1, 128)), mul).then_inc(S("stats_done"), 1)

            def stats(L):
                t0 = out_tiles(L)[0]
                nt = NT - t0
                dve.wait_ge(S("sq_stats"), 2 * L + 2)

                def sq(off, tiles, width, h, a, n):
                    v = ar(sca + off, tiles * width).rearrange("p (t d) -> p t d", t=tiles)[:, :, a:a + n]
                    return heads(v, h)
                dve.tensor_reduce(ss3[:, :, 0:4], sq(0, NT, 256, 4, 0, 256), AX.X, ALU.add)
                dve.tensor_reduce(ss3[:, :, 8:16], sq(NT * 256, NT, 256, 8, 0, 256), AX.X, ALU.add)
                dve.tensor_reduce(ss3[:, t0:, 4:8], sq(NT * 512, nt, 512, 4, 0, 256), AX.X, ALU.add)
                link(dve.tensor_reduce(ss3[:, t0:, 16:24], sq(NT * 512, nt, 512, 8, 256, 256), AX.X, ALU.add))
                dve.tensor_scalar(ss3[:, :, 0:8], ss3[:, :, 0:8], 1.0 / HD, EPS, mul, ALU.add)
                dve.tensor_scalar(ss3[:, :, 8:24], ss3[:, :, 8:24], 1.0 / DQK, EPS, mul, ALU.add).then_inc(S("var_s"), 1)
                dve.wait_ge(S("sqrt_s"), 2 * L + 2)
                link(dve.reciprocal(ss3[:, :, 0:24], ss3[:, :, 0:24]))
                dve.tensor_scalar(ss3[:, :, 4:8], ss3[:, :, 4:8], HD ** -0.5, None, mul)
                dve.tensor_scalar(ss3[:, :, 16:24], ss3[:, :, 16:24], DQK ** -0.5, None, mul).then_inc(S("rstd_done"), 1)
                dve.wait_ge(S("rstd_done"), L + 1)
                vk, vq = heads(p[:, :, PDK:PDK + 256], 8), heads(p[:, t0:, PDQ:PDQ + 256], 8)
                dve.tensor_tensor(vk, vk, over(ss3[:, :, 8:16], DQK), mul)
                link(dve.tensor_tensor(vq, vq, over(ss3[:, t0:, 16:24], DQK), mul))
                dve.tensor_tensor(vk, vk, gain("diff_g_k", NT, 8), mul)
                link(dve.tensor_tensor(vq, vq, gain("diff_g_q", nt, 8), mul))
                link(rotate(vk[:, CT:], A_F + F_XB, 8))
                rotate(vq[:, CT - t0:], A_F + F_XB, 8).then_inc(S("dif_norm"), 1)

            def mla_prep(L):
                for t in range(NT):
                    dve.wait_ge(S("mla_ps"), NT * L + t + 1)
                    kv = PS[:, 4 + t % 2, :].rearrange("p (h d) -> p h d", h=HEADS)
                    mk = ot[:, t, 640:1024].rearrange("p (h d) -> p h d", h=HEADS)
                    dve.tensor_copy(mk[:, :, 0:HD], kv[:, :, 0:HD])
                    dve.tensor_copy(p[:, t, PM:PM + 256].rearrange("p (h d) -> p h d", h=HEADS), kv[:, :, HD:2 * HD])
                    dve.tensor_copy(mk[:, :, HD:MLA_D], bc(p[:, t, PM + 384:PM + 385], (0, HEADS), (1, 32))
                                    ).then_inc(S("mkv_ev"), 1)
                dve.wait_ge(S("sq_m"), L + 1)
                link(dve.tensor_reduce(ss23, ar(scr, NT * 768).rearrange("p (t h d) -> p t h d", t=NT, h=8), AX.X, ALU.add))
                dve.tensor_scalar(ss2[:, :], ss2[:, :], 1.0 / MLA_D, EPS, mul, ALU.add).then_inc(S("var_m"), 1)
                dve.wait_ge(S("sqrt_m"), L + 1)
                link(dve.reciprocal(ss2[:, :], ss2[:, :]))
                link(dve.tensor_scalar(ss23[:, :, 0:4], ss23[:, :, 0:4], MLA_D ** -0.5, None, mul))
                v = heads(ot[:, :, 256:1024], 8)
                link(dve.tensor_tensor(v, v, over(ss23, MLA_D), mul))
                dve.tensor_tensor(v[:, :, 0:4], v[:, :, 0:4], gain("mla_g_q", NT, 4), mul)
                link(dve.tensor_tensor(v[:, :, 4:8], v[:, :, 4:8], gain("mla_g_k", NT, 4), mul))
                rotate(v[:, CT:, :, HD:MLA_D], scr, 8).then_inc(S("m_norm"), 1)

            def attention(L):
                n, u0 = len(UN[L]), U0[L]
                lv = row("diff_lambda")
                lt = ssd[:, 0:64].rearrange("p (a d) -> p a d", a=2)
                link(dve.tensor_tensor(lt, bc(lv, (64, 2), (1, 32)), bc(row("diff_lambda", 32, 96), (64, 2), (1, 32)), mul))
                dve.tensor_reduce(sc[:, 0:2], lt, AX.X, ALU.add).then_inc(S("lam_in"), 1)
                dve.wait_ge(S("lam_exp"), L + 1)
                link(dve.tensor_tensor(sc[:, 2:3], sc[:, 1:2], sc[:, 0:1], ALU.subtract))
                link(dve.tensor_scalar(sc[:, 3:4], sc[:, 2:3], -LAM_INIT[L], None, ALU.add))

                def maxima(u):
                    _, _, t, w = ALLU[u]
                    kw = N if t >= CT else CTX
                    dve.wait_ge(S("s_ps"), u + 1)
                    sp_ = PS[:, 2 * (u % 2):2 * (u % 2) + 2, :].rearrange("p b n -> p (b n)")[:, 0:w * kw]
                    link(dve.tensor_reduce(att_cols(0, u, w), sp_.rearrange("p (h n) -> p h n", h=w) if w > 1 else sp_,
                                           AX.X, ALU.max))
                    dve.tensor_scalar(att_cols(1, u, w), att_cols(0, u, w), -1.0, None, mul).then_inc(S("nm_done"), 1)

                def probs_evac(u):
                    _, _, t, w = ALLU[u]
                    dve.wait_ge(S("t_ps"), u + 1)
                    if u >= 2:
                        dve.wait_ge(S("o_ps"), u - 1)
                    e = N if t >= CT else CTX * w
                    dve.tensor_copy(PTb[:, u % 2, 512:e], PS[:, 5, 0:e - 512]).then_inc(S("pt_ev_d"), 1)

                def outputs(u):
                    g, h, t, w = ALLU[u]
                    dve.wait_ge(S("o_ps"), u + 1)
                    link(dve.reciprocal(recip[:, 0:w], att_cols(2, u, w)))
                    c0 = {"mla": HD * h, "na": 256 + HD * h, "dif": 512 + HD * (h // 2)}[g]

                    def head(k):
                        return PS[:, 6, at(k, w) * HD:(at(k, w) + 1) * HD]

                    if g == "dif":
                        if w > 1:
                            link(dve.tensor_tensor(recip_l, recip[:, 2:4], bc(sc[:, 3:4], (0, 2)), mul))
                        elif h % 2:
                            link(dve.tensor_tensor(recip_l[:, 0:1], recip[:, 0:1], sc[:, 3:4], mul))
                        for k in range(w):
                            dst = ot[:, t, c0 + HD * (k // 2):c0 + HD * (k // 2 + 1)]
                            if (h + k) % 2:
                                last = dve.scalar_tensor_tensor(out=dst, in0=head(k), scalar=recip_l[:, k // 2:k // 2 + 1], in1=dst,
                                                                op0=mul, op1=ALU.add)
                            else:
                                last = dve.tensor_scalar(dst, head(k), recip[:, at(k, w):at(k, w) + 1], None, mul)
                            if k < w - 1:
                                link(last)
                    elif w > 1:
                        last = dve.tensor_tensor(ot[:, t, c0:c0 + HD * w].rearrange("p (a b d) -> p b a d", a=2, b=2),
                                                 PS[:, 6, 0:HD * w].rearrange("p (b a d) -> p b a d", a=2, b=2),
                                                 bc(recip[:, 0:1], (2, 2), (1, 2), (0, HD)), mul)
                    else:
                        last = dve.tensor_scalar(ot[:, t, c0:c0 + HD], head(0), recip[:, 0:1], None, mul)
                    last.then_inc(S("o_ev"), 1)
                    dve.wait_ge(S("o_ev"), u + 1)

                for u in range(u0, u0 + n + 2):
                    if u < u0 + n:
                        maxima(u)
                    if u0 < u <= u0 + n:
                        probs_evac(u - 1)
                    if u >= u0 + 2:
                        outputs(u - 2)

            def scan(L):
                la, dt, cum, tot, toend, ecum, etot, x_, u_, w_ = [ssd[:, k * 48:(k + 1) * 48] for k in range(10)]
                la3, dt3, cum3, tot3, toend3, ecum3, etot3 = [sv(k) for k in range(7)]
                ul = out_tiles(L)
                dve.wait_ge(S("rows_in"), 16 * len(ROWS) * (L + 1))
                dve.wait_ge(S("pj_ev"), PJ0[L] + NT)
                link(dve.tensor_tensor(sv(7), p[:, :, PDT:PDT + 8], bc(row("ssd_dt_bias"), (0, NT), (1, 8)), ALU.add))
                link(dve.tensor_scalar(u_, x_, -1.0, None, mul))
                dve.tensor_tensor(u_, u_, x_, ALU.min).then_inc(S("sp_in"), 1)
                dve.wait_ge(S("sp_u"), L + 1)
                dve.tensor_scalar(w_, u_, 1.0, None, ALU.add).then_inc(S("sp_w"), 1)
                dve.wait_ge(S("sp_ln"), L + 1)
                link(dve.tensor_scalar(cum, w_, -1.0, 1e-7, ALU.add, ALU.max))
                link(dve.reciprocal(cum, cum))
                link(dve.tensor_tensor(cum, cum, u_, mul))
                link(dve.tensor_tensor(dt, dt, cum, mul))
                link(dve.tensor_scalar(w_, w_, 1.0, None, ALU.is_equal))
                link(dve.tensor_tensor(w_, w_, u_, mul))
                link(dve.tensor_tensor(dt, dt, w_, ALU.max))
                link(dve.tensor_scalar(x_, x_, 0.0, None, ALU.max))
                link(dve.tensor_tensor(dt, dt, x_, ALU.add))
                link(dve.tensor_tensor(la3, dt3, bc(sc[:, 8:16], (0, NT), (1, 8)), mul))
                dve.tensor_scalar(la, la, -1.0, None, mul).then_inc(S("la_done"), 1)
                if L == 0:
                    for q in range(2):
                        dve.wait_ge(S(f"y_out{q}"), 16)
                    dve.wait_ge(S("f_zero"), 16)
                for dd in range(2):
                    last = dve.memset(state(dd), 0.0)
                link(last)
                latent_stats(L)
                dve.wait_ge(S("cum_ps"), L + 1)
                pc = PS[:, 7, 0:96]
                for dd in range(2):
                    dve.tensor_copy(cum3[:, :, 4 * dd:4 * dd + 4], pc[:, 24 * dd:24 * dd + 24].rearrange("p (t h) -> p t h", t=NT))
                link(dve.tensor_copy(tot, pc[:, 48:96]))
                dve.tensor_tensor(toend, tot, cum, ALU.subtract).then_inc(S("cum_in"), 1)
                dve.wait_ge(S("cum_exp"), L + 1)
                dve.tensor_copy(w_, cum).then_inc(S("cum_done"), 1)
                dve.wait_ge(S("cum_done"), L + 1)

                def hp(v2):
                    return v2.rearrange("p (h d) -> p h d", h=HEADS)

                def front(w):
                    _, dd, t = SU[w]
                    if t in ul:
                        dve.wait_ge(S("rg_ps"), YU[w] + 1)
                        yp = YU[w] % 2
                        tri = triU if dd == 0 else triL
                        if YU[w] >= 2:
                            dve.wait_ge(S("y_ps"), YU[w] - 1)
                        dve.tensor_tensor(GMb(w).rearrange("p (g n) -> p g n", g=2), PS[:, 2, 0:256].rearrange("p (g n) -> p g n", g=2),
                                          bc(tri, (0, 2), (1, P)), mul)
                        for h in range(HEADS):
                            last = dve.tensor_scalar(Mb(w, h), PS[:, yp, h * P:(h + 1) * P],
                                                     cum3[:, t, 4 * dd + h:4 * dd + h + 1], 0.0, ALU.subtract, ALU.min)
                        last.then_inc(S("front_done"), 1)
                    if w >= 2:
                        dve.wait_ge(S("st_ps"), w - 1)
                    link(dve.tensor_tensor(hp(xdt(w)), hp(xB[:, t, 0:256]), bc(dt3[:, t, 4 * dd:4 * dd + 4], (1, 4), (0, HD)), mul))
                    dve.tensor_tensor(hp(xdte(w)), hp(xdt(w)), bc(toend3[:, t, 4 * dd:4 * dd + 4], (1, 4), (0, HD)), mul
                                      ).then_inc(S("xdt_done"), 1)
                    if t in ul:
                        dve.wait_ge(S("seg_exp"), YU[w] + 1)
                        dve.wait_ge(S("xdt_done"), w + 1)
                        m4 = Mall(w).rearrange("p (g h n) -> p g h n", g=2, h=2)
                        dve.tensor_tensor(m4, m4, bc(GMb(w), (P, 2), (0, 2), (1, P)), mul).then_inc(S("m_done"), 1)

                def back(w):
                    _, dd, t = SU[w]
                    if t in ul:
                        dve.wait_ge(S("y_ps"), YU[w] + 1)
                        yp = YU[w] % 2
                        link(dve.tensor_tensor(hp(ytmp), hp(PS[:, 3, 256:512]), bc(ecum3[:, t, 4 * dd:4 * dd + 4], (1, 4), (0, HD)), mul))
                        acc = yacc[:, t]
                        if (L, 1 - dd, t) in SU[2 * NT * L:w]:
                            link(dve.tensor_tensor(acc, acc, ytmp, ALU.add))
                            dve.tensor_tensor(acc, PS[:, 3, 0:256], acc, ALU.add).then_inc(S("y_done"), 1)
                        else:
                            dve.tensor_tensor(acc, PS[:, 3, 0:256], ytmp, ALU.add).then_inc(S("y_done"), 1)
                        dve.wait_ge(S("y_done"), YU[w] + 1)
                    dve.wait_ge(S("st_ps"), w + 1)
                    link(dve.tensor_tensor(hp(state(dd)), hp(state(dd)), bc(etot3[:, t, 4 * dd:4 * dd + 4], (1, 4), (0, HD)), mul))
                    dve.tensor_tensor(state(dd), PS[:, 6, 0:256], state(dd), ALU.add).then_inc(S("state_done"), 1)
                    dve.wait_ge(S("state_done"), w + 1)

                w0 = 2 * NT * L
                for i in range(2 * NT + 1):
                    if i < 2 * NT:
                        front(w0 + i)
                    if i:
                        back(w0 + i - 1)
                t0 = ul[0]
                nt = NT - t0
                y = yacc[:, t0:]
                link(dve.tensor_tensor(sc[:, 16:20], row("ssd_d", 0, 4), row("ssd_d", 4, 4), ALU.add))
                xs = xB[:, t0:, 0:256]
                tmp = ar(sca, nt * 256)
                link(dve.tensor_tensor(tmp.rearrange("p (t h d) -> p t h d", t=nt, h=4), heads(xs, 4),
                                       bc(sc[:, 16:20], (0, nt), (1, 4), (0, HD)), mul))
                tmp3 = tmp.rearrange("p (t d) -> p t d", t=nt)
                dve.tensor_tensor(y, y, tmp3, ALU.add).then_inc(S("scan_done"), 1)

            def finish(L):
                t0 = out_tiles(L)[0]
                f3 = ss[:, 0:30].rearrange("p (t h) -> p t h", t=NT)[:, t0:]
                dve.wait_ge(S("fin_in"), 2 * L + 2)
                dve.tensor_reduce(f3[:, :, 4], sq_scan[:, t0:], AX.X, ALU.add)
                dve.wait_ge(S("fin_sq"), L + 1)
                link(dve.tensor_reduce(f3[:, :, 0:4], heads(sq_dif[:, t0:], 4), AX.X, ALU.add))
                dve.tensor_scalar(f3[:, :, 0:4], f3[:, :, 0:4], 1.0 / HD, EPS, mul, ALU.add)
                dve.tensor_scalar(f3[:, :, 4:5], f3[:, :, 4:5], 1.0 / GW, EPS, mul, ALU.add).then_inc(S("var_f"), 1)
                dve.wait_ge(S("sqrt_f"), L + 1)
                link(dve.reciprocal(ss[:, 5 * t0:30], ss[:, 5 * t0:30]))
                link(dve.tensor_scalar(f3[:, :, 0:4], f3[:, :, 0:4], 1.0 - LAM_INIT[L], None, mul))
                vd = heads(ot[:, t0:, 512:768], 4)
                link(dve.tensor_tensor(vd, vd, over(f3[:, :, 0:4], HD), mul))
                dve.tensor_tensor(vd, vd, gain("diff_g_sub", NT - t0, 4), mul)
                dve.tensor_tensor(ot[:, t0:, 768:1024], ot[:, t0:, 768:1024], bc(f3[:, :, 4], (5, NT - t0), (0, 256)), mul
                                  ).then_inc(S("mix_done"), 1)

            def out_proj(L):
                for i, t in enumerate(out_tiles(L)):
                    dve.wait_ge(S("oT_ps"), OT0[L] + i + 1)
                    dve.tensor_copy(oT[:, 4:8, t * P:(t + 1) * P],
                                    PS[:, 2 * (i % 2) + 1, :].rearrange("p (c n) -> p c n", c=4)).then_inc(S("oT_d"), 1)
                for m in range(DC):
                    dve.wait_ge(S("op_ps"), DC * L + m + 1)
                    parts = []
                    for bk, (a, b) in enumerate(segs(tok_lo(L))):
                        parts += [(bk, a, max(a, a2), min(b, b2), s) for s, a2, b2 in streams(tok_lo(L), N) if max(a, a2) < min(b, b2)]
                    for q, (bk, a, c0, c1, s) in enumerate(parts):
                        last = dve.scalar_tensor_tensor(out=hT[:, m, c0:c1], in0=PS[:, 4 + 2 * (m % 2) + bk, c0 - a:c1 - a],
                                                        scalar=mod4[:, L, 16 + m, s:s + 1], in1=hT[:, m, c0:c1], op0=mul, op1=ALU.add)
                    last.then_inc(S("op_ev"), 1)
                dve.wait_ge(S("op_ev"), DC * (L + 1))
                dve.memset(sc[:, 20:21], 0.0).then_inc(S("h_mid"), 1)

            def route(L):
                tl = out_tiles(L)
                t0, T = tl[0], len(tl)
                dve.wait_ge(S("lgT_ps"), L + 1)
                for bk, (a, b) in enumerate(segs(tok_lo(L))):
                    last = dve.tensor_copy(lgT[0:20, a:b], PS[0:20, 4 + bk, 0:b - a])
                last.then_inc(S("lgT_ev"), 1)
                dve.wait_ge(S("lg_ps"), L + 1)
                lg = r_lg[:, t0:]
                link(dve.tensor_tensor(lg, PS[:, 6, t0 * 20:NT * 20].rearrange("p (t n) -> p t n", t=T),
                                       bc(row("moe_b_group"), (0, T), (1, 20)), ALU.add))
                g4 = lg[:, :, 0:4]

                def v24(off):
                    return r_(off, 24).rearrange("p (t g) -> p t g", t=NT)[:, t0:]

                def v96(off):
                    return r_(off, 96).rearrange("p (t e) -> p t e", t=NT)[:, t0:]

                def s6(k):
                    return r6(k)[:, t0:]

                def first_max(v, w, mx, tmp, oh):
                    link(dve.tensor_reduce(mx, v, AX.X, ALU.max))
                    link(dve.tensor_tensor(tmp, v, bc(mx, (1, T), (0, w)), ALU.is_equal))
                    link(dve.tensor_tensor(tmp, tmp, bc(K[:, C_DEC:C_DEC + 1], (0, T), (1, w)), mul))
                    link(dve.tensor_reduce(s6(9), tmp, AX.X, ALU.max))
                    link(dve.tensor_tensor(oh, tmp, bc(s6(9), (1, T), (0, w)), ALU.is_equal))

                ohg = v24(144)
                first_max(g4, 4, s6(0), v24(120), ohg)
                if t0:
                    link(dve.memset(r_(120, 24), 0.0))
                    link(dve.memset(r6(4), 0.0))
                dve.tensor_tensor(v24(120), g4, bc(s6(0), (1, T), (0, 4)), ALU.subtract).then_inc(S("rt_g"), 1)
                dve.wait_ge(S("rt_ge"), L + 1)
                link(dve.tensor_reduce(s6(1), v24(120), AX.X, ALU.add))
                link(dve.reciprocal(s6(1), s6(1)))
                em = v96(228)
                em4 = em.rearrange("p t (g e) -> p t g e", g=GROUPS)
                ohg4 = bc(ohg, (4, T), (1, 4), (0, EPG))
                link(dve.tensor_tensor(em4, lg[:, :, 4:20].rearrange("p t (g e) -> p t g e", g=GROUPS), ohg4, mul))
                link(dve.tensor_scalar(v24(120), ohg, -1.0, BIG, ALU.add, mul))
                link(dve.tensor_tensor(em4, em4, bc(v24(120), (4, T), (1, 4), (0, EPG)), ALU.add))
                first_max(em, EXP, s6(2), v96(324), r_oh[0][:, t0:])
                link(dve.scalar_tensor_tensor(out=em, in0=r_oh[0][:, t0:], scalar=-3 * BIG, in1=em, op0=mul, op1=ALU.add))
                first_max(em, EXP, s6(3), v96(324), r_oh[1][:, t0:])
                link(dve.tensor_tensor(r_sel[:, t0:], r_oh[0][:, t0:], r_oh[1][:, t0:], ALU.add))
                link(dve.memset(r_pre[:, 0, :], 0.0))
                for j in range(T):
                    last = dve.tensor_tensor(r_pre[:, j + 1, :], r_pre[:, j, :], r_sel[:, t0 + j, :], ALU.add)
                    if j < T - 1:
                        link(last)
                last.then_inc(S("sel_done"), 1)
                dve.tensor_tensor(s6(4), s6(3), s6(2), ALU.subtract).then_inc(S("rt_m"), 1)
                dve.wait_ge(S("rt_me"), L + 1)
                link(dve.tensor_scalar(s6(5), s6(4), 1.0, None, ALU.add))
                link(dve.reciprocal(s6(5), s6(5)))
                link(dve.tensor_tensor(wtok[:, t0:NT], s6(5), s6(1), mul))
                link(dve.tensor_tensor(wtok[:, NT + t0:2 * NT], wtok[:, t0:NT], s6(4), mul))
                dve.wait_ge(S("rank_ps"), L + 1)
                dm = v96(708)
                dve.tensor_copy(dm, PS[:, 5, t0 * EXP:NT * EXP].rearrange("p (t e) -> p t e", t=T))
                cnt, blocks, pex = r_(804, EXP), r_(820, EXP), r_(836, EXP)
                link(dve.tensor_copy(cnt, PS[:, 5, NT * EXP:(NT + 1) * EXP]))
                c6 = r_(852, EXP * NT).rearrange("p (e j) -> p e j", e=EXP)
                link(dve.tensor_tensor(c6, bc(cnt, (1, EXP), (0, NT)), bc(K[:, C_THR:C_THR + 1], (0, EXP), (1, NT)), ALU.is_gt))
                link(dve.tensor_reduce(blocks, c6, AX.X, ALU.add))
                t16 = r_(852, EXP * EXP).rearrange("p (e j) -> p e j", e=EXP)
                link(dve.tensor_tensor(t16, K[:, C_TRI:C_TRI + EXP * EXP].rearrange("p (e j) -> p e j", e=EXP),
                                       bc(blocks, (0, EXP), (1, EXP)), mul))
                link(dve.tensor_reduce(pex, t16, AX.X, ALU.add))
                link(dve.tensor_tensor(cnt, pex, blocks, ALU.add))
                cb = r_(1108, NBMAX * EXP).rearrange("p (b e) -> p b e", b=NBMAX)
                link(dve.tensor_tensor(cb, bc(K[:, C_BLK:C_BLK + 1], (1, NBMAX), (0, EXP)), bc(cnt, (0, NBMAX), (1, EXP)), ALU.is_ge))
                link(dve.tensor_reduce(r_(852, NBMAX), cb, AX.X, ALU.add))
                link(dve.tensor_scalar(blk_e[:, :], r_(852, NBMAX), float(EXP - 1), None, ALU.min))
                pj = r_(852, PAIRS[L])
                link(dve.tensor_scalar(pj, K[:, C_BLK:C_BLK + PAIRS[L]], 2.0, cnt[:, EXP - 1:EXP], mul, ALU.is_lt))
                link(dve.tensor_reduce(r_(900, 1), pj, AX.X, ALU.add))
                dve.tensor_scalar(npair[:, :], r_(900, 1), -2.0, None, ALU.add).then_inc(S("blk_ready"), 1)
                dve.wait_ge(S("blk_ready"), L + 1)
                link(dve.tensor_scalar(pex, pex, float(P), None, mul))
                link(dve.tensor_tensor(dm, dm, bc(pex, (0, T), (1, EXP)), ALU.add))
                for k in range(TOPK):
                    link(dve.tensor_tensor(v96(324), r_oh[k][:, t0:], dm, mul))
                    link(dve.tensor_reduce(s6(6 + k), v96(324), AX.X, ALU.add))
                dst = r_(168 + 36, TOPK * NT).rearrange("p (k t) -> p k t", k=TOPK)[:, :, t0:]
                blk = r_(168 + 48, TOPK * NT).rearrange("p (k t) -> p k t", k=TOPK)[:, :, t0:]
                ob, orow = oh_blk[:, :, 0:T, :], oh_row[:, :, 0:T, :]
                link(dve.tensor_copy(dest[:, :].rearrange("p (k t) -> p k t", k=TOPK)[:, :, t0:], dst))
                blocks_b = bc(K[:, C_BLK:C_BLK + 1], (0, TOPK), (0, T), (1, NBMAX))
                link(dve.tensor_scalar(blk, dst, 1.0 / P, None, mul))
                link(dve.tensor_tensor(ob, bc(blk, (NT, TOPK), (1, T), (0, NBMAX)), blocks_b, ALU.is_ge))
                link(dve.tensor_reduce(blk, ob, AX.X, ALU.add))
                link(dve.tensor_scalar(blk, blk, -1.0, None, ALU.add))
                link(dve.scalar_tensor_tensor(out=dst, in0=blk, scalar=-float(P), in1=dst, op0=mul, op1=ALU.add))
                link(dve.tensor_tensor(ob, bc(blk, (NT, TOPK), (1, T), (0, NBMAX)), blocks_b, ALU.is_equal))
                link(dve.tensor_tensor(ob, ob, bc(K[:, C_TOK + t0:C_TOK + t0 + 1], (0, TOPK), (1, T), (0, NBMAX)), mul))
                dve.tensor_tensor(orow, bc(dst, (NT, TOPK), (1, T), (0, P)), bc(K[:, C_IOTA:C_IOTA + 1], (0, TOPK), (0, T), (1, P)),
                                  ALU.is_equal).then_inc(S("oh_ready"), 1)
                dve.wait_ge(S("oh_ready"), L + 1)
                dve.wait_ge(S("slot_ps"), L + 1)
                dve.tensor_scalar(slots[:, :], PS[:, 6, 0:NBMAX], float(N), None, ALU.add).then_inc(S("slots_ready"), 1)

            def experts(L):
                n0 = NB0[L]

                def x_evac(i, par):
                    b = 2 * i + par
                    dve.wait_ge(S("xt_ps"), n0 + b + 1)
                    dve.tensor_copy(xT(par)[:, 512:], PS[:, 1, :]).then_inc(S("xT_d"), 1)

                def up(i, par):
                    b = 2 * i + par
                    dve.wait_ge(S("silu_done"), n0 + b + 1)
                    dve.tensor_tensor(hid(par), PS[:, 3, :], hid(par), mul).then_inc(S("h_done"), 1)

                def h_evac(i, par):
                    b = 2 * i + par
                    dve.wait_ge(S("ht_ps"), n0 + b + 1)
                    dve.tensor_copy(hidT(par), PS[:, 4, :]).then_inc(S("hT_ev"), 1)

                def y_evac(i, par, back=0):
                    b = 2 * i + (par - 2 * back)
                    dve.wait_ge(S("dn_ps"), n0 + b + 1)
                    dve.wait_ge(S(f"y_out{par}"), 16 * i + (16 * (n0 // 2) + 16 - 16 * back))
                    dve.tensor_copy(ysb(par)[:, 512:], PS[:, 6, :]).then_inc(S("y_d"), 1)

                before, lastp = last_pair(dve, L)
                x_evac(0, 0)
                up(0, 0)
                x_evac(0, 1)
                h_evac(0, 0)
                up(0, 1)
                x_evac(1, 0)
                y_evac(0, 0)
                h_evac(0, 1)
                with dve.Fori(1, lastp) as i:
                    up(i, 0)
                    x_evac(i, 1)
                    y_evac(i, 1, back=1)
                    h_evac(i, 0)
                    up(i, 1)
                    x_evac(i + 1, 0)
                    y_evac(i, 0)
                    h_evac(i, 1)
                up(lastp, 0)
                x_evac(lastp, 1)
                y_evac(before, 1)
                h_evac(lastp, 0)
                up(lastp, 1)
                y_evac(lastp, 0)
                h_evac(lastp, 1)
                y_evac(lastp, 1)
                dve.drain()
                with dve.Fori(lastp + 1, PAIRS[L] + 1):
                    for nm in ("xT_d", "h_done", "hT_ev", "y_d"):
                        dve.sem_inc(S(nm), 2)

            def combine(L):
                for i, t in enumerate(out_tiles(L)):
                    dve.wait_ge(S(f"g_in{i % 2}"), 32 * (cnt2(L, i) + 1))
                    a, b = r12(i, 0), r12(i, 1)
                    link(dve.tensor_scalar(a, a, wtok[:, t:t + 1], None, mul))
                    dve.scalar_tensor_tensor(out=a, in0=b, scalar=wtok[:, NT + t:NT + t + 1], in1=a, op0=mul, op1=ALU.add
                                             ).then_inc(S("comb"), 1)
                    dve.wait_ge(S("comb_ps"), OT0[L] + i + 1)
                    s = 1 if t < CT else 0
                    for c in range(DC):
                        v = hT[:, c, t * P:(t + 1) * P]
                        last = dve.scalar_tensor_tensor(out=v, in0=PS[:, 2 * (i % 2) + c // 4, (c % 4) * P:(c % 4 + 1) * P],
                                                        scalar=mod4[:, L, 40 + c, s:s + 1], in1=v, op0=mul, op1=ALU.add)
                    last.then_inc(S("hup"), 1)
                dve.wait_ge(S("hup"), OT0[L] + OTN[L])
                dve.memset(sc[:, 21:22], 0.0).then_inc(S("h_final"), 1)

            for L in range(LAYERS):
                norm(L, 0)
                conv(L)
                scan(L)
                stats(L)
                mla_prep(L)
                attention(L)
                finish(L)
                out_proj(L)
                norm(L, 1)
                route(L)
                experts(L)
                combine(L)
            for i, t in enumerate(out_tiles(1)):
                dve.wait_ge(S("res_ps"), i + 1)
                if i >= 2:
                    dve.wait_ge(S(f"res_out{i % 2}"), 16 * (i // 2))
                dve.tensor_copy(restok[:, i % 2, 512:], PS[:, 2 * (i % 2) + 1, :]).then_inc(S("res_d"), 1)

        @block.gpsimd
        def _(pool):
            pool.wait_ge(S("consts_in"), 16)
            pool.memset(modrow, 0.0).then_inc(S("zeros"), 1)
            pool.memset(zrows, 0.0).then_inc(S("zeros"), 1)
            for L in range(LAYERS):
                pool.wait_ge(S("rstd_done"), L + 1)
                pool.wait_ge(S("rows_in"), 16 * len(ROWS) * (L + 1))
                ss3 = ss[:, :].rearrange("p (t h) -> p t h", t=NT)
                t0 = out_tiles(L)[0]
                vk = p[:, :, PNK:PNK + 256].rearrange("p t (h d) -> p t h d", h=HEADS)
                vq = p[:, t0:, PNQ:PNQ + 256].rearrange("p t (h d) -> p t h d", h=HEADS)
                pool.tensor_tensor(vk, vk, bc(ss3[:, :, 0:4], (26, NT), (1, 4), (0, HD)), ALU.mult)
                pool.tensor_tensor(vq, vq, bc(ss3[:, t0:, 4:8], (26, NT - t0), (1, 4), (0, HD)), ALU.mult).then_inc(S("na_r"), 1)
                pool.wait_ge(S("na_r"), L + 1)
                pool.tensor_tensor(vk, vk, bc(row("na_g_k"), (0, NT), (0, 4), (1, HD)), ALU.mult)
                pool.tensor_tensor(vq, vq, bc(row("na_g_q"), (0, NT - t0), (0, 4), (1, HD)), ALU.mult).then_inc(S("na_norm"), 1)
                pool.wait_ge(S("bias_in"), 16 * 2 * HEADS * (L + 1))
                bv = bias4[:, :, 1:, :]
                pool.tensor_tensor(bv, bv, bc(K[:, C_MASK:C_MASK + 1], (0, HEADS), (0, ROFF - 1), (1, GRID)), ALU.add
                                   ).then_inc(S("bias_ready"), 1)
                pool.wait_ge(S("z_silu"), L + 1)
                pool.wait_ge(S("kt_ev"), 2 * NT * (L + 1))
                ys, yo = yacc[:, t0:], ot[:, t0:, 768:1024]
                pool.tensor_tensor(ys, ys, p[:, t0:, PZ:PZ + GW], ALU.mult).then_inc(S("fin_in"), 1)
                pool.wait_ge(S("fin_in"), 2 * L + 1)
                pool.tensor_tensor(yo, ys, bc(row("ssd_g_norm"), (0, NT - t0), (1, 256)), ALU.mult)
                pool.tensor_tensor(sq_scan[:, t0:], ys, ys, ALU.mult).then_inc(S("fin_in"), 1)
                pool.wait_ge(S("slots_ready"), L + 1)
                for q in range(2):
                    pool.wait_ge(S(f"f_out{q}"), 16 * (NT // 2 * L + OTN[L] // 2))
                pool.wait_ge(S("f_zero"), 16)
                n0 = NB0[L]

                def gather(i, par, first=False):
                    b = 2 * i + par
                    if not first:
                        pool.wait_ge(S("xt_ps"), n0 + b - 1)
                        pool.wait_ge(S(f"xg_in{L}{par}"), 16 * i)
                    pool.tensor_copy(slot1[:, par:par + 1], slots[:, bass.ds(b, 1)]).then_inc(S("slot1_done"), 1)
                    pool.wait_ge(S("slot1_done"), n0 + b + 1)
                    pool.nop(nofuse=True)
                    pool.indirect_dma_start(
                        out=xg(par), out_offset=None, in_=dram["f_rows"],
                        in_offset=bass.IndirectOffsetOnAxis(ap=slot1[:, par:par + 1], axis=0)).then_inc(S(f"xg_in{L}{par}"), 16)

                for par in range(2):
                    gather(0, par, True)
                _, lastp = last_pair(pool, L)
                with pool.Fori(1, lastp + 1) as i:
                    for par in range(2):
                        gather(i, par)
                pool.drain()
                with pool.Fori(lastp + 1, PAIRS[L] + 1):
                    pool.sem_inc(S("slot1_done"), 2)
                for q in range(2):
                    pool.wait_ge(S(f"y_out{q}"), 8 * (NB0[L] + NB[L] + 2) + 16)
                for i, t in enumerate(out_tiles(L)):
                    if i >= 2:
                        pool.wait_ge(S("hup"), OT0[L] + i - 1)
                    for k in range(TOPK):
                        pool.indirect_dma_start(
                            out=r12(i, k), out_offset=None, in_=dram["y_rows"],
                            in_offset=bass.IndirectOffsetOnAxis(ap=dest[:, k * NT + t:k * NT + t + 1], axis=0)
                        ).then_inc(S(f"g_in{i % 2}"), 16)


_INS = ["x", "c", "ctx", "c_ctx", "w_mod", "b_mod", "g_mix", "w_in", "w_out", "na_g_q", "na_g_k",
        "mla_g_qa", "mla_w_qb", "mla_g_kva", "mla_w_kvb", "mla_g_q", "mla_g_k", "diff_g_q", "diff_g_k", "diff_lambda",
        "diff_g_sub", "ssd_conv_w", "ssd_conv_b", "ssd_dt_bias", "ssd_a_log", "ssd_d", "ssd_g_norm", "g_ffn",
        "moe_w_group", "moe_b_group", "moe_w_expert", "moe_b_expert", "moe_w_gate", "moe_w_up", "moe_w_down"]


def kernel(**inputs):
    import numpy as _np
    import concourse.bacc as _bacc
    from concourse import mybir as _mybir
    from concourse.bass_utils import run_bass_kernel_spmd as _run

    nc = _bacc.Bacc("TRN2", target_bir_lowering=False, num_devices=1)
    arrays, io = {}, {}
    rel = _np.ascontiguousarray(inputs["na_rel_bias"]).reshape(LAYERS, -1)
    data = {k: _np.ascontiguousarray(inputs[k]) for k in _INS}
    data["rel_pad"] = _np.pad(rel, ((0, 0), (REL_PAD, REL_PAD)))
    data["consts"] = constants()
    for name, a in data.items():
        arrays[f"in_{name}"] = a
        io[name] = nc.dram_tensor(f"in_{name}", a.shape, _mybir.dt.from_np(a.dtype), kind="ExternalInput").ap()
    out = nc.dram_tensor("out", (1, SEQ, D), F32, kind="ExternalOutput").ap()
    build(nc, io, out)
    r = _run(nc, [arrays], core_ids=[0])
    return r.results[0]["out"]
```
